# Optimizing a Trainium2 kernel written in Bass

```python
import jax, jax.numpy as jnp
from jax import lax
import numpy as np

D_MODEL = 1024
BATCH = 1
SEQ = 256
DEPTH = 2

CHUNK = 64
N_META = 16
N_PAD = CHUNK - N_META
N_MIXERS = 2
RMS_EPS = 1e-6
L2_EPS = 1e-6

GDN_QK_HEADS = 8
GDN_V_HEADS = 16
GDN_HEAD_DIM = 128
GDN_CONV = 4
GDN_KEY_DIM = GDN_QK_HEADS * GDN_HEAD_DIM
GDN_VAL_DIM = GDN_V_HEADS * GDN_HEAD_DIM
GDN_QKV_DIM = 2 * GDN_KEY_DIM + GDN_VAL_DIM
GDN_IN = GDN_QKV_DIM + GDN_VAL_DIM + 2 * GDN_V_HEADS

ML_HEADS = 4
ML_QK_DIM = 128
ML_V_DIM = 256
ML_GATE_CAP = 15.0
ML_QK_TOT = ML_HEADS * ML_QK_DIM
ML_V_TOT = ML_HEADS * ML_V_DIM
ML_IN = 2 * ML_QK_TOT + 2 * ML_V_TOT + 2 * ML_HEADS

FFN_DIM = 2816
FFN_CONV = 3

N_GDN_LAYERS = (DEPTH + 1) // 2
N_ML_LAYERS = DEPTH // 2


def rms_norm(x, w):
    xf = x.astype(jnp.float32)
    y = xf * lax.rsqrt(jnp.mean(xf * xf, -1, keepdims=True) + RMS_EPS)
    return (y * w.astype(jnp.float32)).astype(x.dtype)

def l2_normalize(x):
    return x * lax.rsqrt(jnp.sum(x * x, -1, keepdims=True) + L2_EPS)

def causal_depthwise_conv(x, w):
    K, C = w.shape
    return lax.conv_general_dilated(x, w[:, None, :].astype(x.dtype), window_strides=(1,),
                                    padding=[(K - 1, 0)], dimension_numbers=('NWC', 'WIO', 'NWC'),
                                    feature_group_count=C)

def to_chunks(t):
    B, L, H = t.shape[:3]
    t = t.reshape((B, L // CHUNK, CHUNK, H) + t.shape[3:])
    return jnp.moveaxis(t, 3, 1)

def from_chunks(t):
    B, H, nc, C, d = t.shape
    return jnp.moveaxis(t, 1, 3).reshape(B, nc * C, H, d)

def gated_deltanet(h, valid, w_in, conv_w, a_log, dt_bias, norm_w, w_out):
    f32 = jnp.float32
    B, L, _ = h.shape
    proj = h @ w_in
    o1 = GDN_QKV_DIM
    o2 = o1 + GDN_VAL_DIM
    o3 = o2 + GDN_V_HEADS
    qkv = jax.nn.silu(causal_depthwise_conv(proj[..., :o1], conv_w)).astype(f32)
    z = proj[..., o1:o2].astype(f32).reshape(B, L, GDN_V_HEADS, GDN_HEAD_DIM)
    beta = jax.nn.sigmoid(proj[..., o2:o3].astype(f32))
    g = -jnp.exp(a_log.astype(f32)) * jax.nn.softplus(proj[..., o3:].astype(f32) + dt_bias.astype(f32))

    rep = GDN_V_HEADS // GDN_QK_HEADS
    mask = valid[None, :, None, None]
    q = qkv[..., :GDN_KEY_DIM].reshape(B, L, GDN_QK_HEADS, GDN_HEAD_DIM)
    k = qkv[..., GDN_KEY_DIM:2 * GDN_KEY_DIM].reshape(B, L, GDN_QK_HEADS, GDN_HEAD_DIM)
    v = qkv[..., 2 * GDN_KEY_DIM:].reshape(B, L, GDN_V_HEADS, GDN_HEAD_DIM) * mask
    q = jnp.repeat(l2_normalize(q), rep, axis=2) * (GDN_HEAD_DIM ** -0.5)
    k = jnp.repeat(l2_normalize(k), rep, axis=2) * mask

    qc, kc, vc = to_chunks(q), to_chunks(k), to_chunks(v)
    bc, gc = to_chunks(beta), to_chunks(g)
    G = jnp.cumsum(gc, -1)
    incl = jnp.tri(CHUNK, dtype=bool)
    strict = jnp.tri(CHUNK, k=-1, dtype=f32)
    decay = jnp.exp(jnp.where(incl, G[..., :, None] - G[..., None, :], -jnp.inf))
    kb = kc * bc[..., None]
    a_mat = jnp.eye(CHUNK, dtype=f32) + jnp.einsum('bhnid,bhnjd->bhnij', kb, kc) * decay * strict
    rhs = jnp.concatenate([vc * bc[..., None], kb * jnp.exp(G)[..., None]], -1)
    sol = lax.linalg.triangular_solve(a_mat, rhs, left_side=True, lower=True)
    u, w = sol[..., :GDN_HEAD_DIM], sol[..., GDN_HEAD_DIM:]
    attn = jnp.einsum('bhnid,bhnjd->bhnij', qc, kc) * decay
    qd = qc * jnp.exp(G)[..., None]
    kt = kc * jnp.exp(G[..., -1:] - G)[..., None]
    gt = jnp.exp(G[..., -1])

    def step(S, xs):
        u_c, w_c, qd_c, att_c, kt_c, gt_c = xs
        v_new = u_c - jnp.einsum('bhck,bhkv->bhcv', w_c, S)
        o_c = jnp.einsum('bhck,bhkv->bhcv', qd_c, S) + jnp.einsum('bhij,bhjv->bhiv', att_c, v_new)
        S = S * gt_c[..., None, None] + jnp.einsum('bhck,bhcv->bhkv', kt_c, v_new)
        return S, o_c

    xs = tuple(jnp.moveaxis(t, 2, 0) for t in (u, w, qd, attn, kt, gt))
    S0 = jnp.zeros((B, GDN_V_HEADS, GDN_HEAD_DIM, GDN_HEAD_DIM), f32)
    _, o = lax.scan(step, S0, xs)
    o = from_chunks(jnp.moveaxis(o, 0, 2))
    o = rms_norm(o, norm_w) * jax.nn.silu(z)
    return o.reshape(B, L, GDN_VAL_DIM).astype(h.dtype) @ w_out

def mlstm(h, valid, w_in, gate_b, norm_w, w_out):
    f32 = jnp.float32
    B, L, _ = h.shape
    proj = h @ w_in
    o1 = ML_QK_TOT
    o2 = 2 * ML_QK_TOT
    o3 = o2 + ML_V_TOT
    o4 = o3 + ML_V_TOT
    mask = valid[None, :, None, None]
    q = proj[..., :o1].astype(f32).reshape(B, L, ML_HEADS, ML_QK_DIM) * (ML_QK_DIM ** -0.5)
    k = proj[..., o1:o2].astype(f32).reshape(B, L, ML_HEADS, ML_QK_DIM) * mask
    v = proj[..., o2:o3].astype(f32).reshape(B, L, ML_HEADS, ML_V_DIM) * mask
    o_gate = jax.nn.sigmoid(proj[..., o3:o4].astype(f32)).reshape(B, L, ML_HEADS, ML_V_DIM)
    gates = proj[..., o4:].astype(f32) + gate_b.astype(f32)
    gates = ML_GATE_CAP * jnp.tanh(gates / ML_GATE_CAP)
    log_i = gates[..., :ML_HEADS]
    log_f = jax.nn.log_sigmoid(gates[..., ML_HEADS:])

    qc, kc, vc = to_chunks(q), to_chunks(k), to_chunks(v)
    lic, lfc = to_chunks(log_i), to_chunks(log_f)
    b = jnp.cumsum(lfc, -1)
    b_last = b[..., -1]
    a = b_last[..., None] - b + lic

    def step(carry, xs):
        Cs, ns, ms = carry
        k_c, v_c, a_c, bl_c = xs
        m_new = jnp.maximum(bl_c + ms, jnp.max(a_c, -1))
        dec = jnp.exp(bl_c + ms - m_new)
        kw = k_c * jnp.exp(a_c - m_new[..., None])[..., None]
        C_new = dec[..., None, None] * Cs + jnp.einsum('bhck,bhcv->bhkv', kw, v_c)
        n_new = dec[..., None] * ns + jnp.sum(kw, -2)
        return (C_new, n_new, m_new), (Cs, ns, ms)

    xs = tuple(jnp.moveaxis(t, 2, 0) for t in (kc, vc, a, b_last))
    init = (jnp.zeros((B, ML_HEADS, ML_QK_DIM, ML_V_DIM), f32),
            jnp.zeros((B, ML_HEADS, ML_QK_DIM), f32),
            jnp.zeros((B, ML_HEADS), f32))
    _, (C_st, n_st, m_st) = lax.scan(step, init, xs)
    C_st = jnp.moveaxis(C_st, 0, 2)
    n_st = jnp.moveaxis(n_st, 0, 2)
    m_st = jnp.moveaxis(m_st, 0, 2)

    incl = jnp.tri(CHUNK, dtype=bool)
    D = jnp.where(incl, b[..., :, None] - b[..., None, :] + lic[..., None, :], -jnp.inf)
    inter = b + m_st[..., None]
    m_t = jnp.maximum(jnp.max(D, -1), inter)
    wD = jnp.exp(D - m_t[..., None]) * jnp.einsum('bhnid,bhnjd->bhnij', qc, kc)
    sc = jnp.exp(inter - m_t)
    num = sc[..., None] * jnp.einsum('bhnck,bhnkv->bhncv', qc, C_st) + jnp.einsum('bhnij,bhnjv->bhniv', wD, vc)
    den = sc * jnp.einsum('bhnck,bhnk->bhnc', qc, n_st) + jnp.sum(wD, -1)
    hh = num / jnp.maximum(jnp.abs(den), jnp.exp(-m_t))[..., None]
    hh = from_chunks(hh)
    hh = rms_norm(hh, norm_w.reshape(ML_HEADS, ML_V_DIM)) * o_gate
    return hh.reshape(B, L, ML_V_TOT).astype(h.dtype) @ w_out

def conv_ffn(h, w_up, conv_w, conv_b, w_down):
    u = causal_depthwise_conv(h @ w_up, conv_w) + conv_b
    gate, up = u[..., :FFN_DIM], u[..., FFN_DIM:]
    return (jax.nn.silu(gate) * up) @ w_down

def first_inputs(seed: int = 0) -> dict:
    key = jax.random.key(seed)
    ks = jax.random.split(key, 20)
    f32 = jnp.float32
    nrm = lambda k, shape, s: jax.random.normal(k, shape, f32) * s
    x = nrm(ks[0], (BATCH, SEQ, D_MODEL), 1.0)
    meta_tokens = nrm(ks[1], (N_META, D_MODEL), 1.0)
    norm_w = 1.0 + nrm(ks[2], (DEPTH, 4, D_MODEL), 0.05)
    gdn_w_in = nrm(ks[3], (N_GDN_LAYERS, D_MODEL, GDN_IN), D_MODEL ** -0.5)
    gdn_conv_w = nrm(ks[4], (N_GDN_LAYERS, GDN_CONV, GDN_QKV_DIM), GDN_CONV ** -0.5)
    gdn_a_log = jnp.log(jax.random.uniform(ks[5], (N_GDN_LAYERS, GDN_V_HEADS), f32, 1.0, 16.0))
    dt = jnp.exp(jax.random.uniform(ks[6], (N_GDN_LAYERS, GDN_V_HEADS), f32, np.log(1e-3), np.log(1e-1)))
    gdn_dt_bias = dt + jnp.log(-jnp.expm1(-dt))
    gdn_norm_w = 1.0 + nrm(ks[7], (N_GDN_LAYERS, GDN_HEAD_DIM), 0.05)
    gdn_w_out = nrm(ks[8], (N_GDN_LAYERS, GDN_VAL_DIM, D_MODEL), GDN_VAL_DIM ** -0.5)
    ml_w_in = nrm(ks[9], (N_ML_LAYERS, D_MODEL, ML_IN), D_MODEL ** -0.5)
    ig_b = nrm(ks[10], (N_ML_LAYERS, ML_HEADS), 0.1)
    fg_b = jnp.linspace(3.0, 6.0, ML_HEADS, dtype=f32)[None] + nrm(ks[11], (N_ML_LAYERS, ML_HEADS), 0.1)
    ml_gate_b = jnp.concatenate([ig_b, fg_b], -1)
    ml_norm_w = 1.0 + nrm(ks[12], (N_ML_LAYERS, ML_V_TOT), 0.05)
    ml_w_out = nrm(ks[13], (N_ML_LAYERS, ML_V_TOT, D_MODEL), ML_V_TOT ** -0.5)
    ffn_w_up = nrm(ks[14], (DEPTH, D_MODEL, 2 * FFN_DIM), D_MODEL ** -0.5)
    ffn_conv_w = nrm(ks[15], (DEPTH, FFN_CONV, 2 * FFN_DIM), FFN_CONV ** -0.5)
    ffn_conv_b = nrm(ks[16], (DEPTH, 2 * FFN_DIM), 0.01)
    ffn_w_down = nrm(ks[17], (DEPTH, FFN_DIM, D_MODEL), FFN_DIM ** -0.5)
    return {"x": x, "meta_tokens": meta_tokens, "norm_w": norm_w,
            "gdn_w_in": gdn_w_in, "gdn_conv_w": gdn_conv_w, "gdn_a_log": gdn_a_log,
            "gdn_dt_bias": gdn_dt_bias, "gdn_norm_w": gdn_norm_w, "gdn_w_out": gdn_w_out,
            "ml_w_in": ml_w_in, "ml_gate_b": ml_gate_b, "ml_norm_w": ml_norm_w, "ml_w_out": ml_w_out,
            "ffn_w_up": ffn_w_up, "ffn_conv_w": ffn_conv_w, "ffn_conv_b": ffn_conv_b, "ffn_w_down": ffn_w_down}

def first_block(x, meta_tokens, norm_w, gdn_w_in, gdn_conv_w, gdn_a_log, gdn_dt_bias, gdn_norm_w, gdn_w_out,
              ml_w_in, ml_gate_b, ml_norm_w, ml_w_out, ffn_w_up, ffn_conv_w, ffn_conv_b, ffn_w_down):
    B, S, D = x.shape
    pad = jnp.zeros((B, N_PAD, D), x.dtype)
    meta = jnp.broadcast_to(meta_tokens[None].astype(x.dtype), (B, N_META, D))
    hs = jnp.concatenate([pad, meta, x], 1)
    L = hs.shape[1]
    valid = (jnp.arange(L) >= N_PAD).astype(jnp.float32)
    keep = valid.astype(x.dtype)[None, :, None]
    for i in range(DEPTH):
        j = i // N_MIXERS
        a_in = rms_norm(hs, norm_w[i, 0])
        if i % N_MIXERS == 0:
            mix = gated_deltanet(a_in, valid, gdn_w_in[j], gdn_conv_w[j], gdn_a_log[j], gdn_dt_bias[j],
                                 gdn_norm_w[j], gdn_w_out[j])
        else:
            mix = mlstm(a_in, valid, ml_w_in[j], ml_gate_b[j], ml_norm_w[j], ml_w_out[j])
        hs = hs + keep * rms_norm(mix, norm_w[i, 1])
        f = conv_ffn(rms_norm(hs, norm_w[i, 2]), ffn_w_up[i], ffn_conv_w[i], ffn_conv_b[i], ffn_w_down[i])
        hs = hs + keep * rms_norm(f, norm_w[i, 3])
    return hs[:, N_PAD + N_META:]


DEPTH_2 = 1

MEM_LEN = 256
CHUNK_2 = 128
SG_GROUPS = 8
SG_GROUP_DIM = 64
SG_WIDTH = SG_GROUPS * SG_GROUP_DIM
MLA_HEADS = 8
MLA_NOPE = 64
MLA_ROPE = 32
MLA_V = 64
MLA_QK = MLA_NOPE + MLA_ROPE
MLA_Q_RANK = 384
MLA_KV_RANK = 256
MLA_WIDTH = MLA_HEADS * MLA_V
MEM_HEADS = 4
MEM_HEAD_DIM = 128
MEM_WIDTH = MEM_HEADS * MEM_HEAD_DIM
N_BRANCH = 3
D_FF = 2816
ROPE_BASE = 10000.0
EPS = 1e-6
Q_BLOCK = 128
NEG = -1e30

COL_U = 0
COL_V = COL_U + SG_WIDTH
COL_CQ = COL_V + SG_WIDTH
COL_CKV = COL_CQ + MLA_Q_RANK
COL_KR = COL_CKV + MLA_KV_RANK
COL_QM = COL_KR + MLA_ROPE
COL_GATE = COL_QM + MEM_WIDTH
IN_COLS = COL_GATE + N_BRANCH * D_MODEL


def rmsnorm(x, g):
    xf = x.astype(jnp.float32)
    y = xf * lax.rsqrt(jnp.mean(xf * xf, axis=-1, keepdims=True) + EPS)
    return (y * g.astype(jnp.float32)).astype(x.dtype)

def layernorm(x, g, b):
    xf = x.astype(jnp.float32)
    mu = jnp.mean(xf, axis=-1, keepdims=True)
    xc = xf - mu
    y = xc * lax.rsqrt(jnp.mean(xc * xc, axis=-1, keepdims=True) + EPS)
    return (y * g.astype(jnp.float32) + b.astype(jnp.float32)).astype(x.dtype)

def rope(x, positions):
    half = x.shape[-1] // 2
    inv = ROPE_BASE ** (-jnp.arange(half, dtype=jnp.float32) / half)
    ang = positions.astype(jnp.float32)[:, :, None] * inv
    cos = jnp.cos(ang)[:, :, None, :]
    sin = jnp.sin(ang)[:, :, None, :]
    x1 = x[..., :half].astype(jnp.float32)
    x2 = x[..., half:].astype(jnp.float32)
    return jnp.concatenate([x1 * cos - x2 * sin, x2 * cos + x1 * sin], axis=-1).astype(x.dtype)

def swiglu(x, w_gu, w_down):
    g, u = jnp.split(x @ w_gu, 2, axis=-1)
    return (jax.nn.silu(g) * u) @ w_down

def spatial_gating(u, v, ln_g, ln_b, w_s, b_s):
    B, S, _ = v.shape
    nc = S // CHUNK_2
    v = layernorm(v, ln_g, ln_b).reshape(B, nc, CHUNK_2, SG_GROUPS, SG_GROUP_DIM)
    causal = jnp.tril(jnp.ones((CHUNK_2, CHUNK_2), dtype=bool))
    w = jnp.where(causal[None], w_s, jnp.zeros_like(w_s))
    mixed = jnp.einsum('gts,bcsgd->bctgd', w, v) + b_s.T[None, None, :, :, None]
    return u * mixed.reshape(B, S, SG_WIDTH)

def causal_block_attention(q, k, v):
    B, S, H, Dqk = q.shape
    Dv = v.shape[-1]
    nb = S // Q_BLOCK
    scale = Dqk ** -0.5
    qb = q.reshape(B, nb, Q_BLOCK, H, Dqk).transpose(1, 0, 2, 3, 4)
    kpos = jnp.arange(S)

    def one_block(args):
        i, qi = args
        s = jnp.einsum('bqhd,bkhd->bhqk', qi, k).astype(jnp.float32) * scale
        qpos = i * Q_BLOCK + jnp.arange(Q_BLOCK)
        mask = kpos[None, :] <= qpos[:, None]
        s = jnp.where(mask[None, None], s, NEG)
        p = jax.nn.softmax(s, axis=-1)
        return jnp.einsum('bhqk,bkhd->bqhd', p.astype(v.dtype), v)

    out = lax.map(one_block, (jnp.arange(nb), qb))
    return out.transpose(1, 0, 2, 3, 4).reshape(B, S, H * Dv)

def mla(c_q, c_kv, k_rope, positions, cq_norm, w_uq, ckv_norm, w_ukv, q_norm, k_norm):
    B, S, _ = c_q.shape
    q = (rmsnorm(c_q, cq_norm) @ w_uq).reshape(B, S, MLA_HEADS, MLA_QK)
    q = rmsnorm(q, q_norm)
    q = jnp.concatenate([q[..., :MLA_NOPE], rope(q[..., MLA_NOPE:], positions)], axis=-1)
    kv = (rmsnorm(c_kv, ckv_norm) @ w_ukv).reshape(B, S, MLA_HEADS, MLA_NOPE + MLA_V)
    k_nope, v = kv[..., :MLA_NOPE], kv[..., MLA_NOPE:]
    k_pe = jnp.broadcast_to(k_rope[:, :, None, :], (B, S, MLA_HEADS, MLA_ROPE))
    k = rmsnorm(jnp.concatenate([k_nope, k_pe], axis=-1), k_norm)
    k = jnp.concatenate([k[..., :MLA_NOPE], rope(k[..., MLA_NOPE:], positions)], axis=-1)
    return causal_block_attention(q, k, v)

def memory_attention(q_m, mem, mem_norm, w_kv, q_norm, k_norm):
    B, S, _ = q_m.shape
    q = rmsnorm(q_m.reshape(B, S, MEM_HEADS, MEM_HEAD_DIM), q_norm)
    kv = rmsnorm(mem, mem_norm) @ w_kv
    M = mem.shape[1]
    k = rmsnorm(kv[..., :MEM_WIDTH].reshape(B, M, MEM_HEADS, MEM_HEAD_DIM), k_norm)
    v = kv[..., MEM_WIDTH:].reshape(B, M, MEM_HEADS, MEM_HEAD_DIM)
    s = jnp.einsum('bshd,bmhd->bhsm', q, k).astype(jnp.float32) * (MEM_HEAD_DIM ** -0.5)
    p = jax.nn.softmax(s, axis=-1)
    return jnp.einsum('bhsm,bmhd->bshd', p.astype(v.dtype), v).reshape(B, S, MEM_WIDTH)

def second_inputs(seed: int = 0) -> dict:
    key = jax.random.key(seed)
    ks = iter(jax.random.split(key, 40))

    def nrm(shape, scale):
        return jax.random.normal(next(ks), shape, jnp.float32) * scale

    def gain(n):
        return 1.0 + nrm((DEPTH_2, n), 0.05)

    L = DEPTH_2
    d = D_MODEL
    x = nrm((BATCH, SEQ, d), 1.0)
    mem = nrm((BATCH, MEM_LEN, d), 1.0)
    offset = jax.random.randint(next(ks), (BATCH, 1), 0, 1024, dtype=jnp.int32)
    positions = offset + jnp.arange(SEQ, dtype=jnp.int32)[None, :]
    return {
        "x": x,
        "mem": mem,
        "positions": positions,
        "ffn1_norm": gain(d),
        "ffn1_w_gu": nrm((L, d, 2 * D_FF), d ** -0.5),
        "ffn1_w_down": nrm((L, D_FF, d), D_FF ** -0.5),
        "mix_norm": gain(d),
        "w_in": nrm((L, d, IN_COLS), d ** -0.5),
        "b_gate": nrm((L, N_BRANCH * d), 0.02),
        "sg_ln_g": gain(SG_WIDTH),
        "sg_ln_b": nrm((L, SG_WIDTH), 0.02),
        "sg_w": nrm((L, SG_GROUPS, CHUNK_2, CHUNK_2), 0.5 * CHUNK_2 ** -0.5),
        "sg_b": 1.0 + nrm((L, SG_GROUPS, CHUNK_2), 0.1),
        "mla_cq_norm": gain(MLA_Q_RANK),
        "mla_w_uq": nrm((L, MLA_Q_RANK, MLA_HEADS * MLA_QK), MLA_Q_RANK ** -0.5),
        "mla_ckv_norm": gain(MLA_KV_RANK),
        "mla_w_ukv": nrm((L, MLA_KV_RANK, MLA_HEADS * (MLA_NOPE + MLA_V)), MLA_KV_RANK ** -0.5),
        "mla_q_norm": gain(MLA_QK),
        "mla_k_norm": gain(MLA_QK),
        "mem_norm": gain(d),
        "mem_w_kv": nrm((L, d, 2 * MEM_WIDTH), d ** -0.5),
        "mem_q_norm": gain(MEM_HEAD_DIM),
        "mem_k_norm": gain(MEM_HEAD_DIM),
        "w_branch_a": nrm((L, SG_WIDTH, d), SG_WIDTH ** -0.5),
        "w_branch_b": nrm((L, MLA_WIDTH, d), MLA_WIDTH ** -0.5),
        "w_branch_c": nrm((L, MEM_WIDTH, d), MEM_WIDTH ** -0.5),
        "w_out": nrm((L, d, d), d ** -0.5),
        "ffn2_norm": gain(d),
        "ffn2_w_gu": nrm((L, d, 2 * D_FF), d ** -0.5),
        "ffn2_w_down": nrm((L, D_FF, d), D_FF ** -0.5),
    }

def second_block(x, mem, positions, ffn1_norm, ffn1_w_gu, ffn1_w_down, mix_norm, w_in, b_gate,
              sg_ln_g, sg_ln_b, sg_w, sg_b, mla_cq_norm, mla_w_uq, mla_ckv_norm, mla_w_ukv,
              mla_q_norm, mla_k_norm, mem_norm, mem_w_kv, mem_q_norm, mem_k_norm,
              w_branch_a, w_branch_b, w_branch_c, w_out, ffn2_norm, ffn2_w_gu, ffn2_w_down):
    B, S, _ = x.shape
    for l in range(DEPTH_2):
        x = x + 0.5 * swiglu(rmsnorm(x, ffn1_norm[l]), ffn1_w_gu[l], ffn1_w_down[l])
        h = rmsnorm(x, mix_norm[l])
        z = h @ w_in[l]
        u = jax.nn.gelu(z[..., COL_U:COL_V], approximate=False)
        v = jax.nn.gelu(z[..., COL_V:COL_CQ], approximate=False)
        y_a = spatial_gating(u, v, sg_ln_g[l], sg_ln_b[l], sg_w[l], sg_b[l])
        y_b = mla(z[..., COL_CQ:COL_CKV], z[..., COL_CKV:COL_KR], z[..., COL_KR:COL_QM], positions,
                  mla_cq_norm[l], mla_w_uq[l], mla_ckv_norm[l], mla_w_ukv[l],
                  mla_q_norm[l], mla_k_norm[l])
        y_c = memory_attention(z[..., COL_QM:COL_GATE], mem, mem_norm[l], mem_w_kv[l],
                               mem_q_norm[l], mem_k_norm[l])
        gates = jax.nn.sigmoid(z[..., COL_GATE:] + b_gate[l]).reshape(B, S, N_BRANCH, D_MODEL)
        merged = (gates[:, :, 0] * (y_a @ w_branch_a[l])
                  + gates[:, :, 1] * (y_b @ w_branch_b[l])
                  + gates[:, :, 2] * (y_c @ w_branch_c[l]))
        x = x + merged @ w_out[l]
        x = x + 0.5 * swiglu(rmsnorm(x, ffn2_norm[l]), ffn2_w_gu[l], ffn2_w_down[l])
    return x


def setup_inputs(seed=0):
    out = dict(first_inputs(seed))
    for name, value in second_inputs(seed + 1).items():
        if name != "x":
            out[name + "_2"] = value
    return out


def reference(
    x, meta_tokens, norm_w, gdn_w_in, gdn_conv_w, gdn_a_log, gdn_dt_bias, gdn_norm_w, gdn_w_out,
    ml_w_in, ml_gate_b, ml_norm_w, ml_w_out, ffn_w_up, ffn_conv_w, ffn_conv_b, ffn_w_down,
    mem_2, positions_2, ffn1_norm_2, ffn1_w_gu_2, ffn1_w_down_2, mix_norm_2, w_in_2, b_gate_2,
    sg_ln_g_2, sg_ln_b_2, sg_w_2, sg_b_2, mla_cq_norm_2, mla_w_uq_2, mla_ckv_norm_2,
    mla_w_ukv_2, mla_q_norm_2, mla_k_norm_2, mem_norm_2, mem_w_kv_2, mem_q_norm_2, mem_k_norm_2,
    w_branch_a_2, w_branch_b_2, w_branch_c_2, w_out_2, ffn2_norm_2, ffn2_w_gu_2, ffn2_w_down_2,
):
    x = first_block(
        x, meta_tokens, norm_w, gdn_w_in, gdn_conv_w, gdn_a_log, gdn_dt_bias, gdn_norm_w,
        gdn_w_out, ml_w_in, ml_gate_b, ml_norm_w, ml_w_out, ffn_w_up, ffn_conv_w, ffn_conv_b,
        ffn_w_down,
    )
    return second_block(
        x, mem_2, positions_2, ffn1_norm_2, ffn1_w_gu_2, ffn1_w_down_2, mix_norm_2, w_in_2,
        b_gate_2, sg_ln_g_2, sg_ln_b_2, sg_w_2, sg_b_2, mla_cq_norm_2, mla_w_uq_2,
        mla_ckv_norm_2, mla_w_ukv_2, mla_q_norm_2, mla_k_norm_2, mem_norm_2, mem_w_kv_2,
        mem_q_norm_2, mem_k_norm_2, w_branch_a_2, w_branch_b_2, w_branch_c_2, w_out_2,
        ffn2_norm_2, ffn2_w_gu_2, ffn2_w_down_2,
    )


_drawn_inputs = setup_inputs


def setup_inputs(seed=0):
    import zlib

    import numpy as np

    out = dict(_drawn_inputs(seed))
    spreads = {}
    factors = {'ffn_conv_b': 4.093,
     'ffn1_norm_2': 5.904,
     'mix_norm_2': 5.487,
     'b_gate_2': 8.0,
     'sg_ln_g_2': 22.352,
     'sg_ln_b_2': 47.763,
     'sg_b_2': 3.609,
     'mla_cq_norm_2': 8.0,
     'mla_ckv_norm_2': 8.0,
     'mla_q_norm_2': 8.0,
     'mla_k_norm_2': 8.0,
     'mem_norm_2': 8.0,
     'mem_q_norm_2': 8.0,
     'mem_k_norm_2': 8.0,
     'ffn2_norm_2': 6.057}
    for name, (base, spread) in spreads.items():
        noise = np.random.default_rng([zlib.crc32(name.encode()), seed]).standard_normal(out[name].shape)
        drawn = base * np.exp(spread * noise) if base else spread * noise
        out[name] = __import__('jax').numpy.asarray(drawn.astype(out[name].dtype))
    for name, factor in factors.items():
        out[name] = (out[name] * factor).astype(out[name].dtype)
    return out
```

```python
from contextlib import ExitStack

import numpy as np

import concourse.bass as bass
from concourse import mybir

F32 = mybir.dt.float32
I32 = mybir.dt.int32
ALU = mybir.AluOpType
ACT = mybir.ActivationFunctionType
AX_X = mybir.AxisListType.X

P = 128
D = 1024
DB = D // P
SEQ = 256
META = 16
T = META + SEQ
TILES = [(0, META), (META, P), (META + P, P)]
HQ, HV = 8, 16
FF = 2816
FB = FF // P
ML_H = 4
MLA_H, NOPE, ROPE, QK = 8, 64, 32, 96
MEM_H = 4
EPS = 1e-6
NEG = -1e30
TWO_PI_HI = 6.28125
TWO_PI_LO = float(np.float32(2 * np.pi - 6.28125))
ROUND = 12582912.0
PI_IN = 3.1415925

SLOTS = 4
SLOT = 4096
BANKS = 4

PHASES = [
    ("gdn_ba", 1, 1, 8), ("gdn_qkv", 8, 4, 32), ("gdn_z", 4, 4, 32), ("gdn_out", 4, 2, 32),
    ("up0", 11, 4, 32), ("down0", 8, 1, 22),
    ("ml_gates", 1, 1, 8), ("ml_in", 6, 4, 32), ("ml_out", 2, 4, 32),
    ("up1", 11, 4, 32), ("down1", 8, 1, 22),
    ("mem_k", 1, 4, 32), ("mem_v", 1, 2, 32),
    ("up2", 11, 4, 32), ("down2", 8, 1, 22),
    ("in_uv", 2, 4, 32), ("in_cq_kr", 1, 4, 32), ("in_qm", 1, 4, 32), ("in_ckv", 1, 2, 16),
    ("in_gates", 6, 4, 32), ("mla_q", 1, 8, 24), ("mla_kv", 1, 10, 24),
    ("branches", 4, 6, 24), ("mix_out", 2, 4, 32),
    ("up3", 11, 4, 32), ("down3", 8, 1, 22),
]


class Phase:
    def __init__(self, name, slabs, products, blocks, slab0, product0, word0):
        self.name, self.slabs, self.products, self.blocks = name, slabs, products, blocks
        self.slab0, self.product0, self.word0 = slab0, product0, word0
        self.end = product0 + slabs * products


def plan():
    out, slab, product, word = {}, 0, 0, 0
    for name, slabs, products, blocks in PHASES:
        out[name] = Phase(name, slabs, products, blocks, slab, product, word)
        slab += slabs
        product += slabs * products
        word += slabs * blocks * P * P
    return out, slab, word


PLAN, SLABS, STREAM_WORDS = plan()
SLAB_OF = [ph for ph in PLAN.values() for _ in range(ph.slabs)]

CONST_COLS, PARAM_COLS = {}, {}


def columns(table, sizes):
    at = 0
    for name, n in sizes:
        table[name] = (at, n)
        at += n
    return at


N_CONST = columns(CONST_COLS, [
    ("ident", P), ("ones", P), ("causal", T), ("level", 7 * P), ("rot", QK), ("inv_freq", 1),
    ("row_of", 31), ("score_mask", 3 * P), ("tri", P),
    ("l2_scale", 1)])
N_PARAM = columns(PARAM_COLS, [
    ("norm_w", 8 * DB), ("gdn_conv", 32 * 4), ("ffn_conv", 2 * 2 * FB * 3), ("ffn_bias", 2 * 2 * FB),
    ("gdn_norm", 1), ("a_log", 1), ("dt_bias", 1), ("ml_gate_i", 1), ("ml_gate_f", 1), ("ml_norm", 8),
    ("ffn1_norm", DB), ("mix_norm", DB), ("ffn2_norm", DB), ("mem_norm", DB), ("b_gate", 24),
    ("sg_g", 4), ("sg_b", 4), ("cq_norm", 3), ("ckv_norm", 2), ("q_norm", 1), ("k_norm", 1),
    ("mq_norm", 1), ("mk_norm", 1)])


class Steps:

    def __init__(self, make_sem, counts):
        self.make_sem, self.counts, self.sems = make_sem, counts, {}
        self.pos, self.seen = {}, {}

    def sem(self, name):
        if name not in self.sems:
            self.sems[name] = self.make_sem(name)
        return self.sems[name]

    def begin(self, name):
        self.pos[name] = 0

    def inc(self, ins, name, step=None):
        self.pos[name] = self.pos.get(name, 0) + 1
        if step is not None:
            key = (name, step)
            assert self.seen.get(key, self.pos[name]) == self.pos[name], key
            self.seen[key] = self.pos[name]
        self.seen[name] = max(self.seen.get(name, 0), self.pos[name])
        return ins.then_inc(self.sem(name), 1)

    def value(self, name, step, turn=0):
        per = self.counts.get(name, 1)
        at = per if step == "last" else self.counts.get((name, step), 1)
        if self.counts and step != "last" and (name, step) not in self.counts:
            raise KeyError((name, step))
        return at if isinstance(turn, int) and turn == 0 else turn * per + at

    def wait(self, eng, name, step="last", turn=0):
        v = self.value(name, step, turn)
        if not isinstance(v, int) or v > 0:
            eng.wait_ge(self.sem(name), v)

    def own(self, eng, name, turn=0):
        n = self.pos.get(name, 0)
        if n > 0:
            eng.wait_ge(self.sem(name), n if isinstance(turn, int) and turn == 0 else turn * self.counts.get(name, 1) + n)


def program(nc, x_t, meta_t, mem_t, positions, stream, consts, params, sg_w_t, sg_bias, out_t, counts):
    with ExitStack() as ctx:
        sem_list = []

        def make_sem(name):
            s = ctx.enter_context(nc.semaphore(name))
            sem_list.append(s)
            return s

        S = Steps(make_sem, counts)

        def sb(name, shape, dt=F32):
            return ctx.enter_context(nc.sbuf_tensor(name, shape, dt))

        ring = sb("ring", [P, SLOTS, SLOT])
        Cn = sb("consts_sb", [P, N_CONST])
        Pm = sb("params_sb", [P, N_PARAM])
        hs = sb("hs", [P, DB, T])
        a = sb("a", [P, DB, T])
        mix = sb("mix", [P, DB, T])
        sq = sb("sq", [P, DB, T])
        rs = sb("rs", [P, 2, T])
        work = sb("work", [P, 23100])
        ps = [ctx.enter_context(nc.psum_tensor(f"bank{i}", [P, 512], F32))[:, :] for i in range(8)]

        def cn(name, lo=0, n=None):
            at, size = CONST_COLS[name]
            return Cn[:, at + lo:at + lo + (size if n is None else n)]

        def pm(name, col=0):
            at, _ = PARAM_COLS[name]
            return Pm[:, at + col:at + col + 1]

        def area(at, *shape):
            n = int(np.prod(shape))
            v = work[:, at:at + n]
            if len(shape) == 2:
                v = v.rearrange("p (a b) -> p a b", b=shape[1])
            if len(shape) == 3:
                v = v.rearrange("p (a b c) -> p a b c", b=shape[1], c=shape[2])
            return v

        ident, ones = cn("ident"), cn("ones")
        weights_in = [S.sem(f"weights_in{i}") for i in range(SLOTS)]
        product_done = S.sem("product_done")
        bank_free = [S.sem(f"bank_free{i}") for i in range(BANKS)]
        small_in = S.sem("small_in")
        x_in = S.sem("x_in")

        class Unit:

            def __init__(self, ph, size, j, i, per_turn):
                self.j = j
                self.u = j if per_turn == 0 else i * per_turn + j
                self.first = ph.product0 + j * size
                self.more = 0 if per_turn == 0 else i * (per_turn * size)
                self.more4 = 0 if per_turn == 0 else i * (per_turn * size // BANKS)

            def ready(self, eng, m=0):
                eng.wait_ge(product_done, self.more + (self.first + m + 1))

            def bank(self, m=0):
                return ps[(self.first + m) % BANKS]

            def free(self, ins, m=0):
                return ins.then_inc(bank_free[(self.first + m) % BANKS], 1)

            def was_read(self, eng, m=0, before=0):
                b = self.first + m - before
                eng.wait_ge(bank_free[b % BANKS], self.more4 + (b // BANKS + 2))

        def each_product(eng, name, size, body, table=None):
            ph = PLAN[name]
            per_turn = SLOTS * ph.products // size
            total = ph.slabs * ph.products // size
            turns = ph.slabs // SLOTS
            done = 0
            if turns >= 2:
                if table is not None:
                    eng.preload_act_table(table)
                with eng.Fori(0, turns) as i:
                    for j in range(per_turn):
                        body(Unit(ph, size, j, i, per_turn))
                done = turns * per_turn
            for j in range(done, total):
                body(Unit(ph, size, j, 0, 0))

        def stream_pe(pe, name, rhs, n):
            ph = PLAN[name]
            kb = ph.blocks // ph.products

            def slab(j, i, looped):
                nslab = ph.slab0 + j
                arrived = 16 * (nslab // SLOTS + 1)
                pe.wait_ge(weights_in[nslab % SLOTS], i * 16 + arrived if looped else arrived)
                for m in range(ph.products):
                    b = ph.product0 + j * ph.products + m
                    free = b // BANKS + 1
                    pe.wait_ge(bank_free[b % BANKS], i * ph.products + free if looped else free)
                    for k in range(kb):
                        at = (m * kb + k) * P
                        mm = pe.matmul(ps[b % BANKS][:, 0:n], ring[:, nslab % SLOTS, at:at + P],
                                       rhs(m, k), start=(k == 0), stop=(k == kb - 1))
                    mm.then_inc(product_done, 1)

            turns, done = ph.slabs // SLOTS, 0
            if turns >= 2:
                with pe.Fori(0, turns) as i:
                    for j in range(SLOTS):
                        slab(j, i, True)
                done = turns * SLOTS
            for j in range(done, ph.slabs):
                slab(j, 0, False)

        STAT = ps[4]

        def norm_act(act, use, src, blocks, n):
            S.begin("norm_act")
            S.inc(act.activation(sq[:, 0:blocks, 0:n], src, ACT.Square), "norm_act", "squares")
            S.wait(act, "norm_dve", "mean", use)
            S.inc(act.activation(rs[:, 1, 0:n], rs[:, 0, 0:n], ACT.Sqrt), "norm_act", "root")

        def norm_pe(pe, use, blocks, n):
            S.begin("norm_pe")
            S.wait(pe, "norm_act", "squares", use)
            for k in range(blocks):
                mm = pe.matmul(STAT[:, 0:n], ones, sq[:, k, 0:n], start=(k == 0), stop=(k == blocks - 1))
            S.inc(mm, "norm_pe", "sums")

        def norm_dve(dve, use, width, n, src, gain, dst, blocks, add=None):
            S.begin("norm_dve")
            if use:
                S.wait(dve, "norm_dve", "done", use - 1)
            S.wait(dve, "norm_pe", "sums", use)
            S.inc(dve.tensor_scalar(rs[:, 0, 0:n], STAT[:, 0:n], 1.0 / width, EPS, ALU.mult, ALU.add), "norm_dve", "mean")
            S.wait(dve, "norm_act", "root", use)
            S.inc(dve.reciprocal(rs[:, 0, 0:n], rs[:, 1, 0:n]), "norm_dve", "rstd")
            S.wait(dve, "norm_dve", "rstd", use)
            for k in range(blocks):
                ins = dve.scalar_tensor_tensor(out=dst(k), in0=src(k), scalar=gain(k), in1=rs[:, 0, 0:n],
                                               op0=ALU.mult, op1=ALU.mult)
                if add is None and k == blocks - 2 or add is not None and k == blocks - 1:
                    S.inc(ins, "norm_dve", "scaled")
            if add is not None:
                S.wait(dve, "norm_dve", "scaled", use)
                ins = dve.tensor_tensor(add[0], add[0], add[1], ALU.add)
            S.inc(ins, "norm_dve", "done")

        rrow = sb("rrow", [HV, 2, T])

        def rown_act(act, use, squares, n, rows):
            S.begin("rown_act")
            for src, dst in squares:
                act.activation(dst, src, ACT.Square).then_inc(S.sem("rown_squares"), 1)
            S.wait(act, "rown_dve", "mean", use)
            S.inc(act.activation(rrow[0:rows, 1, 0:n], rrow[0:rows, 0, 0:n], ACT.Sqrt), "rown_act", "root")

        def rown_pe(pe, use, sqr, blocks, per_row, n, rows):
            S.begin("rown_pe")
            if use == 3:
                S.wait(pe, "mla_act", "ksq")
            else:
                pe.wait_ge(S.sem("rown_squares"), (1, 2, 3, 3, 5)[use])
            for k in range(blocks):
                src = sqr(k)
                h = k // per_row
                mm = pe.matmul(ps[4][0:rows, 0:n], cn("row_of", 15 - h, rows)[0:src.shape[0], :], src,
                               start=(k == 0), stop=(k == blocks - 1))
            S.inc(mm, "rown_pe", "sums")

        def rown_dve(dve, use, scale, eps, n, rows, after):
            S.begin("rown_dve")
            S.wait(dve, "rown_pe", "sums", use)
            S.inc(dve.tensor_scalar(rrow[0:rows, 0, 0:n], ps[4][0:rows, 0:n], scale, eps, ALU.mult, ALU.add), "rown_dve", "mean")
            S.wait(dve, "rown_act", "root", use)
            S.inc(dve.reciprocal(rrow[0:rows, 0, 0:n], rrow[0:rows, 1, 0:n]), "rown_dve")
            S.own(dve, "rown_dve", use)
            S.inc(dve.tensor_scalar(rrow[0:rows, 0, 0:n], rrow[0:rows, 0, 0:n], after, None, ALU.mult), "rown_dve", "rows")

        qkv = area(0, 32, T)
        raw_c = area(8704, 4, T + 3)
        conv_y = area(8704 + 4 * (T + 3), 4, T)
        rows_at = 8704 + 8 * T + 12
        R_BETA, R_G, R_EG, R_EGL, R_NBEG, R_X, R_Y, R_A, R_Z = range(9)
        row = [work[0:HV, rows_at + i * T:rows_at + (i + 1) * T] for i in range(9)]
        sqh = area(rows_at + 9 * T, 16, T)
        colv = sb("colv", [P, 3, 3, HV])
        colb = sb("colb", [P, 3, HV])

        bc = area(8704, 16, T)
        qn = area(8704 + 4352, 2, T)
        kn = area(8704 + 4896, 2, T)
        kbeta = area(8704 + 5440, 4, T)
        qd = area(8704 + 6528, 4, T)
        vs = area(8704 + 7616, 4, T)
        St = area(8704 + 8704, 4, P)
        par0 = 8704 + 9216
        mixw = mix[:, :, :].rearrange("p a b -> p (a b)")
        sqw = sq[:, :, :].rearrange("p a b -> p (a b)")
        names = ["vb", "nkbe", "ktl", "dec", "A0T", "attn", "X", "XT", "Am"]

        def tile4(v):
            return v.rearrange("p (a b) -> p a b", b=P)

        buf = [{n: area(par0 + 512 * i, 4, P) for i, n in enumerate(names)},
               {n: tile4(mixw[:, 512 * i:512 * (i + 1)]) if i < 4 else tile4(sqw[:, 512 * (i - 4):512 * (i - 3)])
                for i, n in enumerate(names[:8])}]
        buf[1]["Am"] = area(par0 + 512 * 9, 4, P)
        obc = area(8704, HV, T)
        osq = area(8704 + 16 * T, HV, T)
        zs = area(8704 + 32 * T, 4, T)

        hidden = area(0, FB, T)
        f_at = FB * T
        raw = [area(f_at + i * 2 * (T + 2), 2, T + 2) for i in range(2)]
        y_gu = [area(f_at + 4 * (T + 2) + i * 2 * T, 2, T) for i in range(2)]
        silu_g = [area(f_at + 4 * (T + 2) + (4 + i) * T, T) for i in range(2)]

        mlT = area(0, 24, T)
        v_tok = area(6528, 3, 8, P)
        bc2 = area(9600, 2, ML_H, T)
        mrow = [work[0:ML_H, 11776 + i * T:11776 + (i + 1) * T] for i in range(9)]
        M_LI, M_Y, M_E, M_ONE, M_B, M_C, M_M, M_EM, M_T = range(9)
        mcol = sb("mcol", [P, 3, ML_H])
        Wt = [[area(14300 + (3 * i + t) * T, T) for t in range(3)] for i in range(2)]
        Pt = [[area(14300 + (6 + 3 * i + t) * T, T) for t in range(3)] for i in range(2)]
        den = area(14300 + 12 * T, 2, T)
        hT = area(14300 + 14 * T, 8, T)
        mbc = area(9600, ML_H, T)
        hsq = area(0, 8, T)

        scratch = nc.dram_tensor("rows_scratch", (64, T), F32, kind="Internal").ap()
        scr_o = nc.dram_tensor("rows_scratch_o", (HV, T), F32, kind="Internal").ap()
        scr_m = nc.dram_tensor("rows_scratch_m", (2 * ML_H, T), F32, kind="Internal").ap()
        scr_h = nc.dram_tensor("rows_scratch_h", (ML_H, T), F32, kind="Internal").ap()
        scr_q = nc.dram_tensor("rows_scratch_q", (16, SEQ), F32, kind="Internal").ap()
        scr_c = nc.dram_tensor("rows_scratch_c", (8, SEQ), F32, kind="Internal").ap()

        def on_all(ap_tensor, offset, *dims):
            return bass.AP(ap_tensor.tensor, offset, [[0, P], *[list(d) for d in dims]])

        PSA, PSB, PSC, PSD = ps[4], ps[5], ps[6], ps[7]

        def b4(v, c):
            return v.rearrange("p (a b) -> p a b", b=P)[:, :, 0:c]

        BA = Unit(PLAN["gdn_ba"], 1, 0, 0, 0)

        def rows_act(act):
            BA.ready(act)
            S.inc(act.activation(row[R_BETA], BA.bank()[0:HV, 0:T], ACT.Sigmoid), "rows_act", "beta")
            S.wait(act, "rows_dve", "x")
            S.inc(act.activation(row[R_Y], row[R_X], ACT.Abs), "rows_act", "abs")
            S.own(act, "rows_act")
            S.inc(act.activation(row[R_Y], row[R_Y], ACT.Exp, scale=-1.0), "rows_act")
            S.inc(act.activation(row[R_A][:, 0:1], pm("a_log")[0:HV, :], ACT.Exp), "rows_act")
            S.own(act, "rows_act")
            S.inc(act.activation(row[R_Y], row[R_Y], ACT.Ln, bias=1.0), "rows_act", "ln")
            S.wait(act, "rows_dve", "diff")
            S.inc(act.activation(row[R_EG], row[R_G], ACT.Exp), "rows_act")
            S.inc(act.activation(row[R_EGL], row[R_EGL], ACT.Exp), "rows_act", "exps")

        def rows_dve(dve):
            BA.ready(dve)
            S.wait(dve, "rows_act", "beta")
            BA.free(dve.tensor_scalar(row[R_Z], BA.bank()[32:32 + HV, 0:T], pm("dt_bias")[0:HV, :], None, ALU.add))
            BA.was_read(dve)
            S.inc(dve.tensor_copy(row[R_X], row[R_Z]), "rows_dve", "x")
            S.wait(dve, "rows_act", "ln")
            S.inc(dve.scalar_tensor_tensor(out=row[R_Z], in0=row[R_X], scalar=0.0, in1=row[R_Y], op0=ALU.max, op1=ALU.add), "rows_dve")
            S.own(dve, "rows_dve")
            S.inc(dve.tensor_scalar(row[R_X], row[R_Z], row[R_A][:, 0:1], -1.0, ALU.mult, ALU.mult), "rows_dve")
            S.inc(dve.memset(row[R_Y], 1.0), "rows_dve")
            S.own(dve, "rows_dve")
            for t0, c in TILES:
                S.inc(dve.tensor_tensor_scan(row[R_G][:, t0:t0 + c], row[R_Y][:, t0:t0 + c], row[R_X][:, t0:t0 + c], 0.0,
                                             ALU.mult, ALU.add), "rows_dve")
            S.own(dve, "rows_dve")
            for t0, c in TILES:
                S.inc(dve.tensor_scalar(row[R_EGL][:, t0:t0 + c], row[R_G][:, t0:t0 + c], row[R_G][:, t0 + c - 1:t0 + c], -1.0,
                                        ALU.subtract, ALU.mult), "rows_dve", "diff" if t0 == TILES[-1][0] else None)
            S.wait(dve, "rows_act", "exps")
            S.inc(dve.scalar_tensor_tensor(out=row[R_NBEG], in0=row[R_BETA], scalar=-1.0, in1=row[R_EG], op0=ALU.mult, op1=ALU.mult),
                  "rows_dve", "rows")

        def rows_pe(pe):
            S.wait(pe, "rows_dve", "rows")
            for c, (t0, n) in enumerate(TILES):
                for q, r in enumerate((R_BETA, R_G, R_EGL, R_NBEG)):
                    mm = pe.transpose(PSB[0:n, (c * 4 + q) * HV:(c * 4 + q + 1) * HV], row[r][:, t0:t0 + n], ident[0:HV, 0:HV])
            S.inc(mm, "rows_pe")

        def cols_dve(dve):
            S.wait(dve, "rows_pe")
            for c, (t0, n) in enumerate(TILES):
                src = PSB[0:n, c * 64:c * 64 + 64].rearrange("p (a b) -> p a b", b=HV)
                S.inc(dve.tensor_copy(colv[0:n, c, :, :], src[:, 0:3, :]), "cols_dve")
                S.inc(dve.tensor_copy(colb[0:n, c, :], src[:, 3, :]), "cols_dve")

        CONV_AHEAD = 4

        def qkv_act(act):
            def body(un):
                S.wait(act, "qkv_dve", turn=un.u)
                un.ready(act)
                un.free(act.activation(raw_c[:, un.j % 4, 3:T + 3], un.bank()[:, 0:T], ACT.Copy))
                S.begin("qkv_act")
                S.wait(act, "qkv_dve", turn=un.u + CONV_AHEAD)
                S.inc(act.activation(qkv[:, un.u, :], conv_y[:, un.j % 4, :], ACT.Silu), "qkv_act", "silu")
            each_product(act, "gdn_qkv", 1, body, ACT.Silu)

        def qkv_dve(dve):
            at, n = PARAM_COLS["gdn_conv"]
            taps = Pm[:, at:at + n].rearrange("p (b t) -> p b t", t=4)

            def body(un):
                S.begin("qkv_dve")
                un.was_read(dve)
                S.wait(dve, "qkv_act", turn=un.u)
                y, r = conv_y[:, un.j % 4, :], raw_c[:, un.j % 4, :]
                S.inc(dve.tensor_scalar(y, r[:, 0:T], taps[:, un.u, 0:1], None, ALU.mult), "qkv_dve")
                for t in (1, 2, 3):
                    S.own(dve, "qkv_dve", un.u + CONV_AHEAD)
                    S.inc(dve.scalar_tensor_tensor(out=y, in0=r[:, t:t + T], scalar=taps[:, un.u, t:t + 1], in1=y,
                                                   op0=ALU.mult, op1=ALU.add), "qkv_dve")
            each_product(dve, "gdn_qkv", 1, body)

        LEVELS = {META: 4, P: 7}
        lvl = cn("level").rearrange("p (l b) -> p l b", b=P)

        def par(c):
            return c % 2

        def bank(c, i):
            return ps[4 * (c % 2) + i]

        def pair(v):
            return v.unsqueeze(2).broadcast_to([v.shape[0], 2, 2, v.shape[-1]])

        def quad(v):
            return v.rearrange("p (a b) n -> p a b n", b=2)

        def over4(v):
            return v.unsqueeze(1).broadcast_to([v.shape[0], 4, v.shape[-1]])

        def down4(v, n):
            return v.unsqueeze(2).broadcast_to([v.shape[0], 4, n])

        def scan_order():
            yield "setup", 0, 0
            for l in range(1, LEVELS[META]):
                yield "level", 0, l
            yield "finish", 0, 0
            yield "setup", 1, 0
            yield "setup", 2, 0
            for l in range(1, LEVELS[P]):
                yield "level", 1, l
                yield "level", 2, l
            yield "finish", 1, 0
            yield "finish", 2, 0

        def last_level(c):
            return LEVELS[TILES[c][1]] - 1

        def scan_pool(pool):
            for g in range(1):
                S.wait(pool, "rows_dve", "rows")
                S.wait(pool, "rown_dve", "rows", 0)
            for q, src in enumerate((rrow[:, 0, :], row[R_BETA], row[R_G], row[R_EG])):
                pool.dma_start(scratch[16 * q:16 * q + 16, :], src).then_inc(S.sem("scan_rows_out"), 16)
            pool.wait_ge(S.sem("scan_rows_out"), 64)
            S.wait(pool, "cols_dve")
            with pool.Fori(0, 4) as g:
                S.begin("scan_pool")
                pool.wait_ge(S.sem("group_done"), g + 1)
                pool.dma_start(bc[:, 0:2, :], on_all(scratch, g * (2 * T), (T, 2), (1, T))).then_inc(S.sem("bc_in"), 16)
                pool.dma_start(bc[:, 2:4, :], on_all(scratch, g * (2 * T) + 8 * T, (T, 2), (1, T))).then_inc(S.sem("bc_in"), 16)
                pool.dma_start(bc[:, 4:16, :].rearrange("p (a b) t -> p a b t", b=4),
                               on_all(scratch, g * (4 * T) + 16 * T, (16 * T, 3), (T, 4), (1, T))).then_inc(S.sem("bc_in"), 16)
                S.inc(pool.tensor_copy(vs, work[:, 16 * T:32 * T].rearrange("p (g h t) -> p g h t", h=4, t=T)[:, g, :, :]), "scan_pool", "v")
                S.wait(pool, "scan_dve", "kn", g)
                S.inc(pool.tensor_tensor(quad(kbeta), pair(kn), quad(bc[:, 4:8, :]), ALU.mult), "scan_pool", "kbeta")
                S.inc(pool.tensor_tensor(quad(qd), pair(qn), quad(bc[:, 12:16, :]), ALU.mult), "scan_pool", "qd")
                for what, c, l in scan_order():
                    t0, n = TILES[c]
                    B = buf[par(c)]
                    if what == "finish" or (what == "level" and l > last_level(c)):
                        continue
                    if what == "setup":
                        S.wait(pool, "scan_dve", f"A0T{c}", g)
                    else:
                        if l == 1:
                            S.wait(pool, "scan_dve", f"XT{c}.0", g)
                        else:
                            S.wait(pool, "scan_pe", f"Y{c}.{l - 1}", g)
                    S.inc(pool.tensor_tensor(B["Am"][0:n, :, 0:n], B["A0T"][0:n, :, 0:n], over4(lvl[0:n, l, 0:n]), ALU.mult),
                          "scan_pool", f"Am{c}.{l}")

        def scan_dve(dve):
            with dve.Fori(0, 4) as g:
                S.begin("scan_dve")
                dve.wait_ge(S.sem("bc_in"), g * 48 + 48)
                own = lambda: S.own(dve, "scan_dve", g)
                inc = lambda ins, step=None: S.inc(ins, "scan_dve", step)
                qk = work[:, 0:16 * T].rearrange("p (s g h t) -> p s g h t", s=2, h=2, t=T)
                inc(dve.tensor_tensor(qn, qk[:, 0, g, :, :], bc[:, 0:2, :], ALU.mult))
                inc(dve.tensor_tensor(kn, qk[:, 1, g, :, :], bc[:, 2:4, :], ALU.mult), "kn")
                cv = colv[:, :, :, :].rearrange("p c q (g h) -> p c q g h", h=4)
                cb = colb[:, :, :].rearrange("p c (g h) -> p c g h", h=4)
                for what, c, l in scan_order():
                    t0, n = TILES[c]
                    B = buf[par(c)]
                    if what == "setup":
                        inc(dve.tensor_tensor(B["dec"][0:n, :, 0:n], bc[0:n, 8:12, t0:t0 + n], over4(cn("causal")[0:n, 0:n]), ALU.add))
                        own()
                        inc(dve.tensor_tensor(B["dec"][0:n, :, 0:n], B["dec"][0:n, :, 0:n], down4(cv[0:n, c, 1, g, :], n), ALU.subtract),
                            f"diff{c}")
                        S.wait(dve, "scan_pe", f"tok{c}", g)
                        inc(dve.tensor_tensor(B["vb"][0:n], tile4(bank(c, 1)[0:n, :]), down4(cv[0:n, c, 0, g, :], P), ALU.mult))
                        kt = pair(bank(c, 0)[0:n, 0:2 * P].rearrange("p (a b) -> p a b", b=P))
                        inc(dve.tensor_tensor(quad(B["nkbe"][0:n]), kt, quad(down4(cb[0:n, c, g, :], P)), ALU.mult))
                        inc(dve.tensor_tensor(quad(B["ktl"][0:n]), kt, quad(down4(cv[0:n, c, 2, g, :], P)), ALU.mult), f"ktl{c}")
                        S.wait(dve, "scan_pe", f"kq{c}", g)
                        S.wait(dve, "scan_act", f"dec{c}", g)
                        inc(dve.tensor_tensor(B["A0T"][0:n, :, 0:n], b4(bank(c, 2)[0:n, :], n), B["dec"][0:n, :, 0:n], ALU.mult), f"A0T{c}")
                        inc(dve.tensor_tensor(quad(B["attn"][0:n, :, 0:n]), pair(b4(bank(c, 3)[0:n, 0:2 * P], n)),
                                              quad(B["dec"][0:n, :, 0:n]), ALU.mult), f"attn{c}")
                        S.wait(dve, "scan_pool", f"Am{c}.0", g)
                        inc(dve.tensor_tensor(B["XT"][0:n, :, 0:n], over4(ident[0:n, 0:n]), B["Am"][0:n, :, 0:n], ALU.subtract), f"XT{c}.0")
                    elif what == "level" and l <= last_level(c):
                        if l < last_level(c):
                            S.wait(dve, "scan_pe", f"XX{c}.{l}", g)
                            inc(dve.tensor_tensor(B["X"][0:n, :, 0:n], B["X"][0:n, :, 0:n], b4(bank(c, 1)[0:n, :], n), ALU.subtract))
                        S.wait(dve, "scan_pe", f"XXT{c}.{l}", g)
                        inc(dve.tensor_tensor(B["XT"][0:n, :, 0:n], B["XT"][0:n, :, 0:n], b4(bank(c, 2)[0:n, :], n), ALU.subtract), f"XT{c}.{l}")
                    elif what == "finish" and c < 2:
                        S.wait(dve, "scan_pe", f"S{c}", g)
                        if c == 0:
                            inc(dve.tensor_copy(St, tile4(bank(c, 3))), f"S{c}")
                        else:
                            gt = bc[:, 12:16, t0 + n - 1:t0 + n].broadcast_to([P, 4, P])
                            inc(dve.tensor_tensor(St, St, gt, ALU.mult))
                            own()
                            inc(dve.tensor_tensor(St, St, tile4(bank(c, 3)), ALU.add), f"S{c}")
                S.wait(dve, "scan_act", "last", g)
                S.wait(dve, "scan_pool", "last", g)
                own()
                dve.tensor_copy(rs[:, 0, 0:1], rs[:, 0, 1:2]).then_inc(S.sem("group_done"), 1)
                dve.wait_ge(S.sem("group_done"), g + 2)

        def scan_act(act):
            act.preload_act_table(ACT.Exp)
            with act.Fori(0, 4) as g:
                S.begin("scan_act")
                act.wait_ge(S.sem("group_done"), g + 1)
                inc = lambda ins, step=None: S.inc(ins, "scan_act", step)
                for what, c, l in scan_order():
                    t0, n = TILES[c]
                    B = buf[par(c)]
                    if what == "setup":
                        S.wait(act, "scan_dve", f"diff{c}", g)
                        inc(act.activation(B["dec"][0:n, :, 0:n], B["dec"][0:n, :, 0:n], ACT.Exp), f"dec{c}")
                        S.wait(act, "scan_pe", f"X{c}", g)
                        inc(act.activation(B["X"][0:n, :, 0:n], b4(bank(c, 0)[0:n, :], n), ACT.Copy), f"X{c}")
                    elif what == "level" and l <= last_level(c):
                        S.wait(act, "scan_pe", f"Y{c}.{l}", g)
                        inc(act.activation(B["dec"][0:n, :, 0:n], b4(bank(c, 0)[0:n, :], n), ACT.Copy), f"Y{c}.{l}")
                    elif what == "finish":
                        if c > 0:
                            S.wait(act, "scan_pe", f"wT{c}", g)
                            inc(act.activation(B["Am"][:, :, 0:n], b4(bank(c, 0), n), ACT.Copy), f"wT{c}")
                        S.wait(act, "scan_pe", f"vn{c}", g)
                        inc(act.activation(B["X"][0:n], tile4(bank(c, 1)[0:n, :]), ACT.Copy), f"vn{c}")
                        S.wait(act, "scan_pe", f"o{c}", g)
                        dst = work[:, 16 * T:32 * T].rearrange("p (g h t) -> p g h t", h=4, t=T)[:, g, :, t0:t0 + n]
                        inc(act.activation(dst, b4(bank(c, 2), n), ACT.Copy), f"o{c}")

        def scan_pe(pe):
            def settle(c, bank_):
                if TILES[c][1] < P:
                    pe.matmul(bank_[0:META, 0:1], ones[:, 0:META], ones[:, 0:1], start=True, stop=True)

            with pe.Fori(0, 4) as g:
                S.begin("scan_pe")
                inc = lambda ins, step=None: S.inc(ins, "scan_pe", step)
                S.wait(pe, "scan_dve", "kn", g)
                S.wait(pe, "scan_pool", "qd", g)
                for what, c, l in scan_order():
                    t0, n = TILES[c]
                    B = buf[par(c)]
                    hs4 = range(4)
                    if what == "setup":
                        if c == 2:
                            S.wait(pe, "scan_act", "o0", g)
                            S.wait(pe, "scan_dve", "S0", g)
                        for h in range(2):
                            pe.transpose(bank(c, 0)[0:n, h * P:(h + 1) * P], kn[:, h, t0:t0 + n], ident)
                        for h in hs4:
                            mm = pe.transpose(bank(c, 1)[0:n, h * P:(h + 1) * P], vs[:, h, t0:t0 + n], ident)
                        inc(mm, f"tok{c}")
                        for h in hs4:
                            pe.matmul(bank(c, 2)[0:n, h * P:h * P + n], kn[:, h // 2, t0:t0 + n], kbeta[:, h, t0:t0 + n], start=True, stop=True)
                        for h in range(2):
                            mm = pe.matmul(bank(c, 3)[0:n, h * P:h * P + n], kn[:, h, t0:t0 + n], qn[:, h, t0:t0 + n], start=True, stop=True)
                        inc(mm, f"kq{c}")
                        S.wait(pe, "scan_dve", f"XT{c}.0", g)
                        settle(c, bank(c, 0))
                        for h in hs4:
                            mm = pe.transpose(bank(c, 0)[0:n, h * P:h * P + n], B["XT"][0:n, h, 0:n], ident[0:n, 0:n])
                        inc(mm, f"X{c}")
                    elif what == "level" and l <= last_level(c):
                        S.wait(pe, "scan_pool", f"Am{c}.{l}", g)
                        if l == 1:
                            S.wait(pe, "scan_act", f"X{c}", g)
                        S.wait(pe, "scan_dve", f"XT{c}.{l - 1}", g)
                        settle(c, bank(c, 0))
                        for h in hs4:
                            mm = pe.matmul(bank(c, 0)[0:n, h * P:h * P + n], B["Am"][0:n, h, 0:n], B["X"][0:n, h, 0:n], start=True, stop=True)
                        inc(mm, f"Y{c}.{l}")
                        S.wait(pe, "scan_act", f"Y{c}.{l}", g)
                        settle(c, bank(c, 1 if l < last_level(c) else 2))
                        if l < last_level(c):
                            for h in hs4:
                                mm = pe.matmul(bank(c, 1)[0:n, h * P:h * P + n], B["XT"][0:n, h, 0:n], B["dec"][0:n, h, 0:n], start=True, stop=True)
                            inc(mm, f"XX{c}.{l}")
                        for h in hs4:
                            mm = pe.matmul(bank(c, 2)[0:n, h * P:h * P + n], B["dec"][0:n, h, 0:n], B["XT"][0:n, h, 0:n], start=True, stop=True)
                        inc(mm, f"XXT{c}.{l}")
                    elif what == "finish":
                        S.wait(pe, "scan_dve", f"XT{c}.{last_level(c)}", g)
                        settle(c, bank(c, 1))
                        if c > 0:
                            for h in hs4:
                                mm = pe.matmul(bank(c, 0)[:, h * P:h * P + n], B["nkbe"][0:n, h, :], B["XT"][0:n, h, 0:n], start=True, stop=True)
                            inc(mm, f"wT{c}")
                            S.wait(pe, "scan_act", f"wT{c}", g)
                            S.wait(pe, "scan_dve", f"S{c - 1}", g)
                        for h in hs4:
                            out = bank(c, 1)[0:n, h * P:(h + 1) * P]
                            mm = pe.matmul(out, B["XT"][0:n, h, 0:n], B["vb"][0:n, h, :], start=True, stop=(c == 0))
                            if c > 0:
                                mm = pe.matmul(out, B["Am"][:, h, 0:n], St[:, h, :], start=False, stop=True)
                        inc(mm, f"vn{c}")
                        S.wait(pe, "scan_act", f"vn{c}", g)
                        for h in hs4:
                            out = bank(c, 2)[:, h * P:h * P + n]
                            if c > 0:
                                pe.matmul(out, St[:, h, :], qd[:, h, t0:t0 + n], start=True, stop=False)
                            mm = pe.matmul(out, B["X"][0:n, h, :], B["attn"][0:n, h, 0:n], start=(c == 0), stop=True)
                        inc(mm, f"o{c}")
                        if c < 2:
                            for h in hs4:
                                mm = pe.matmul(bank(c, 3)[:, h * P:(h + 1) * P], B["ktl"][0:n, h, :], B["X"][0:n, h, :], start=True, stop=True)
                            inc(mm, f"S{c}")
                pe.wait_ge(S.sem("group_done"), g + 2)

        def gate_pool(pool):
            S.wait(pool, "rown_dve", "rows", 1)
            pool.dma_start(scr_o, rrow[:, 0, :]).then_inc(S.sem("o_rows_out"), 16)
            pool.wait_ge(S.sem("o_rows_out"), 16)
            pool.dma_start(obc, on_all(scr_o, 0, (T, HV), (1, T))).then_inc(S.sem("o_rows_in"), 16)

        def gate_act(act):
            def body(un):
                un.ready(act)
                if un.j >= 4:
                    S.wait(act, "gate_dve", turn=un.u - 4)
                un.free(act.activation(zs[:, un.j % 4, :], un.bank()[:, 0:T], ACT.Silu))
            each_product(act, "gdn_z", 1, body)

        def gate_dve(dve):
            dve.wait_ge(S.sem("o_rows_in"), 16)

            def body(un):
                S.begin("gate_dve")
                o = qkv[:, 16 + un.u, :]
                S.inc(dve.scalar_tensor_tensor(out=o, in0=o, scalar=pm("gdn_norm"), in1=obc[:, un.u, :], op0=ALU.mult, op1=ALU.mult), "gate_dve")
                S.own(dve, "gate_dve", un.u)
                un.was_read(dve)
                S.inc(dve.tensor_tensor(o, o, zs[:, un.j % 4, :], ALU.mult), "gate_dve")
            each_product(dve, "gdn_z", 1, body)

        def evac_mix_act(act, name):
            each_product(act, name, 1, lambda un: (un.ready(act), un.free(act.activation(mix[:, un.u, :], un.bank()[:, 0:T], ACT.Copy))))

        def mix_was_read(eng, name):
            for j in range(4, 8):
                Unit(PLAN[name], 1, j, 0, 0).was_read(eng)

        def conv_up_act(act, layer):
            def body(un):
                p2 = un.j % 2
                S.wait(act, "up_dve", turn=un.u + 22 * layer)
                for m in range(2):
                    un.ready(act, m)
                    un.free(act.activation(raw[p2][:, m, 2:T + 2], un.bank(m)[:, 0:T], ACT.Copy), m)
                S.begin("up_act")
                S.wait(act, "up_dve", turn=un.u + 22 * layer + 2)
                S.wait(act, "up_pool", turn=un.u + 22 * layer)
                S.inc(act.activation(silu_g[p2], y_gu[p2][:, 0, :], ACT.Silu), "up_act")
            each_product(act, f"up{layer}", 2, body, ACT.Silu)

        def conv_up_dve(dve, layer):
            at, n = PARAM_COLS["ffn_conv"]
            taps = Pm[:, at + n // 2 * layer:at + n // 2 * (layer + 1)].rearrange("p (b m t) -> p b m t", m=2, t=3)
            at, n = PARAM_COLS["ffn_bias"]
            bias = Pm[:, at + n // 2 * layer:at + n // 2 * (layer + 1)].rearrange("p (b m) -> p b m", m=2)

            def body(un):
                p2 = un.j % 2
                S.begin("up_dve")
                S.wait(dve, "up_act", turn=un.u + 22 * layer)
                S.wait(dve, "up_pool", turn=un.u + 22 * layer)
                for t in range(3):
                    if t:
                        S.own(dve, "up_dve", un.u + 22 * layer + 2)
                    for m in range(2):
                        y, r = y_gu[p2][:, m, :], raw[p2][:, m, t:t + T]
                        if t == 0:
                            un.was_read(dve, m)
                            S.inc(dve.tensor_scalar(y, r, taps[:, un.u, m, 0:1], bias[:, un.u, m:m + 1], ALU.mult, ALU.add), "up_dve")
                        else:
                            S.inc(dve.scalar_tensor_tensor(out=y, in0=r, scalar=taps[:, un.u, m, t:t + 1], in1=y,
                                                           op0=ALU.mult, op1=ALU.add), "up_dve")
            each_product(dve, f"up{layer}", 2, body)

        def conv_up_pool(pool, layer):
            def body(un):
                S.begin("up_pool")
                S.wait(pool, "up_act", turn=un.u + 22 * layer + 2)
                S.inc(pool.tensor_tensor(hidden[:, un.u, :], silu_g[un.j % 2], y_gu[un.j % 2][:, 1, :], ALU.mult), "up_pool")
            each_product(pool, f"up{layer}", 2, body)
        MG = Unit(PLAN["ml_gates"], 1, 0, 0, 0)

        def ml_rows_act(act):
            inc = lambda ins, step=None: S.inc(ins, "mlr_act", step)
            S.wait(act, "mlr_dve", "raw")
            inc(act.activation(mrow[M_Y], mrow[M_Y], ACT.Tanh, scale=1.0 / 15.0))
            inc(act.activation(mrow[M_LI], mrow[M_LI], ACT.Tanh, scale=1.0 / 15.0), "tanh")
            S.own(act, "mlr_act")
            inc(act.activation(mrow[M_E], mrow[M_Y], ACT.Abs))
            S.own(act, "mlr_act")
            inc(act.activation(mrow[M_E], mrow[M_E], ACT.Exp, scale=-15.0))
            S.own(act, "mlr_act")
            inc(act.activation(mrow[M_E], mrow[M_E], ACT.Ln, bias=1.0), "ln")
            S.wait(act, "mlr_dve", "m")
            inc(act.activation(mrow[M_EM], mrow[M_T], ACT.Exp, scale=-1.0), "em")

        def ml_rows_dve(dve):
            inc = lambda ins, step=None: S.inc(ins, "mlr_dve", step)
            own = lambda: S.own(dve, "mlr_dve")
            MG.ready(dve)
            inc(dve.tensor_scalar(mrow[M_LI], MG.bank()[0:ML_H, 0:T], pm("ml_gate_i")[0:ML_H, :], None, ALU.add))
            own()
            MG.free(dve.tensor_scalar(mrow[M_T], MG.bank()[32:32 + ML_H, 0:T], pm("ml_gate_f")[0:ML_H, :], None, ALU.add))
            MG.was_read(dve)
            inc(dve.tensor_copy(mrow[M_Y], mrow[M_T]), "raw")
            inc(dve.memset(mrow[M_ONE], 1.0))
            S.wait(dve, "mlr_act", "ln")
            own()
            inc(dve.tensor_scalar(mrow[M_T], mrow[M_Y], 15.0, 0.0, ALU.mult, ALU.min))
            own()
            inc(dve.tensor_tensor(mrow[M_C], mrow[M_T], mrow[M_E], ALU.subtract))
            own()
            inc(dve.tensor_tensor_scan(mrow[M_B], mrow[M_ONE], mrow[M_C], 0.0, ALU.mult, ALU.add))
            own()
            inc(dve.scalar_tensor_tensor(out=mrow[M_C], in0=mrow[M_LI], scalar=15.0, in1=mrow[M_B], op0=ALU.mult, op1=ALU.subtract), "c")
            own()
            inc(dve.tensor_tensor_scan(mrow[M_M], mrow[M_ONE], mrow[M_C], 0.0, ALU.mult, ALU.max))
            own()
            inc(dve.tensor_tensor(mrow[M_T], mrow[M_B], mrow[M_M], ALU.add), "m")

        def ml_rows_pe(pe):
            S.wait(pe, "mlr_dve", "c")
            for c, (t0, n) in enumerate(TILES):
                mm = pe.transpose(PSB[0:n, c * ML_H:(c + 1) * ML_H], mrow[M_C][:, t0:t0 + n], ident[0:ML_H, 0:ML_H])
            S.inc(mm, "mlr_pe")

        def ml_cols_dve(dve):
            S.wait(dve, "mlr_pe")
            for c, (t0, n) in enumerate(TILES):
                S.inc(dve.tensor_copy(mcol[0:n, c, :], PSB[0:n, c * ML_H:(c + 1) * ML_H]), "mcol_dve")

        def ml_pool(pool):
            S.wait(pool, "mlr_act", "em")
            pool.dma_start(scr_m[0:ML_H, :], mrow[M_M]).then_inc(S.sem("ml_rows_out"), 16)
            pool.dma_start(scr_m[ML_H:2 * ML_H, :], mrow[M_EM]).then_inc(S.sem("ml_rows_out"), 16)
            pool.wait_ge(S.sem("ml_rows_out"), 32)
            pool.dma_start(bc2, on_all(scr_m, 0, (ML_H * T, 2), (T, ML_H), (1, T))).then_inc(S.sem("ml_rows_in"), 16)

        def ml_in_act(act):
            def body(un):
                un.ready(act)
                un.free(act.activation(mlT[:, un.u, :], un.bank()[:, 0:T], ACT.Copy if un.j < 16 else ACT.Sigmoid))
            each_product(act, "ml_in", 1, body)

        def ml_read(eng, last):
            for j in range(last - 4, last):
                Unit(PLAN["ml_in"], 1, j, 0, 0).was_read(eng)

        def ml_pe(pe):
            inc = lambda ins, step=None: S.inc(ins, "ml_pe", step)
            ml_read(pe, 24)
            for c, (t0, n) in enumerate(TILES):
                for k in range(8):
                    mm = pe.transpose(ps[4 + k // 4][0:n, (k % 4) * P:(k % 4 + 1) * P], mlT[:, 8 + k, t0:t0 + n], ident)
                    if k % 4 == 3:
                        inc(mm, f"v{c}.{k // 4}")
                if c < 2:
                    S.wait(pe, "ml_act", f"v{c}.1")
            S.wait(pe, "ml_act", "v2.1")
            for h in range(ML_H):
                bank4 = ps[4 * (h % 2):4 * (h % 2) + 4]
                if h >= 2:
                    S.wait(pe, "ml_dve", f"h{h - 2}")
                for c, (t0, n) in enumerate(TILES):
                    if c > 0:
                        S.wait(pe, "ml_dve", f"P{h}.{c - 1}")
                    inc(pe.matmul(bank4[0][0:n, 0:T - t0], mlT[:, 4 + h, t0:t0 + n], mlT[:, h, t0:T], start=True, stop=True), f"S{h}.{c}")
                for c, (t0, n) in enumerate(TILES):
                    S.wait(pe, "ml_dve", f"P{h}.{c}")
                    Pm_ = Pt[h % 2][c][0:n, 0:T - t0]
                    kw = dict(start=(c == 0), stop=(c == 2))
                    pe.matmul(bank4[1][:, t0:T], v_tok[0:n, c, 2 * h, :], Pm_, **kw)
                    pe.matmul(bank4[2][:, t0:T], v_tok[0:n, c, 2 * h + 1, :], Pm_, **kw)
                    mm = pe.matmul(bank4[3][:, t0:T], ones[0:n, :], Pm_, **kw)
                inc(mm, f"num{h}")

        def ml_act(act):
            inc = lambda ins, step=None: S.inc(ins, "ml_act", step)
            for c, (t0, n) in enumerate(TILES):
                for q in range(2):
                    S.wait(act, "ml_pe", f"v{c}.{q}")
                    inc(act.activation(v_tok[0:n, c, 4 * q:4 * q + 4, :], tile4(ps[4 + q][0:n, :]), ACT.Copy), f"v{c}.{q}")
            for h in range(ML_H):
                for c, (t0, n) in enumerate(TILES):
                    S.wait(act, "ml_dve", f"D{h}.{c}")
                    w = Wt[h % 2][c][0:n, 0:T - t0]
                    inc(act.activation(w, w, ACT.Exp, bias=mcol[0:n, c, h:h + 1]), f"W{h}.{c}")

        def ml_dve(dve):
            inc = lambda ins, step=None: S.inc(ins, "ml_dve", step)
            own = lambda: S.own(dve, "ml_dve")
            dve.wait_ge(S.sem("ml_rows_in"), 16)
            S.own(dve, "mcol_dve")

            def distances(h):
                for c, (t0, n) in enumerate(TILES):
                    inc(dve.scalar_tensor_tensor(out=Wt[h % 2][c][0:n, 0:T - t0], in0=bc2[0:n, 0, h, t0:T], scalar=-1.0,
                                                 in1=cn("causal")[0:n, 0:T - t0], op0=ALU.mult, op1=ALU.add), f"D{h}.{c}")

            distances(0)
            for h in range(ML_H):
                for c, (t0, n) in enumerate(TILES):
                    S.wait(dve, "ml_pe", f"S{h}.{c}")
                    S.wait(dve, "ml_act", f"W{h}.{c}")
                    inc(dve.scalar_tensor_tensor(out=Pt[h % 2][c][0:n, 0:T - t0], in0=ps[4 * (h % 2)][0:n, 0:T - t0], scalar=P ** -0.5,
                                                 in1=Wt[h % 2][c][0:n, 0:T - t0], op0=ALU.mult, op1=ALU.mult), f"P{h}.{c}")
                if h + 1 < ML_H:
                    own()
                    distances(h + 1)
                S.wait(dve, "ml_pe", f"num{h}")
                own()
                dn = ps[4 * (h % 2) + 3][:, 0:T]
                inc(dve.scalar_tensor_tensor(out=den[:, 0, :], in0=dn, scalar=-1.0, in1=bc2[:, 1, h, :], op0=ALU.mult, op1=ALU.max))
                own()
                inc(dve.tensor_tensor(den[:, 0, :], den[:, 0, :], dn, ALU.max))
                own()
                inc(dve.reciprocal(den[:, 1, :], den[:, 0, :]))
                own()
                inc(dve.tensor_tensor(hT[:, 2 * h, :], ps[4 * (h % 2) + 1][:, 0:T], den[:, 1, :], ALU.mult))
                inc(dve.tensor_tensor(hT[:, 2 * h + 1, :], ps[4 * (h % 2) + 2][:, 0:T], den[:, 1, :], ALU.mult), f"h{h}")
            own()

        def ml_norm_pool(pool):
            S.wait(pool, "rown_dve", "rows", 2)
            pool.dma_start(scr_h, rrow[0:ML_H, 0, :]).then_inc(S.sem("ml_norm_out"), 16)
            pool.wait_ge(S.sem("ml_norm_out"), 16)
            pool.dma_start(mbc, on_all(scr_h, 0, (T, ML_H), (1, T))).then_inc(S.sem("ml_norm_in"), 16)

        def ml_norm_dve(dve):
            dve.wait_ge(S.sem("ml_norm_in"), 16)
            for k in range(8):
                S.inc(dve.scalar_tensor_tensor(out=hT[:, k, :], in0=hT[:, k, :], scalar=pm("ml_norm", k), in1=mbc[:, k // 2, :],
                                               op0=ALU.mult, op1=ALU.mult), "mln_dve")
            S.own(dve, "mln_dve")
            S.inc(dve.tensor_tensor(hT, hT, mlT[:, 16:24, :], ALU.mult), "mln_dve")

        h2 = hs[:, :, META:T]
        mem_sb = area(0, DB, SEQ)
        memn = area(2048, DB, SEQ)
        kmem = area(4096, MEM_H, SEQ)
        vmem = area(5120, 2, 512)
        keep_at = 6144
        hid2 = area(keep_at, FB, SEQ)
        sg2 = [area(keep_at + FB * SEQ + i * SEQ, SEQ) for i in range(4)]

        def mem_pool(pool):
            S.wait(pool, "norm_dve", "done", 7)
            pool.dma_start(mem_sb, mem_t.rearrange("(k p) t -> p k t", p=P)).then_inc(S.sem("mem_in"), 16)

        def mem_act(act):
            act.wait_ge(S.sem("mem_in"), 16)
            norm_act(act, 8, mem_sb, 8, SEQ)
            ph = PLAN["mem_k"]
            for j in range(4):
                un = Unit(ph, 1, j, 0, 0)
                un.ready(act)
                un.free(act.activation(kmem[:, j, :], un.bank()[:, 0:SEQ], ACT.Copy))
            for j in range(2):
                un = Unit(PLAN["mem_v"], 1, j, 0, 0)
                un.ready(act)
                un.free(act.activation(vmem[:, j, :], un.bank()[:, :], ACT.Copy))

        def mem_pe(pe):
            norm_pe(pe, 8, 8, SEQ)
            S.wait(pe, "norm_dve", "done", 8)
            stream_pe(pe, "mem_k", lambda m, k: memn[:, k, :], SEQ)
            ph = PLAN["mem_v"]
            pe.wait_ge(weights_in[ph.slab0 % SLOTS], 16 * (ph.slab0 // SLOTS + 1))
            for m in range(2):
                b = ph.product0 + m
                pe.wait_ge(bank_free[b % BANKS], b // BANKS + 1)
                for k in range(8):
                    mm = pe.matmul(ps[b % BANKS][:, :], memn[:, k, m * P:(m + 1) * P], ring[:, ph.slab0 % SLOTS, k * 512:(k + 1) * 512],
                                   start=(k == 0), stop=(k == 7))
                mm.then_inc(product_done, 1)

        def up_act(act, name):
            def body(un):
                un.ready(act)
                un.was_read(act, 1, before=8)
                un.free(act.activation(sg2[un.j % 4], un.bank()[:, 0:SEQ], ACT.Silu))
            each_product(act, name, 2, body, ACT.Silu)

        def up_dve(dve, name):
            def body(un):
                un.ready(dve, 1)
                un.was_read(dve, 0)
                un.free(dve.tensor_tensor(hid2[:, un.u, :], un.bank(1)[:, 0:SEQ], sg2[un.j % 4], ALU.mult), 1)
            each_product(dve, name, 2, body)

        def down_dve(dve, name):
            each_product(dve, name, 1, lambda un: (
                un.ready(dve), un.free(dve.scalar_tensor_tensor(out=h2[:, un.u, :], in0=un.bank()[:, 0:SEQ], scalar=0.5,
                                                                in1=h2[:, un.u, :], op0=ALU.mult, op1=ALU.add))))

        def phase_read(eng, name, upto=None):
            ph = PLAN[name]
            total = ph.slabs * ph.products if upto is None else upto
            for j in range(max(0, total - 4), total):
                Unit(ph, 1, j, 0, 0).was_read(eng)

        u_at = 6144
        uT = area(u_at, 4, SEQ)
        vT = area(u_at + 1024, 4, SEQ)
        cqT = area(u_at + 2048, 4, SEQ)
        qmT = area(u_at + 3072, MEM_H, SEQ)
        ckvT = area(u_at + 4096, 2, SEQ)
        gat = area(u_at + 4608, 24, SEQ)
        br_at = u_at + 4608 + 6144
        yT = [area(br_at + i * 1024, 4, SEQ) for i in range(3)]
        t_at = br_at + 3072
        sq2 = sq[:, :, :].rearrange("p a b -> p (a b)")
        mix2 = mix[:, :, :].rearrange("p a b -> p (a b)")
        a2 = a[:, :, :].rearrange("p a b -> p (a b)")

        def in_act(act):
            for name, fn, dst in (("in_uv", ACT.Gelu, lambda j: (uT if j < 4 else vT)[:, j % 4, :]),
                                  ("in_cq_kr", ACT.Copy, lambda j: cqT[:, j, :]),
                                  ("in_qm", ACT.Copy, lambda j: qmT[:, j, :]),
                                  ("in_ckv", ACT.Copy, lambda j: ckvT[:, j, :])):
                ph = PLAN[name]
                for j in range(ph.slabs * ph.products):
                    un = Unit(ph, 1, j, 0, 0)
                    un.ready(act)
                    un.free(act.activation(dst(j), un.bank()[:, 0:SEQ], fn))
            ph = PLAN["in_gates"]
            for j in range(24):
                un = Unit(ph, 1, j, 0, 0)
                un.ready(act)
                un.free(act.activation(gat[:, j, :], un.bank()[:, 0:SEQ], ACT.Sigmoid, bias=pm("b_gate", j)))

        Wsg = area(t_at, 8, P)
        sg_tok = area(t_at + 1024, 2, 512)
        sg_bt = area(t_at + 2048, 4, P)
        vln = mix2[:, 0:1024].rearrange("p (a b) -> p a b", b=SEQ)
        rstat = mix2[:, 1024:2048].rearrange("p (a b) -> p a b", b=SEQ)

        def sg_pool(pool):
            pool.dma_start(Wsg, sg_w_t).then_inc(S.sem("sg_in"), 16)
            for half in range(2):
                pool.dma_start(sg_bt[64 * half:64 * half + 64, :, :],
                               bass.AP(sg_bias.tensor, half * P, [[0, 64], [2 * P, 4], [1, P]])).then_inc(S.sem("sg_in"), 16)

        def sg_pe(pe):
            inc = lambda ins, step=None: S.inc(ins, "sg_pe", step)
            for k in range(4):
                mm = pe.matmul(PSA[:, 0:SEQ], ones, vT[:, k, :], start=(k == 0), stop=(k == 3))
            inc(mm, "mean")
            S.wait(pe, "sg_act", "squares")
            for k in range(4):
                mm = pe.matmul(PSB[:, 0:SEQ], ones, sq[:, k, 0:SEQ], start=(k == 0), stop=(k == 3))
            inc(mm, "var")
            S.wait(pe, "sg_dve", "vln")
            for c in range(2):
                for k in range(4):
                    mm = pe.transpose(ps[6 + c][:, k * P:(k + 1) * P], vln[:, k, c * P:(c + 1) * P], ident)
                inc(mm, f"tok{c}")
            S.wait(pe, "sg_dve", "w")
            for k in range(4):
                if k == 0:
                    S.wait(pe, "sg_act", "tok1")
                if k >= 2:
                    S.wait(pe, "sg_dve", f"y{k - 2}")
                out = ps[4 + k % 2]
                for c in range(2):
                    for q in range(2):
                        mm = pe.matmul(out[64 * q:64 * q + 64, c * P:(c + 1) * P], sg_tok[:, c, (2 * k + q) * 64:(2 * k + q + 1) * 64],
                                       Wsg[:, 2 * k + q, :], start=True, stop=True)
                inc(mm, f"mix{k}")

        def sg_act(act):
            inc = lambda ins, step=None: S.inc(ins, "sg_act", step)
            S.wait(act, "sg_dve", "centred")
            inc(act.activation(sq[:, 0:4, 0:SEQ], vT, ACT.Square), "squares")
            S.wait(act, "sg_dve", "var")
            inc(act.activation(rstat[:, 2, :], rstat[:, 1, :], ACT.Sqrt), "root")
            for c in range(2):
                S.wait(act, "sg_pe", f"tok{c}")
                inc(act.activation(sg_tok[:, c, :], ps[6 + c], ACT.Copy), f"tok{c}")

        def sg_dve(dve):
            inc = lambda ins, step=None: S.inc(ins, "sg_dve", step)
            own = lambda: S.own(dve, "sg_dve")
            S.wait(dve, "sg_pe", "mean")
            inc(dve.tensor_scalar(rstat[:, 0, :], PSA[:, 0:SEQ], 1.0 / 512, None, ALU.mult))
            own()
            inc(dve.tensor_tensor(vT, vT, rstat[:, 0, :].unsqueeze(1).broadcast_to([P, 4, SEQ]), ALU.subtract), "centred")
            S.wait(dve, "sg_pe", "var")
            inc(dve.tensor_scalar(rstat[:, 1, :], PSB[:, 0:SEQ], 1.0 / 512, EPS, ALU.mult, ALU.add), "var")
            S.wait(dve, "sg_act", "root")
            inc(dve.reciprocal(rstat[:, 3, :], rstat[:, 2, :]))
            own()
            for k in range(4):
                inc(dve.scalar_tensor_tensor(out=vln[:, k, :], in0=vT[:, k, :], scalar=pm("sg_g", k), in1=rstat[:, 3, :], op0=ALU.mult, op1=ALU.mult))
            own()
            for k in range(4):
                inc(dve.tensor_scalar(vln[:, k, :], vln[:, k, :], pm("sg_b", k), None, ALU.add), "vln" if k == 3 else None)
            dve.wait_ge(S.sem("sg_in"), 48)
            inc(dve.tensor_tensor(Wsg, Wsg, cn("tri").unsqueeze(1).broadcast_to([P, 8, P]), ALU.mult), "w")
            for k in range(4):
                S.wait(dve, "sg_pe", f"mix{k}")
                y = yT[0][:, k, :].rearrange("p (a b) -> p a b", b=P)
                inc(dve.tensor_tensor(y, ps[4 + k % 2][:, 0:SEQ].rearrange("p (a b) -> p a b", b=P),
                                      sg_bt[:, k, :].unsqueeze(1).broadcast_to([P, 2, P]), ALU.add))
                own()
                inc(dve.tensor_tensor(yT[0][:, k, :], yT[0][:, k, :], uT[:, k, :], ALU.mult), f"y{k}")
            own()

        cqn = mix2[:, 0:768].rearrange("p (a b) -> p a b", b=SEQ)
        ckvn = mix2[:, 768:1280].rearrange("p (a b) -> p a b", b=SEQ)
        trig = a2[:, 0:6 * SEQ].rearrange("p (a b) -> p a b", b=SEQ)
        pos_i = sb("pos_i", [P, SEQ], I32)
        qk16 = area(0, 16, SEQ)
        sq_q = area(u_at, 8, SEQ)
        sq_k = sq2[:, 0:2048].rearrange("p (a b) -> p a b", b=SEQ)
        vtk = area(t_at, 2, 512)
        prob = [area(t_at + 1024 + 512 * i, 512) for i in range(2)]
        probT = [area(t_at + 2048 + 512 * i, 512) for i in range(2)]
        soft = sb("soft", [P, 2, 4, 2])

        def rope_pool(pool):
            pool.dma_start(pos_i[0:QK, :], bass.AP(positions.tensor, 0, [[0, QK], [1, SEQ]])).then_inc(S.sem("pos_in"), 16)

        def rope_dve(dve):
            inc = lambda ins, step=None: S.inc(ins, "rope_dve", step)
            own = lambda: S.own(dve, "rope_dve")
            t = lambda i: trig[0:QK, i, :]
            dve.wait_ge(S.sem("pos_in"), 16)
            inc(dve.tensor_copy(t(1), pos_i[0:QK, :]))
            own()
            inc(dve.tensor_scalar(t(0), t(1), cn("inv_freq")[0:QK, :], None, ALU.mult))
            own()
            for i, quarter in ((2, 0.0), (3, 0.25)):
                inc(dve.tensor_scalar(t(1), t(0), 1.0 / (2 * np.pi), quarter, ALU.mult, ALU.add))
                own()
                inc(dve.tensor_scalar(t(4), t(1), ROUND, None, ALU.add))
                own()
                inc(dve.tensor_scalar(t(1), t(4), -ROUND, None, ALU.add))
                own()
                inc(dve.scalar_tensor_tensor(out=t(4), in0=t(1), scalar=-TWO_PI_HI, in1=t(0), op0=ALU.mult, op1=ALU.add))
                own()
                inc(dve.scalar_tensor_tensor(out=t(i), in0=t(1), scalar=-TWO_PI_LO, in1=t(4), op0=ALU.mult, op1=ALU.add))
                own()
                if quarter:
                    inc(dve.tensor_scalar(t(i), t(i), float(np.pi / 2), None, ALU.add))
                    own()
                inc(dve.tensor_scalar(t(i), t(i), PI_IN, -PI_IN, ALU.min, ALU.max), "args" if quarter else None)
                own()

        def rope_act(act):
            S.wait(act, "rope_dve", "args")
            S.inc(act.activation(trig[0:QK, 2:4, :], trig[0:QK, 2:4, :], ACT.Sin), "rope_act")

        MQ, MK = PLAN["mla_q"], PLAN["mla_kv"]

        def mla_in_pe(pe):
            stream_pe(pe, "mla_q", lambda m, k: cqn[:, k, :], SEQ)
            S.wait(pe, "norm_dve", "done", 12)
            slot = MK.slab0 % SLOTS
            pe.wait_ge(weights_in[slot], 16 * (MK.slab0 // SLOTS + 1))
            for m in range(10):
                b = MK.product0 + m
                pe.wait_ge(bank_free[b % BANKS], b // BANKS + 1)
                for k in range(2):
                    if m < 8:
                        mm = pe.matmul(ps[b % BANKS][:, 0:SEQ], ring[:, slot, (2 * m + k) * P:(2 * m + k + 1) * P], ckvn[:, k, :],
                                       start=(k == 0), stop=(k == 1))
                    else:
                        mm = pe.matmul(ps[b % BANKS][:, :], ckvn[:, k, (m - 8) * P:(m - 7) * P],
                                       ring[:, slot, (16 + 4 * k) * P:(20 + 4 * k) * P], start=(k == 0), stop=(k == 1))
                mm.then_inc(product_done, 1)
            rown_pe(pe, 3, lambda k: (sq_q if k < 8 else sq_k)[0:QK, k % 8, :], 16, 1, SEQ, 16)
            for i in range(8):
                if i == 0:
                    S.wait(pe, "mla_dve", "gained")
                    S.wait(pe, "rown_dve", "mean", 3)
                if i >= 2:
                    S.wait(pe, "mla_dve", f"rope{i - 2}")
                S.inc(pe.matmul(ps[4 + i % 2][0:QK, :], cn("rot")[0:QK, :], qk16[0:QK, 2 * i:2 * i + 2, :].rearrange("p a b -> p (a b)"),
                                start=True, stop=True), "mla_pe", f"rot{i}")

        def mla_in_act(act):
            inc = lambda ins, step=None: S.inc(ins, "mla_act", step)
            for h in range(8):
                un = Unit(MQ, 1, h, 0, 0)
                un.ready(act)
                inc(act.activation(sq_q[0:QK, h, :], un.bank()[0:QK, 0:SEQ], ACT.Square))
                un.free(act.activation(qk16[0:QK, h, :], un.bank()[0:QK, 0:SEQ], ACT.Identity, scale=pm("q_norm")[0:QK, :]))
            for h in range(8):
                Unit(MK, 1, h, 0, 0).was_read(act)
                inc(act.activation(sq_k[0:QK, h, :], qk16[0:QK, 8 + h, :], ACT.Square), "ksq" if h == 7 else None)
            for c in range(2):
                un = Unit(MK, 1, 8 + c, 0, 0)
                un.ready(act)
                un.free(act.activation(vtk[:, c, :], un.bank(), ACT.Copy))

        def mla_in_dve(dve):
            inc = lambda ins, step=None: S.inc(ins, "mla_dve", step)
            own = lambda: S.own(dve, "mla_dve")
            for h in range(8):
                un = Unit(MK, 1, h, 0, 0)
                un.ready(dve)
                un.free(dve.tensor_tensor(qk16[0:QK, 8 + h, :], un.bank()[0:QK, 0:SEQ], cqT[0:QK, 3, :], ALU.add))
            S.wait(dve, "mla_act", "ksq")
            inc(dve.tensor_scalar(qk16[0:QK, 8:16, :], qk16[0:QK, 8:16, :], pm("k_norm")[0:QK, :], None, ALU.mult), "gained")

        def mla_rope_dve(dve):
            inc = lambda ins, step=None: S.inc(ins, "mla_dve", step)
            own = lambda: S.own(dve, "mla_dve")
            dve.wait_ge(S.sem("mla_rows_in"), 32)
            S.wait(dve, "rope_act")
            both = lambda v: v.unsqueeze(1).broadcast_to([QK, 2, SEQ])
            for i in range(8):
                x = qk16[0:QK, 2 * i:2 * i + 2, :]
                tmp = prob[i % 2][0:QK, :].rearrange("p (a b) -> p a b", b=SEQ)
                S.wait(dve, "mla_pe", f"rot{i}")
                inc(dve.tensor_tensor(tmp, ps[4 + i % 2][0:QK, :].rearrange("p (a b) -> p a b", b=SEQ), both(trig[0:QK, 2, :]), ALU.mult), f"rope{i}")
                inc(dve.tensor_tensor(x, x, both(trig[0:QK, 3, :]), ALU.mult))
                own()
                inc(dve.tensor_tensor(x, x, tmp, ALU.add))
                own()
                inc(dve.tensor_tensor(x, x, (sq_q if i < 4 else sq_k)[0:QK, 2 * i % 8:2 * i % 8 + 2, :], ALU.mult), "heads" if i == 7 else None)
            own()

        def mla_pool(pool):
            S.wait(pool, "rown_dve", "rows", 3)
            pool.dma_start(scr_q, rrow[:, 0, 0:SEQ]).then_inc(S.sem("mla_rows_out"), 16)
            pool.wait_ge(S.sem("mla_rows_out"), 16)
            pool.dma_start(sq_q, on_all(scr_q, 0, (SEQ, 8), (1, SEQ))).then_inc(S.sem("mla_rows_in"), 16)
            pool.dma_start(sq_k, on_all(scr_q, 8 * SEQ, (SEQ, 8), (1, SEQ))).then_inc(S.sem("mla_rows_in"), 16)

        def memq_act(act):
            rown_act(act, 4, [(qmT, sq_k[:, 0:4, :]), (kmem, sq_k[:, 4:8, :])], SEQ, 8)

        def memq_dve(dve):
            dve.wait_ge(S.sem("mem_rows_in"), 16)
            for h in range(4):
                for x, gain, off in ((qmT, "mq_norm", 0), (kmem, "mk_norm", 4)):
                    S.inc(dve.scalar_tensor_tensor(out=x[:, h, :], in0=x[:, h, :], scalar=pm(gain), in1=sq_q[:, off + h, :],
                                                   op0=ALU.mult, op1=ALU.mult), "memq_dve")
            S.own(dve, "memq_dve")

        def memq_pool(pool):
            S.wait(pool, "rown_dve", "rows", 4)
            pool.dma_start(scr_c, rrow[0:8, 0, 0:SEQ]).then_inc(S.sem("mem_rows_out"), 16)
            pool.wait_ge(S.sem("mem_rows_out"), 16)
            pool.dma_start(sq_q, on_all(scr_c, 0, (SEQ, 8), (1, SEQ))).then_inc(S.sem("mem_rows_in"), 16)

        def attention(eng, engine, kind):
            causal = kind == "mla"
            H = MLA_H if causal else MEM_H
            scale = (QK if causal else P) ** -0.5
            rows = QK if causal else P
            inc = lambda ins, step=None: S.inc(ins, f"{kind}att_{engine}", step)
            wait = lambda other, step: S.wait(eng, f"{kind}att_{other}", step)
            own = lambda: S.own(eng, f"{kind}att_{engine}")
            q = (lambda h: qk16[0:rows, h, :]) if causal else (lambda h: qmT[:, h, :])
            k = (lambda h: qk16[0:rows, 8 + h, :]) if causal else (lambda h: kmem[:, h, :])
            v = (lambda h, c: vtk[:, c, 64 * h:64 * h + 64]) if causal else (lambda h, c: vmem[:, c, P * h:P * h + P])
            part = ((0, P), (P, 3 * P)) if causal else ((0, 2 * P), (2 * P, 4 * P))
            end = part[1][1]

            def out(h):
                return (ps[7][64 * (h % 2):64 * (h % 2) + 64, 0:SEQ], yT[1][64 * (h % 2):64 * (h % 2) + 64, h // 2, :]) if causal \
                    else (ps[7][:, 0:SEQ], yT[2][:, h, :])

            if engine == "pe":
                def scores(h):
                    if h >= 2:
                        wait(*(("dve", f"read{h - 2}") if causal else ("act", f"e{h - 2}")))
                    for i, (lo, hi) in enumerate(part):
                        mm = eng.matmul(ps[4 + h % 2][:, lo:hi], q(h)[:, i * P:(i + 1) * P], k(h)[:, 0:hi - lo], start=True, stop=True)
                    inc(mm, f"s{h}")
                scores(0)
                for h in range(H):
                    if h + 1 < H:
                        scores(h + 1)
                    wait("dve", f"p{h}")
                    if h >= 1:
                        wait("act", f"pt{h - 1}")
                    for i in range(2):
                        for kt in range(2):
                            if causal and kt > i:
                                continue
                            mm = eng.transpose(ps[6][:, kt * SEQ + i * P:kt * SEQ + (i + 1) * P],
                                               prob[h % 2][:, part[i][0] + kt * P:part[i][0] + (kt + 1) * P], ident)
                    inc(mm, f"t{h}")
                    wait("act", f"pt{h}")
                    if h >= 1:
                        wait("act", f"o{h - 1}")
                    o, _ = out(h)
                    eng.matmul(o, v(h, 0), probT[h % 2][:, 0:SEQ], start=True, stop=False)
                    if causal:
                        mm = eng.matmul(o[:, P:SEQ], v(h, 1), probT[h % 2][:, SEQ + P:2 * SEQ], start=False, stop=True)
                    else:
                        mm = eng.matmul(o, v(h, 1), probT[h % 2][:, SEQ:2 * SEQ], start=False, stop=True)
                    inc(mm, f"pv{h}")
            if engine == "dve":
                for h in range(H + 1):
                    if h < H:
                        st = soft[:, h % 2]
                        wait("pe", f"s{h}")
                        if h >= 2:
                            wait("pe", f"t{h - 2}")
                        if causal:
                            inc(eng.tensor_tensor(prob[h % 2][:, 0:end], ps[4 + h % 2][:, 0:end], cn("score_mask"), ALU.add), f"read{h}")
                            own()
                            for i, (lo, hi) in enumerate(part):
                                inc(eng.tensor_reduce(st[:, 0, i:i + 1], prob[h % 2][:, lo:hi], AX_X, ALU.max))
                        else:
                            inc(eng.tensor_reduce(st[:, 0, :], ps[4 + h % 2].rearrange("p (a b) -> p a b", b=SEQ), AX_X, ALU.max))
                        own()
                        inc(eng.tensor_scalar(st[:, 1, :], st[:, 0, :], -scale, None, ALU.mult), f"n{h}")
                    if h >= 1:
                        g = h - 1
                        st = soft[:, g % 2]
                        wait("act", f"e{g}")
                        inc(eng.reciprocal(st[:, 3, :], st[:, 2, :]))
                        own()
                        for i, (lo, hi) in enumerate(part):
                            inc(eng.tensor_scalar(prob[g % 2][:, lo:hi], prob[g % 2][:, lo:hi], st[:, 3, i:i + 1], None, ALU.mult), f"p{g}" if i else None)
            if engine == "act":
                def finish(g):
                    wait("pe", f"t{g}")
                    if causal:
                        inc(eng.activation(probT[g % 2][:, 0:SEQ], ps[6][:, 0:SEQ], ACT.Copy))
                        inc(eng.activation(probT[g % 2][:, SEQ + P:2 * SEQ], ps[6][:, SEQ + P:2 * SEQ], ACT.Copy), f"pt{g}")
                    else:
                        inc(eng.activation(probT[g % 2], ps[6], ACT.Copy), f"pt{g}")
                    wait("pe", f"pv{g}")
                    o, dst = out(g)
                    inc(eng.activation(dst, o, ACT.Copy), f"o{g}")
                for h in range(H + 1):
                    if h < H:
                        st = soft[:, h % 2]
                        wait("dve", f"n{h}")
                        for i, (lo, hi) in enumerate(part):
                            src = prob[h % 2] if causal else ps[4 + h % 2]
                            inc(eng.activation(prob[h % 2][:, lo:hi], src[:, lo:hi], ACT.Exp, bias=st[:, 1, i:i + 1], scale=scale,
                                               accum_out=st[:, 2, i:i + 1]), f"e{h}" if i else None)
                    if h >= 1:
                        finish(h - 1)

        merged = area(u_at, 8, SEQ)

        def branches_dve(dve):
            t1 = [mix2[:, i * SEQ:(i + 1) * SEQ] for i in range(2)]

            def body(un):
                c = un.j
                for m in range(3):
                    un.ready(dve, m)
                    if m and c:
                        S.own(dve, "merge_dve")
                    un.free(dve.tensor_tensor(merged[:, c, :] if m == 0 else t1[m - 1], un.bank(m)[:, 0:SEQ], gat[:, 8 * m + c, :], ALU.mult), m)
                un.was_read(dve, 0)
                un.was_read(dve, 1)
                S.inc(dve.tensor_tensor(merged[:, c, :], merged[:, c, :], t1[0], ALU.add), "merge_dve")
                un.was_read(dve, 2)
                S.own(dve, "merge_dve")
                S.inc(dve.tensor_tensor(merged[:, c, :], merged[:, c, :], t1[1], ALU.add), "merge_dve")
            for j in range(8):
                body(Unit(PLAN["branches"], 3, j, 0, 0))

        def mix_out_dve(dve):
            each_product(dve, "mix_out", 1, lambda un: (
                un.ready(dve), un.free(dve.tensor_tensor(h2[:, un.u, :], un.bank()[:, 0:SEQ], h2[:, un.u, :], ALU.add))))

        block = ctx.enter_context(nc.Block())
        H1 = lambda k: hs[:, k, :]
        A1 = lambda k: a[:, k, :]
        M1 = lambda k: mix[:, k, :]
        H2 = lambda k: h2[:, k, :]
        A2 = lambda k: a[:, k, 0:SEQ]
        gain = lambda name, base=0: (lambda k: pm(name, base + k))

        @block.sync
        def _(sp):
            sp.dma_start(Cn[:, :], consts).then_inc(S.sem("small_in"), 16)
            sp.dma_start(Pm[:, :], params).then_inc(S.sem("small_in"), 16)
            word = 0
            for n, ph in enumerate(SLAB_OF):
                size = ph.blocks * P
                if n >= SLOTS:
                    old = SLAB_OF[n - SLOTS]
                    sp.wait_ge(product_done, old.product0 + (n - SLOTS - old.slab0 + 1) * old.products)
                sp.dma_start(ring[:, n % SLOTS, 0:size],
                             stream[word:word + P * size].rearrange("(p c) -> p c", p=P)).then_inc(weights_in[n % SLOTS], 16)
                word += P * size
            phase_read(sp, "down3")
            sp.dma_start(out_t.rearrange("(k p) t -> p k t", p=P), h2).then_inc(S.sem("out_stored"), 16)
            sp.wait_ge(S.sem("out_stored"), 16)

        @block.gpsimd
        def _(pool):
            pool.dma_start(hs[:, :, META:T], x_t.rearrange("(k p) t -> p k t", p=P)).then_inc(S.sem("x_in"), 16)
            pool.dma_start(hs[:, :, 0:META], meta_t.rearrange("(k p) t -> p k t", p=P)).then_inc(S.sem("x_in"), 16)
            scan_pool(pool)
            gate_pool(pool)
            conv_up_pool(pool, 0)
            ml_pool(pool)
            ml_norm_pool(pool)
            conv_up_pool(pool, 1)
            mem_pool(pool)
            phase_read(pool, "down2")
            sg_pool(pool)
            rope_pool(pool)
            mla_pool(pool)
            memq_pool(pool)

        @block.scalar
        def _(act):
            act.wait_ge(S.sem("small_in"), 32)
            act.wait_ge(S.sem("x_in"), 32)
            norm_act(act, 0, hs[:, :, :], 8, T)
            rows_act(act)
            qkv_act(act)
            S.wait(act, "qkv_act", turn=31 + CONV_AHEAD)
            rown_act(act, 0, [(qkv[:, 0:16, :], sqh)], T, 16)
            scan_act(act)
            S.wait(act, "scan_act", "last", 3)
            rown_act(act, 1, [(qkv[:, 16:32, :], osq)], T, 16)
            gate_act(act)
            evac_mix_act(act, "gdn_out")
            for layer in range(2):
                if layer:
                    norm_act(act, 4, hs[:, :, :], 8, T)
                    ml_rows_act(act)
                    ml_in_act(act)
                    ml_act(act)
                    S.wait(act, "ml_dve")
                    rown_act(act, 2, [(hT, hsq)], T, ML_H)
                    evac_mix_act(act, "ml_out")
                mix_was_read(act, "gdn_out" if layer == 0 else "ml_out")
                norm_act(act, 1 + 4 * layer, mix[:, :, :], 8, T)
                S.wait(act, "norm_dve", "done", 1 + 4 * layer)
                norm_act(act, 2 + 4 * layer, hs[:, :, :], 8, T)
                S.wait(act, "ffn_zero", turn=layer)
                conv_up_act(act, layer)
                evac_mix_act(act, f"down{layer}")
                mix_was_read(act, f"down{layer}")
                norm_act(act, 3 + 4 * layer, mix[:, :, :], 8, T)
                S.wait(act, "norm_dve", "done", 3 + 4 * layer)
            mem_act(act)
            norm_act(act, 9, h2, 8, SEQ)
            up_act(act, "up2")
            phase_read(act, "down2")
            norm_act(act, 10, h2, 8, SEQ)
            in_act(act)
            sg_act(act)
            norm_act(act, 11, cqT[:, 0:3, :], 3, SEQ)
            norm_act(act, 12, ckvT, 2, SEQ)
            rope_act(act)
            mla_in_act(act)
            rown_act(act, 3, [], SEQ, 16)
            attention(act, "act", "mla")
            memq_act(act)
            attention(act, "act", "mem")
            phase_read(act, "mix_out")
            norm_act(act, 13, h2, 8, SEQ)
            up_act(act, "up3")

        @block.vector
        def _(dve):
            for i in range(BANKS):
                dve.memset(rs[:, 0, 4 * i:4 * i + 4], 0.0).then_inc(bank_free[i], 1)
            dve.memset(raw_c[:, :, 0:3], 0.0).then_inc(S.sem("qkv_dve"), CONV_AHEAD * 4)
            dve.memset(rs[:, 0, 16:20], 0.0).then_inc(S.sem("qkv_act"), CONV_AHEAD)
            dve.memset(rs[:, 0, 20:24], 0.0).then_inc(S.sem("up_dve"), 2 * 6)
            dve.memset(rs[:, 0, 24:28], 0.0).then_inc(S.sem("up_act"), 2)
            dve.memset(rs[:, 0, 28:32], 0.0).then_inc(S.sem("up_pool"), 2)
            dve.memset(rs[:, 1, :], 0.0).then_inc(S.sem("group_done"), 1)
            for i in range(BANKS):
                dve.wait_ge(bank_free[i], 1)
            dve.wait_ge(S.sem("up_pool"), 2)
            dve.wait_ge(S.sem("group_done"), 1)
            dve.wait_ge(S.sem("qkv_act"), CONV_AHEAD)
            dve.wait_ge(S.sem("up_act"), 2)
            dve.wait_ge(S.sem("up_dve"), 12)
            dve.wait_ge(S.sem("small_in"), 32)
            dve.wait_ge(S.sem("x_in"), 32)
            norm_dve(dve, 0, D, T, H1, gain("norm_w", 0), A1, 8)
            rows_dve(dve)
            qkv_dve(dve)
            cols_dve(dve)
            rown_dve(dve, 0, 1.0, EPS, T, 16, cn("l2_scale")[0:16, :])
            S.wait(dve, "cols_dve")
            scan_dve(dve)
            rown_dve(dve, 1, 1.0 / P, EPS, T, 16, 1.0)
            gate_dve(dve)
            for layer in range(2):
                if layer:
                    norm_dve(dve, 4, D, T, H1, gain("norm_w", 4 * DB), A1, 8)
                    ml_rows_dve(dve)
                    ml_cols_dve(dve)
                    ml_dve(dve)
                    rown_dve(dve, 2, 1.0 / 256, EPS, T, ML_H, 1.0)
                    ml_norm_dve(dve)
                mix_was_read(dve, "gdn_out" if layer == 0 else "ml_out")
                norm_dve(dve, 1 + 4 * layer, D, T, M1, gain("norm_w", (4 * layer + 1) * DB), M1, 8, add=(hs[:, :, :], mix[:, :, :]))
                S.wait(dve, "norm_dve", "done", 1 + 4 * layer)
                S.begin("ffn_zero")
                for i in range(2):
                    S.inc(dve.memset(raw[i][:, :, 0:2], 0.0), "ffn_zero")
                norm_dve(dve, 2 + 4 * layer, D, T, H1, gain("norm_w", (4 * layer + 2) * DB), A1, 8)
                S.wait(dve, "ffn_zero", turn=layer)
                conv_up_dve(dve, layer)
                mix_was_read(dve, f"down{layer}")
                norm_dve(dve, 3 + 4 * layer, D, T, M1, gain("norm_w", (4 * layer + 3) * DB), M1, 8, add=(hs[:, :, :], mix[:, :, :]))
                S.wait(dve, "norm_dve", "done", 3 + 4 * layer)
            dve.wait_ge(S.sem("mem_in"), 16)
            norm_dve(dve, 8, D, SEQ, lambda k: mem_sb[:, k, :], gain("mem_norm"), lambda k: memn[:, k, :], 8)
            norm_dve(dve, 9, D, SEQ, H2, gain("ffn1_norm"), A2, 8)
            up_dve(dve, "up2")
            down_dve(dve, "down2")
            phase_read(dve, "down2")
            norm_dve(dve, 10, D, SEQ, H2, gain("mix_norm"), A2, 8)
            phase_read(dve, "in_uv")
            sg_dve(dve)
            phase_read(dve, "in_ckv")
            norm_dve(dve, 11, 384, SEQ, lambda k: cqT[:, k, :], gain("cq_norm"), lambda k: cqn[:, k, :], 3)
            norm_dve(dve, 12, 256, SEQ, lambda k: ckvT[:, k, :], gain("ckv_norm"), lambda k: ckvn[:, k, :], 2)
            phase_read(dve, "in_gates")
            rope_dve(dve)
            mla_in_dve(dve)
            rown_dve(dve, 3, 1.0 / QK, EPS, SEQ, 16, 1.0)
            mla_rope_dve(dve)
            attention(dve, "dve", "mla")
            rown_dve(dve, 4, 1.0 / P, EPS, SEQ, 8, 1.0)
            memq_dve(dve)
            attention(dve, "dve", "mem")
            branches_dve(dve)
            mix_out_dve(dve)
            phase_read(dve, "mix_out")
            norm_dve(dve, 13, D, SEQ, H2, gain("ffn2_norm"), A2, 8)
            up_dve(dve, "up3")
            down_dve(dve, "down3")

        @block.tensor
        def _(pe):
            from_a = lambda m, k: a[:, k, :]
            from_a2 = lambda m, k: a[:, k, 0:SEQ]
            norm_pe(pe, 0, 8, T)
            S.wait(pe, "norm_dve", "done", 0)
            stream_pe(pe, "gdn_ba", from_a, T)
            stream_pe(pe, "gdn_qkv", from_a, T)
            rows_pe(pe)
            rown_pe(pe, 0, lambda k: sqh[:, k, :], 16, 1, T, 16)
            scan_pe(pe)
            S.wait(pe, "scan_act", "last", 3)
            rown_pe(pe, 1, lambda k: osq[:, k, :], 16, 1, T, 16)
            stream_pe(pe, "gdn_z", from_a, T)
            S.wait(pe, "gate_dve", turn=15)
            stream_pe(pe, "gdn_out", lambda m, k: qkv[:, 16 + k, :], T)
            for layer in range(2):
                if layer:
                    norm_pe(pe, 4, 8, T)
                    S.wait(pe, "norm_dve", "done", 4)
                    stream_pe(pe, "ml_gates", from_a, T)
                    stream_pe(pe, "ml_in", from_a, T)
                    ml_rows_pe(pe)
                    S.wait(pe, "mcol_dve")
                    ml_pe(pe)
                    rown_pe(pe, 2, lambda k: hsq[:, k, :], 8, 2, T, ML_H)
                    S.wait(pe, "mln_dve")
                    stream_pe(pe, "ml_out", lambda m, k: hT[:, k, :], T)
                norm_pe(pe, 1 + 4 * layer, 8, T)
                norm_pe(pe, 2 + 4 * layer, 8, T)
                S.wait(pe, "norm_dve", "done", 2 + 4 * layer)
                stream_pe(pe, f"up{layer}", from_a, T)
                S.wait(pe, "up_pool", turn=22 * layer + 21 + 2)
                stream_pe(pe, f"down{layer}", lambda m, k: hidden[:, k, :], T)
                norm_pe(pe, 3 + 4 * layer, 8, T)
            mem_pe(pe)
            norm_pe(pe, 9, 8, SEQ)
            S.wait(pe, "norm_dve", "done", 9)
            stream_pe(pe, "up2", from_a2, SEQ)
            phase_read(pe, "up2")
            stream_pe(pe, "down2", lambda m, k: hid2[:, k, :], SEQ)
            norm_pe(pe, 10, 8, SEQ)
            S.wait(pe, "norm_dve", "done", 10)
            for name in ("in_uv", "in_cq_kr", "in_qm", "in_ckv", "in_gates"):
                stream_pe(pe, name, from_a2, SEQ)
            phase_read(pe, "in_uv")
            sg_pe(pe)
            S.wait(pe, "sg_dve", "y3")
            norm_pe(pe, 11, 3, SEQ)
            norm_pe(pe, 12, 2, SEQ)
            S.wait(pe, "norm_dve", "done", 11)
            mla_in_pe(pe)
            S.wait(pe, "mla_dve", "heads")
            phase_read(pe, "mla_kv")
            attention(pe, "pe", "mla")
            rown_pe(pe, 4, lambda k: sq_k[:, k, :], 8, 1, SEQ, 8)
            S.wait(pe, "memq_dve")
            attention(pe, "pe", "mem")
            S.wait(pe, "mlaatt_act", "o7")
            S.wait(pe, "mematt_act", "o3")
            stream_pe(pe, "branches", lambda m, k: yT[m % 3][:, k, :], SEQ)
            S.wait(pe, "merge_dve")
            stream_pe(pe, "mix_out", lambda m, k: merged[:, k, :], SEQ)
            norm_pe(pe, 13, 8, SEQ)
            S.wait(pe, "norm_dve", "done", 13)
            stream_pe(pe, "up3", from_a2, SEQ)
            phase_read(pe, "up3")
            stream_pe(pe, "down3", lambda m, k: hid2[:, k, :], SEQ)

    return S.seen


def stream_layout(w):
    parts = []

    def cat(columns_, kb, per_slab):
        blocks = np.stack([c.reshape(kb, P, P) for c in columns_])
        m = blocks.shape[0]
        blocks = blocks.reshape(m // per_slab, per_slab * kb, P, P).transpose(0, 2, 1, 3)
        parts.append(np.ascontiguousarray(blocks).reshape(-1))

    def split(x):
        return [x[:, i:i + P] for i in range(0, x.shape[1], P)]

    def pad(x, places):
        out = np.zeros((x.shape[0], P), x.dtype)
        for at, src in places:
            out[:, at:at + src.shape[1]] = src
        return out

    def ffn(up, down):
        g, u = split(up[:, :FF]), split(up[:, FF:])
        cat([b for pair in zip(g, u) for b in pair], DB, 4)
        cat(split(down), FB, 1)

    gi = w["gdn_w_in"][0]
    qkv = 2 * HQ * P + HV * P
    cat([pad(gi, [(0, gi[:, qkv + HV * P:qkv + HV * P + HV]), (32, gi[:, qkv + HV * P + HV:])])], DB, 1)
    cat(split(gi[:, :qkv]), DB, 4)
    cat(split(gi[:, qkv:qkv + HV * P]), DB, 4)
    cat(split(w["gdn_w_out"][0]), HV, 2)
    ffn(w["ffn_w_up"][0], w["ffn_w_down"][0])
    mi = w["ml_w_in"][0]
    o4 = 2 * ML_H * P + 2 * ML_H * 256
    cat([pad(mi, [(0, mi[:, o4:o4 + ML_H]), (32, mi[:, o4 + ML_H:])])], DB, 1)
    cat(split(mi[:, :o4]), DB, 4)
    cat(split(w["ml_w_out"][0]), DB, 4)
    ffn(w["ffn_w_up"][1], w["ffn_w_down"][1])
    mk = w["mem_w_kv_2"][0]
    cat(split(mk[:, :512]), DB, 4)
    parts.append(np.ascontiguousarray(mk[:, 512:].reshape(DB, P, 512).transpose(1, 0, 2)).reshape(-1))
    ffn(w["ffn1_w_gu_2"][0], w["ffn1_w_down_2"][0])
    wi = w["w_in_2"][0]
    cat(split(wi[:, 0:1024]), DB, 4)
    cat(split(wi[:, 1024:1408]) + [pad(wi, [(NOPE, wi[:, 1664:1696])])], DB, 4)
    cat(split(wi[:, 1696:2208]), DB, 4)
    cat(split(wi[:, 1408:1664]), DB, 2)
    cat(split(wi[:, 2208:]), DB, 4)
    uq, ukv = w["mla_w_uq_2"][0], w["mla_w_ukv_2"][0]
    cat([pad(uq, [(0, uq[:, QK * h:QK * (h + 1)])]) for h in range(MLA_H)], 3, 8)
    kpart = np.stack([pad(ukv, [(0, ukv[:, P * h:P * h + NOPE])]).reshape(2, P, P) for h in range(MLA_H)])
    kpart = kpart.reshape(16, P, P).transpose(1, 0, 2).reshape(P, 16 * P)
    vpart = ukv.reshape(2, P, MLA_H, 2, NOPE)[:, :, :, 1, :].reshape(2, P, 512).transpose(1, 0, 2).reshape(P, 1024)
    parts.append(np.concatenate([kpart, vpart], 1).reshape(-1))
    br = [split(w[n][0]) for n in ("w_branch_a_2", "w_branch_b_2", "w_branch_c_2")]
    cat([b[c] for c in range(DB) for b in br], 4, 6)
    cat(split(w["w_out_2"][0]), DB, 4)
    ffn(w["ffn2_w_gu_2"][0], w["ffn2_w_down_2"][0])
    out = np.concatenate(parts)
    assert out.size == STREAM_WORDS, (out.size, STREAM_WORDS)
    return out


def const_layout():
    c = np.zeros((P, N_CONST), np.float32)
    i = np.arange(P)

    def put(name, v):
        at, n = CONST_COLS[name]
        c[:v.shape[0], at:at + n] = v

    put("ident", np.eye(P))
    put("ones", np.ones((P, P)))
    put("causal", np.where(np.arange(T)[None] >= i[:, None], 0.0, NEG))
    levels = []
    for l in range(7):
        s = 1 << l
        levels.append(((i[None] // s) % 2 == 1) & (i[None] // s == i[:, None] // s + 1))
    put("level", np.stack(levels, 1).reshape(P, 7 * P))
    rot = np.zeros((QK, QK))
    for r in range(ROPE // 2):
        rot[NOPE + ROPE // 2 + r, NOPE + r] = -1.0
        rot[NOPE + r, NOPE + ROPE // 2 + r] = 1.0
    put("rot", rot)
    half = ROPE // 2
    inv = (np.float32(10000.0) ** (-np.arange(half, dtype=np.float32) / np.float32(half))).astype(np.float32)
    f = np.zeros((QK, 1))
    f[NOPE:NOPE + half, 0] = inv
    f[NOPE + half:, 0] = inv
    put("inv_freq", f)
    row_of = np.zeros((P, 31))
    row_of[:, 15] = 1.0
    put("row_of", row_of)
    tri = np.where(i[None] <= i[:, None], 0.0, NEG)
    put("score_mask", np.concatenate([tri, np.zeros((P, P)), tri], 1))
    put("tri", (i[None] >= i[:, None]) * 1.0)
    l2 = np.ones((P, 1))
    l2[:HQ] = P ** -0.5
    put("l2_scale", l2)
    return c


def param_layout(w):
    p = np.zeros((P, N_PARAM), np.float32)

    def put(name, v):
        at, n = PARAM_COLS[name]
        assert v.shape[1] == n, (name, v.shape, n)
        p[:v.shape[0], at:at + n] = v

    def cols_of(v):
        return v.reshape(-1, P).T

    put("norm_w", cols_of(w["norm_w"].reshape(-1)))
    put("gdn_conv", w["gdn_conv_w"][0].reshape(4, 32, P).transpose(2, 1, 0).reshape(P, -1))
    put("ffn_conv", w["ffn_conv_w"].reshape(2, 3, 2, FB, P).transpose(4, 0, 3, 2, 1).reshape(P, -1))
    put("ffn_bias", w["ffn_conv_b"].reshape(2, 2, FB, P).transpose(3, 0, 2, 1).reshape(P, -1))
    put("gdn_norm", w["gdn_norm_w"][0][:, None])
    put("a_log", w["gdn_a_log"][0][:, None])
    put("dt_bias", w["gdn_dt_bias"][0][:, None])
    put("ml_gate_i", w["ml_gate_b"][0][:ML_H, None])
    put("ml_gate_f", w["ml_gate_b"][0][ML_H:, None])
    put("ml_norm", cols_of(w["ml_norm_w"][0]))
    for name, src in (("ffn1_norm", "ffn1_norm_2"), ("mix_norm", "mix_norm_2"), ("ffn2_norm", "ffn2_norm_2"), ("mem_norm", "mem_norm_2"),
                      ("b_gate", "b_gate_2"), ("sg_g", "sg_ln_g_2"), ("sg_b", "sg_ln_b_2"), ("cq_norm", "mla_cq_norm_2"),
                      ("ckv_norm", "mla_ckv_norm_2"), ("mq_norm", "mem_q_norm_2"), ("mk_norm", "mem_k_norm_2")):
        put(name, cols_of(w[src][0]))
    put("q_norm", w["mla_q_norm_2"][0][:, None])
    put("k_norm", w["mla_k_norm_2"][0][:, None])
    return p


def layout(inputs):
    w = {k: np.asarray(v) for k, v in inputs.items()}
    return {
        "x_t": np.ascontiguousarray(w["x"][0].T),
        "meta_t": np.ascontiguousarray(w["meta_tokens"].T),
        "mem_t": np.ascontiguousarray(w["mem_2"][0].T),
        "positions": np.ascontiguousarray(w["positions_2"]),
        "stream": stream_layout(w),
        "consts": const_layout(),
        "params": param_layout(w),
        "sg_w_t": np.ascontiguousarray(w["sg_w_2"][0].transpose(2, 0, 1)),
        "sg_bias": np.ascontiguousarray(w["sg_b_2"][0]),
    }


def kernel(**inputs):
    import concourse.bacc as bacc
    from concourse.bass_utils import run_bass_kernel_spmd

    arrays = layout(inputs)
    counts = {}
    for _ in range(2):
        nc = bacc.Bacc("TRN2", target_bir_lowering=False, num_devices=1)
        aps = {n: nc.dram_tensor(f"in_{n}", v.shape, mybir.dt.from_np(v.dtype), kind="ExternalInput").ap() for n, v in arrays.items()}
        out = nc.dram_tensor("out_t", (D, SEQ), F32, kind="ExternalOutput").ap()
        counts = program(nc, out_t=out, counts=counts, **aps)
    r = run_bass_kernel_spmd(nc, [{f"in_{n}": v for n, v in arrays.items()}], core_ids=[0])
    return np.ascontiguousarray(r.results[0]["out_t"].T)[None]
```

```python
from contextlib import ExitStack

import numpy as np

import concourse.bass as bass
from concourse import mybir

F32 = mybir.dt.float32
F32R = mybir.dt.float32r
I32 = mybir.dt.int32
ALU = mybir.AluOpType
ACT = mybir.ActivationFunctionType
AX_X = mybir.AxisListType.X

P = 128
D = 1024
DB = D // P
SEQ = 256
META = 16
T = META + SEQ
TILES = [(0, META), (META, P), (META + P, P)]
HQ, HV = 8, 16
FF = 2816
FB = FF // P
ML_H = 4
MLA_H, NOPE, ROPE, QK = 8, 64, 32, 96
MEM_H = 4
EPS = 1e-6
NEG = -1e30
TWO_PI_HI = 6.28125
TWO_PI_LO = float(np.float32(2 * np.pi - 6.28125))
ROUND = 12582912.0
PI_IN = 3.1415925

SLOTS = 4
SLOT = 2048
SPLIT_SLOTS = 2
WORK = 23100
BANKS = 4

PHASES = [
    ("gdn_ba", 1, 1, 1, 8, False), ("gdn_qkv", 16, 2, 1, 16, True), ("gdn_z", 8, 2, 1, 16, True), ("gdn_out", 8, 1, 1, 16, True),
    ("up0", 22, 2, 1, 16, True), ("down0", 16, 1, 2, 11, True),
    ("ml_gates", 1, 1, 1, 8, False), ("ml_in", 12, 2, 1, 16, True), ("ml_out", 4, 2, 1, 16, True),
    ("up1", 22, 2, 1, 16, True), ("down1", 16, 1, 2, 11, True),
    ("mem_k", 2, 2, 1, 16, False), ("mem_v", 2, 2, 1, 16, False),
    ("up2", 22, 2, 1, 16, True), ("down2", 16, 1, 2, 11, True),
    ("in_uv", 4, 2, 1, 16, True), ("in_cq_kr", 2, 2, 1, 16, True), ("in_qm", 2, 2, 1, 16, True), ("in_ckv", 1, 2, 1, 16, True),
    ("in_gates", 12, 2, 1, 16, True), ("mla_q", 2, 4, 1, 12, False), ("mla_k", 1, 8, 1, 16, False), ("mla_v", 1, 2, 1, 8, False),
    ("branches", 8, 3, 1, 12, False), ("mix_out", 4, 2, 1, 16, False),
    ("up3", 22, 2, 1, 16, True), ("down3", 16, 1, 2, 11, True),
]


class Phase:
    def __init__(self, name, slabs, parts, per_product, blocks, split):
        self.name, self.slabs, self.parts, self.per_product, self.blocks, self.split = name, slabs, parts, per_product, blocks, split
        self.products = slabs * parts // per_product
        self.turn = SLOTS * per_product if parts < BANKS and per_product > 1 else SLOTS


def plan():
    out, slab, product, part, word = {}, 0, 0, 0, 0
    for args in PHASES:
        ph = Phase(*args)
        ph.slab0, ph.product0, ph.part0, ph.word0 = slab, product, part, word
        slab += ph.slabs
        product += ph.products
        part += ph.slabs * ph.parts
        word += ph.slabs * ph.blocks * P * P
        ph.end = product
        out[ph.name] = ph
    return out, slab, word


PLAN, SLABS, STREAM_WORDS = plan()
SLAB_OF = [ph for ph in PLAN.values() for _ in range(ph.slabs)]
SPLITS = [n for n in range(SLABS) if SLAB_OF[n].split]
SPLIT_AT = {n: i for i, n in enumerate(SPLITS)}


def done_value(n):
    ph = SLAB_OF[n]
    return ph.part0 + (n - ph.slab0 + 1) * ph.parts


CONST_COLS, PARAM_COLS = {}, {}


def columns(table, sizes):
    at = 0
    for name, n in sizes:
        table[name] = (at, n)
        at += n
    return at


N_CONST = columns(CONST_COLS, [
    ("ident", P), ("ones", P), ("causal", T), ("level", 7 * P), ("rot", QK), ("inv_freq", 1),
    ("row_of", 31), ("score_mask", 3 * P), ("tri", P),
    ("l2_scale", 1)])
N_PARAM = columns(PARAM_COLS, [
    ("norm_w", 8 * DB), ("gdn_conv", 32 * 4), ("ffn_conv", 2 * 2 * FB * 3), ("ffn_bias", 2 * 2 * FB),
    ("gdn_norm", 1), ("a_log", 1), ("dt_bias", 1), ("ml_gate_i", 1), ("ml_gate_f", 1), ("ml_norm", 8),
    ("ffn1_norm", DB), ("mix_norm", DB), ("ffn2_norm", DB), ("mem_norm", DB), ("b_gate", 24),
    ("sg_g", 4), ("sg_b", 4), ("cq_norm", 3), ("ckv_norm", 2), ("q_norm", 1), ("k_norm", 1),
    ("mq_norm", 1), ("mk_norm", 1)])


class Steps:

    def __init__(self, make_sem, counts):
        self.make_sem, self.counts, self.sems = make_sem, counts, {}
        self.pos, self.seen = {}, {}

    def sem(self, name):
        if name not in self.sems:
            self.sems[name] = self.make_sem(name)
        return self.sems[name]

    def begin(self, name):
        self.pos[name] = 0

    def inc(self, ins, name, step=None):
        self.pos[name] = self.pos.get(name, 0) + 1
        if step is not None:
            key = (name, step)
            assert self.seen.get(key, self.pos[name]) == self.pos[name], key
            self.seen[key] = self.pos[name]
        self.seen[name] = max(self.seen.get(name, 0), self.pos[name])
        return ins.then_inc(self.sem(name), 1)

    def value(self, name, step, turn=0):
        per = self.counts.get(name, 1)
        at = per if step == "last" else self.counts.get((name, step), 1)
        if self.counts and step != "last" and (name, step) not in self.counts:
            raise KeyError((name, step))
        return at if isinstance(turn, int) and turn == 0 else turn * per + at

    def at(self, name, step="last", turn=0):
        return self.sem(name), self.value(name, step, turn)

    def own(self, eng, name, turn=0):
        n = self.pos.get(name, 0)
        if n > 0:
            eng.wait_ge(self.sem(name), n if isinstance(turn, int) and turn == 0 else turn * self.counts.get(name, 1) + n)


def program(nc, x_t, meta_t, mem_t, positions, stream, consts, params, sg_w_t, sg_bias, out_t, counts):
    with ExitStack() as ctx:
        sem_list = []

        def make_sem(name):
            s = ctx.enter_context(nc.semaphore(name))
            sem_list.append(s)
            return s

        S = Steps(make_sem, counts)

        def sb(name, shape, dt=F32):
            return ctx.enter_context(nc.sbuf_tensor(name, shape, dt))

        ring = sb("ring", [P, SLOTS, SLOT])
        with nc.sbuf_tensor("w_spare", [P, 2 * SPLIT_SLOTS * SLOT], F32) as t:
            spare = t
        w_hi = sb("w_hi", [P, SPLIT_SLOTS, SLOT], F32R)
        w_lo = sb("w_lo", [P, SPLIT_SLOTS, SLOT], F32R)
        Cn = sb("consts_sb", [P, N_CONST])
        Pm = sb("params_sb", [P, N_PARAM])
        hs = sb("hs", [P, DB, T])
        a = sb("a", [P, DB, T])
        mix = sb("mix", [P, DB, T])
        sq = sb("sq", [P, DB, T])
        rs = sb("rs", [P, 2, T])
        with nc.sbuf_tensor("work_r", [P, WORK], F32R) as t:
            work_r = t
        work = sb("work", [P, WORK])
        ps = [ctx.enter_context(nc.psum_tensor(f"bank{i}", [P, 512], F32))[:, :] for i in range(8)]

        def cn(name, lo=0, n=None):
            at, size = CONST_COLS[name]
            return Cn[:, at + lo:at + lo + (size if n is None else n)]

        def pm(name, col=0):
            at, _ = PARAM_COLS[name]
            return Pm[:, at + col:at + col + 1]

        def area(at, *shape, of=None):
            n = int(np.prod(shape))
            v = (work if of is None else of)[:, at:at + n]
            if len(shape) == 2:
                v = v.rearrange("p (a b) -> p a b", b=shape[1])
            if len(shape) == 3:
                v = v.rearrange("p (a b c) -> p a b c", b=shape[1], c=shape[2])
            return v

        ident, ones = cn("ident"), cn("ones")
        weights_in = [S.sem(f"weights_in{i}") for i in range(SLOTS)]
        product_done = S.sem("product_done")
        bank_free = [S.sem(f"bank_free{i}") for i in range(BANKS)]
        small_in = S.sem("small_in")
        x_in = S.sem("x_in")

        class Unit:

            def __init__(self, ph, size, j, i, per_turn):
                self.j, self.ph = j, ph
                self.u = j if per_turn == 0 else i * per_turn + j
                self.at = j * size
                self.more = 0 if per_turn == 0 else i * (per_turn * size * ph.per_product)
                self.more4 = 0 if per_turn == 0 else i * (per_turn * size // BANKS)

            def ready(self, eng, m=0):
                eng.wait_ge(product_done, self.more + (self.ph.part0 + (self.at + m + 1) * self.ph.per_product))

            def bank(self, m=0):
                return ps[(self.ph.product0 + self.at + m) % BANKS]

            def free(self, ins, m=0):
                return ins.then_inc(bank_free[(self.ph.product0 + self.at + m) % BANKS], 1)

            def was_read(self, eng, m=0, before=0):
                b = self.ph.product0 + self.at + m - before
                eng.wait_ge(bank_free[b % BANKS], self.more4 + (b // BANKS + 2))

        hi_done, lo_done = S.sem("hi_done"), S.sem("lo_done")
        prepared = {"hi": 0, "lo": 0}

        def split_slab(eng, which, s, ph=None, i=None):
            n = SPLITS[s]
            size = SLAB_OF[n].blocks * P
            slot, raw_w = s % SPLIT_SLOTS, ring[:, n % SLOTS, 0:SLAB_OF[n].blocks * P]
            at = lambda per_turn, v: v if i is None else i * per_turn + v
            if which == "hi":
                eng.wait_ge(weights_in[n % SLOTS], at(16, 16 * (n // SLOTS + 1)))
                if s >= SPLIT_SLOTS:
                    eng.wait_ge(product_done, at(SLOTS * ph.parts if ph else 0, done_value(SPLITS[s - SPLIT_SLOTS])))
                eng.activation(w_hi[:, slot, 0:size], raw_w, ACT.Copy).then_inc(hi_done, 1)
            else:
                eng.wait_ge(hi_done, at(SLOTS, s + 1))
                eng.tensor_tensor(w_lo[:, slot, 0:size], raw_w, w_hi[:, slot, 0:size].bitcast(F32), ALU.subtract).then_inc(lo_done, 1)

        def prepare(eng, which, name):
            first = SPLIT_AT[PLAN[name].slab0]
            while prepared[which] < first + SPLIT_SLOTS:
                split_slab(eng, which, prepared[which])
                prepared[which] += 1

        def each_product(eng, name, size, body, table=None, turns=None, split=None, late=None, lag=0):
            ph = PLAN[name]
            per_turn = SLOTS * ph.parts // ph.per_product // size
            total = ph.products // size
            head = lag * size // ph.parts
            most = (ph.slabs - head) // SLOTS if (per_turn * size) % BANKS == 0 else 0
            if split:
                assert prepared[split] == SPLIT_AT[ph.slab0] + SPLIT_SLOTS, name

                def may(j):
                    s = SPLIT_AT[ph.slab0 + j] + SPLIT_SLOTS
                    return s < len(SPLITS) and (name != "gdn_qkv" or j + SPLIT_SLOTS < ph.slabs) and SPLITS[s] == ph.slab0 + j + SPLIT_SLOTS and SLAB_OF[SPLITS[s]].blocks == ph.blocks
                while most and not all(may(j) for j in range(head, head + most * SLOTS)):
                    most -= 1
            turns = most if turns is None else min(turns, most)

            def ahead(j, i):
                n = ph.slab0 + j
                s = SPLIT_AT[n] + SPLIT_SLOTS
                if s < len(SPLITS) and SPLITS[s] - SLOTS <= n and not (name == "gdn_qkv" and s > SPLIT_AT[ph.slab0] + ph.slabs - 1):
                    split_slab(eng, split, s, ph, i)
                    if i is None:
                        assert prepared[split] == s
                        prepared[split] += 1

            def unit(j, i, per_turn_):
                if split:
                    lo, hi = j * size * ph.per_product, (j + 1) * size * ph.per_product
                    for slab in range(lo // ph.parts, hi // ph.parts):
                        ahead(slab, None if per_turn_ == 0 else i)
                body(Unit(ph, size, j, i, per_turn_))
                if late is not None and j >= lag:
                    late(Unit(ph, size, j - lag, i, per_turn_))

            for j in range(lag):
                unit(j, 0, 0)
            done = lag
            if turns >= 2:
                if table is not None:
                    eng.preload_act_table(table)
                with eng.Fori(0, turns) as i:
                    for j in range(lag, lag + per_turn):
                        unit(j, i, per_turn)
                done += turns * per_turn
                if split:
                    prepared[split] += turns * SLOTS
            for j in range(done, total):
                unit(j, 0, 0)
            for j in range(total - lag, total):
                late(Unit(ph, size, j, 0, 0))

        def nothing(unit):
            pass

        def stream_pe(pe, name, x, n):
            ph = PLAN[name]
            kb = ph.blocks // ph.parts

            def slab(j, i, looped):
                nslab = ph.slab0 + j
                if ph.split:
                    done = SPLIT_AT[nslab] + 1
                    slot = (done - 1) % SPLIT_SLOTS
                    pe.wait_ge(lo_done, i * ph.turn + done if looped else done)
                else:
                    arrived = 16 * (nslab // SLOTS + 1)
                    pe.wait_ge(weights_in[nslab % SLOTS], i * (4 * ph.turn) + arrived if looped else arrived)
                for m in range(ph.parts):
                    part = j * ph.parts + m
                    b = ph.product0 + part // ph.per_product
                    free = b // BANKS + 1
                    begins, ends = part % ph.per_product == 0, part % ph.per_product == ph.per_product - 1
                    if begins:
                        pe.wait_ge(bank_free[b % BANKS], i * (ph.turn * ph.parts // ph.per_product // BANKS) + free if looped else free)
                    out = ps[b % BANKS][:, 0:n]
                    for k in range(kb):
                        at = (m * kb + k) * P
                        first, last = begins and k == 0, ends and k == kb - 1
                        kx = part % ph.per_product * kb + k
                        if ph.split:
                            hi, lo = x(m, kx)
                            pe.matmul(out, w_hi[:, slot, at:at + P], hi, start=first, stop=False)
                            pe.matmul(out, w_hi[:, slot, at:at + P], lo, start=False, stop=False)
                            mm = pe.matmul(out, w_lo[:, slot, at:at + P], hi, start=False, stop=last)
                        else:
                            mm = pe.matmul(out, ring[:, nslab % SLOTS, at:at + P], x(m, kx), start=first, stop=last)
                    mm.then_inc(product_done, 1)

            turns, done = ph.slabs // ph.turn, 0
            if turns >= 2:
                with pe.Fori(0, turns) as i:
                    for j in range(ph.turn):
                        slab(j, i, True)
                done = turns * ph.turn
            for j in range(done, ph.slabs):
                slab(j, 0, False)

        A_HI, A_LO = (area(at, DB, T, of=work_r) for at in (WORK - 2 * DB * T, WORK - DB * T))

        def split_act(act, use, src, hi, blocks, n, norm=None):
            S.begin("x_hi")
            for half in range(2):
                if norm is not None:
                    act.wait_ge(*S.at("norm_dve", "done" if half else "scaled", norm))
                k = slice(half * blocks // 2, (half + 1) * blocks // 2)
                S.inc(act.activation(hi[:, k, 0:n], src[:, k, 0:n], ACT.Copy), "x_hi", half)

        def split_dve(dve, use, src, hi, lo, blocks, n):
            S.begin("x_lo")
            for half in range(2):
                k = slice(half * blocks // 2, (half + 1) * blocks // 2)
                dve.wait_ge(*S.at("x_hi", half, use))
                S.inc(dve.tensor_tensor(lo[:, k, 0:n], src[:, k, 0:n], hi[:, k, 0:n].bitcast(F32), ALU.subtract), "x_lo")

        STAT = ps[4]

        def norm_act(act, use, src, blocks, n):
            S.begin("norm_act")
            S.inc(act.activation(sq[:, 0:blocks, 0:n], src, ACT.Square), "norm_act", "squares")
            act.wait_ge(*S.at("norm_dve", "mean", use))
            S.inc(act.activation(rs[:, 1, 0:n], rs[:, 0, 0:n], ACT.Sqrt), "norm_act", "root")

        def norm_pe(pe, use, blocks, n):
            S.begin("norm_pe")
            pe.wait_ge(*S.at("norm_act", "squares", use))
            for k in range(blocks):
                mm = pe.matmul(STAT[:, 0:n], ones, sq[:, k, 0:n], start=(k == 0), stop=(k == blocks - 1))
            S.inc(mm, "norm_pe", "sums")

        def norm_dve(dve, use, width, n, src, gain, dst, blocks, add=None):
            S.begin("norm_dve")
            if use:
                dve.wait_ge(*S.at("norm_dve", "done", use - 1))
            dve.wait_ge(*S.at("norm_pe", "sums", use))
            S.inc(dve.tensor_scalar(rs[:, 0, 0:n], STAT[:, 0:n], 1.0 / width, EPS, ALU.mult, ALU.add), "norm_dve", "mean")
            dve.wait_ge(*S.at("norm_act", "root", use))
            S.inc(dve.reciprocal(rs[:, 0, 0:n], rs[:, 1, 0:n]), "norm_dve", "rstd")
            dve.wait_ge(*S.at("norm_dve", "rstd", use))
            for k in range(blocks):
                ins = dve.scalar_tensor_tensor(out=dst(k), in0=src(k), scalar=gain(k), in1=rs[:, 0, 0:n],
                                               op0=ALU.mult, op1=ALU.mult)
                if add is None and k == blocks // 2 - 1 or add is not None and k == blocks - 1:
                    S.inc(ins, "norm_dve", "scaled")
            if add is not None:
                dve.wait_ge(*S.at("norm_dve", "scaled", use))
                ins = dve.tensor_tensor(add[0], add[0], add[1], ALU.add)
            S.inc(ins, "norm_dve", "done")

        rrow = sb("rrow", [HV, 2, T])

        def rown_act(act, use, squares, n, rows):
            S.begin("rown_act")
            for src, dst in squares:
                act.activation(dst, src, ACT.Square).then_inc(S.sem("rown_squares"), 1)
            act.wait_ge(*S.at("rown_dve", "mean", use))
            S.inc(act.activation(rrow[0:rows, 1, 0:n], rrow[0:rows, 0, 0:n], ACT.Sqrt), "rown_act", "root")

        def rown_pe(pe, use, sqr, blocks, per_row, n, rows):
            S.begin("rown_pe")
            if use == 3:
                pe.wait_ge(*S.at("mla_act", "ksq"))
            else:
                pe.wait_ge(S.sem("rown_squares"), (1, 2, 3, 3, 5)[use])
            for k in range(blocks):
                src = sqr(k)
                h = k // per_row
                mm = pe.matmul(ps[4][0:rows, 0:n], cn("row_of", 15 - h, rows)[0:src.shape[0], :], src,
                               start=(k == 0), stop=(k == blocks - 1))
            S.inc(mm, "rown_pe", "sums")

        def rown_dve(dve, use, scale, eps, n, rows, after):
            S.begin("rown_dve")
            dve.wait_ge(*S.at("rown_pe", "sums", use))
            S.inc(dve.tensor_scalar(rrow[0:rows, 0, 0:n], ps[4][0:rows, 0:n], scale, eps, ALU.mult, ALU.add), "rown_dve", "mean")
            dve.wait_ge(*S.at("rown_act", "root", use))
            S.inc(dve.reciprocal(rrow[0:rows, 0, 0:n], rrow[0:rows, 1, 0:n]), "rown_dve")
            S.own(dve, "rown_dve", use)
            S.inc(dve.tensor_scalar(rrow[0:rows, 0, 0:n], rrow[0:rows, 0, 0:n], after, None, ALU.mult), "rown_dve", "rows")

        qkv = area(0, 32, T)
        raw_c = area(8704, 4, T + 3)
        conv_y = area(8704 + 4 * (T + 3), 4, T)
        rows_at = 8704 + 8 * T + 12
        R_BETA, R_G, R_EG, R_EGL, R_NBEG, R_X, R_Y, R_A, R_Z = range(9)
        row = [work[0:HV, rows_at + i * T:rows_at + (i + 1) * T] for i in range(9)]
        sqh = area(rows_at + 9 * T, 16, T)
        colv = sb("colv", [P, 3, 3, HV])
        colb = sb("colb", [P, 3, HV])

        bc = area(8704, 16, T)
        qn = area(8704 + 4352, 2, T)
        kn = area(8704 + 4896, 2, T)
        qd = area(8704 + 5440, 4, T)
        vs = area(8704 + 6528, 4, T)
        St = area(8704 + 7616, 4, P)
        St2 = area(8704 + 8128, 4, P)
        par0 = 8704 + 8704
        mixw = mix[:, :, :].rearrange("p a b -> p (a b)")
        sqw = sq[:, :, :].rearrange("p a b -> p (a b)")
        names = ["vb", "nkbe", "ktl", "A0T", "attn", "X", "XT", "Am"]

        def tile4(v):
            return v.rearrange("p (a b) -> p a b", b=P)

        buf = {2: {n: area(par0 + 512 * i, 4, P) for i, n in enumerate(names)},
               1: {n: tile4(mixw[:, 512 * i:512 * (i + 1)]) if i < 4 else tile4(sqw[:, 512 * (i - 4):512 * (i - 3)])
                   for i, n in enumerate(names)}}
        St0 = area(0, HV, P, of=spare)
        bc0 = area(2048, 64, META, of=spare)
        for i, n in enumerate(("Y", "decb", "dec")):
            for c in (1, 2):
                buf[c][n] = area(3072 + 1024 * i + 512 * (c - 1), 4, P, of=spare)
        vb0, ktl0 = (area(par0 + 2048 * i, HV, P) for i in range(2))
        c0 = {n: mixw[0:META, 256 * i:256 * (i + 1)].rearrange("p (a b) -> p a b", b=META)
              for i, n in enumerate(("dec", "decb", "A0T", "attn", "X", "XT", "Am", "Y"))}
        kn0, qn0 = (spare[:, 6144 + 128 * i:6144 + 128 * (i + 1)].rearrange("p (a b) -> p a b", b=META) for i in range(2))
        obc = area(8704, HV, T)
        osq = area(8704 + 16 * T, HV, T)
        zs = area(8704 + 32 * T, 4, T)

        hid_hi, hid_lo = (area(i * FB * T, FB, T, of=work_r) for i in range(2))
        f_at = 2 * FB * T
        raw = [area(f_at + i * 2 * (T + 2), 2, T + 2) for i in range(2)]
        y_gu = [area(f_at + 4 * (T + 2) + i * 2 * T, 2, T) for i in range(2)]
        silu_g = [area(f_at + 4 * (T + 2) + (4 + i) * T, T) for i in range(2)]
        h_new = [area(f_at + 4 * (T + 2) + (6 + i) * T, T) for i in range(2)]

        mlT = area(0, 24, T)
        v_tok = area(6528, 3, 8, P)
        bc2 = area(9600, 2, ML_H, T)
        mrow = [work[0:ML_H, 11776 + i * T:11776 + (i + 1) * T] for i in range(9)]
        M_LI, M_Y, M_E, M_ONE, M_B, M_C, M_M, M_EM, M_T = range(9)
        mcol = sb("mcol", [P, 3, ML_H])
        Wt = [[area(14300 + (3 * i + t) * T, T) for t in range(3)] for i in range(2)]
        Pt = [[area(14300 + (6 + 3 * i + t) * T, T) for t in range(3)] for i in range(2)]
        den = area(14300 + 12 * T, 2, T)
        hT = area(14300 + 14 * T, 8, T)
        mbc = area(9600, ML_H, T)
        hsq = area(0, 8, T)

        scratch = nc.dram_tensor("rows_scratch", (64, T), F32, kind="Internal").ap()
        scr_o = nc.dram_tensor("rows_scratch_o", (HV, T), F32, kind="Internal").ap()
        scr_m = nc.dram_tensor("rows_scratch_m", (2 * ML_H, T), F32, kind="Internal").ap()
        scr_h = nc.dram_tensor("rows_scratch_h", (ML_H, T), F32, kind="Internal").ap()
        scr_q = nc.dram_tensor("rows_scratch_q", (16, SEQ), F32, kind="Internal").ap()
        scr_c = nc.dram_tensor("rows_scratch_c", (8, SEQ), F32, kind="Internal").ap()

        def on_all(ap_tensor, offset, *dims):
            return bass.AP(ap_tensor.tensor, offset, [[0, P], *[list(d) for d in dims]])

        PSA, PSB, PSC, PSD = ps[4], ps[5], ps[6], ps[7]

        def b4(v, c):
            return v.rearrange("p (a b) -> p a b", b=P)[:, :, 0:c]

        O_HI, O_LO = area(0, HV, T, of=work_r), area(8704 + 16 * T, HV, T, of=work_r)
        ML_HI, ML_LO = area(0, DB, T, of=work_r), area(DB * T, DB, T, of=work_r)

        BA = Unit(PLAN["gdn_ba"], 1, 0, 0, 0)

        def rows_act(act):
            BA.ready(act)
            S.inc(act.activation(row[R_BETA], BA.bank()[0:HV, 0:T], ACT.Sigmoid), "rows_act", "beta")
            act.wait_ge(*S.at("rows_dve", "x"))
            S.inc(act.activation(row[R_Y], row[R_X], ACT.Abs), "rows_act", "abs")
            S.own(act, "rows_act")
            S.inc(act.activation(row[R_Y], row[R_Y], ACT.Exp, scale=-1.0), "rows_act")
            S.inc(act.activation(row[R_A][:, 0:1], pm("a_log")[0:HV, :], ACT.Exp), "rows_act")
            S.own(act, "rows_act")
            S.inc(act.activation(row[R_Y], row[R_Y], ACT.Ln, bias=1.0), "rows_act", "ln")
            act.wait_ge(*S.at("rows_dve", "diff"))
            S.inc(act.activation(row[R_EG], row[R_G], ACT.Exp), "rows_act")
            S.inc(act.activation(row[R_EGL], row[R_EGL], ACT.Exp), "rows_act", "exps")

        def rows_dve(dve):
            BA.ready(dve)
            dve.wait_ge(*S.at("rows_act", "beta"))
            BA.free(dve.tensor_scalar(row[R_Z], BA.bank()[32:32 + HV, 0:T], pm("dt_bias")[0:HV, :], None, ALU.add))
            BA.was_read(dve)
            S.inc(dve.tensor_copy(row[R_X], row[R_Z]), "rows_dve", "x")
            dve.wait_ge(*S.at("rows_act", "ln"))
            S.inc(dve.scalar_tensor_tensor(out=row[R_Z], in0=row[R_X], scalar=0.0, in1=row[R_Y], op0=ALU.max, op1=ALU.add), "rows_dve")
            S.own(dve, "rows_dve")
            S.inc(dve.tensor_scalar(row[R_X], row[R_Z], row[R_A][:, 0:1], -1.0, ALU.mult, ALU.mult), "rows_dve")
            S.inc(dve.memset(row[R_Y], 1.0), "rows_dve")
            S.own(dve, "rows_dve")
            for t0, c in TILES:
                S.inc(dve.tensor_tensor_scan(row[R_G][:, t0:t0 + c], row[R_Y][:, t0:t0 + c], row[R_X][:, t0:t0 + c], 0.0,
                                             ALU.mult, ALU.add), "rows_dve")
            S.own(dve, "rows_dve")
            for t0, c in TILES:
                S.inc(dve.tensor_scalar(row[R_EGL][:, t0:t0 + c], row[R_G][:, t0:t0 + c], row[R_G][:, t0 + c - 1:t0 + c], -1.0,
                                        ALU.subtract, ALU.mult), "rows_dve", "diff" if t0 == TILES[-1][0] else None)
            dve.wait_ge(*S.at("rows_act", "exps"))
            S.inc(dve.scalar_tensor_tensor(out=row[R_NBEG], in0=row[R_BETA], scalar=-1.0, in1=row[R_EG], op0=ALU.mult, op1=ALU.mult),
                  "rows_dve", "rows")

        def rows_pe(pe):
            pe.wait_ge(*S.at("rows_dve", "rows"))
            for c, (t0, n) in enumerate(TILES):
                for q, r in enumerate((R_BETA, R_G, R_EGL, R_NBEG)):
                    mm = pe.transpose(PSB[0:n, (c * 4 + q) * HV:(c * 4 + q + 1) * HV], row[r][:, t0:t0 + n], ident[0:HV, 0:HV])
            S.inc(mm, "rows_pe")

        def cols_dve(dve):
            dve.wait_ge(*S.at("rows_pe"))
            for c, (t0, n) in enumerate(TILES):
                src = PSB[0:n, c * 64:c * 64 + 64].rearrange("p (a b) -> p a b", b=HV)
                S.inc(dve.tensor_copy(colv[0:n, c, :, :], src[:, 0:3, :]), "cols_dve")
                S.inc(dve.tensor_copy(colb[0:n, c, :], src[:, 3, :]), "cols_dve")

        CONV_AHEAD = 4
        at, n = PARAM_COLS["gdn_conv"]
        gdn_taps = Pm[:, at:at + n].rearrange("p (b t) -> p b t", t=4)

        def qkv_act(act):
            def project(un):
                act.wait_ge(*S.at("qkv_dve", turn=un.u))
                act.wait_ge(*S.at("qkv_act", turn=un.u))
                un.ready(act)
                act.activation(raw_c[:, un.j % 4, 3:T + 3], un.bank()[:, 0:T], ACT.Copy)
                un.free(act.activation(conv_y[:, un.j % 4, :], un.bank()[:, 0:T], ACT.Copy, scale=gdn_taps[:, un.u, 3:4]))

            def silu(un):
                S.begin("qkv_act")
                act.wait_ge(*S.at("qkv_dve", turn=un.u + CONV_AHEAD))
                S.inc(act.activation(qkv[:, un.u, :], conv_y[:, un.j % 4, :], ACT.Silu), "qkv_act", "silu")
            each_product(act, "gdn_qkv", 1, project, ACT.Silu, split="hi", late=silu, lag=2)

        def qkv_dve(dve):
            def body(un):
                S.begin("qkv_dve")
                un.was_read(dve)
                y, r = conv_y[:, un.j % 4, :], raw_c[:, un.j % 4, :]
                for t in (0, 1, 2):
                    S.own(dve, "qkv_dve", un.u + CONV_AHEAD)
                    S.inc(dve.scalar_tensor_tensor(out=y, in0=r[:, t:t + T], scalar=gdn_taps[:, un.u, t:t + 1], in1=y,
                                                   op0=ALU.mult, op1=ALU.add), "qkv_dve")
            each_product(dve, "gdn_qkv", 1, body, split="lo")

        L0, L1 = 4, 7
        lvl = cn("level").rearrange("p (l b) -> p l b", b=P)

        def bank(c, i):
            return ps[4 * (c % 2) + i]

        def two(v):
            return v.unsqueeze(2).broadcast_to([v.shape[0], v.shape[1], 2, v.shape[-1]])

        def by2(v):
            return v.rearrange("p (a b) n -> p a b n", b=2)

        def over(v, n):
            return v.unsqueeze(1).broadcast_to([v.shape[0], n, v.shape[-1]])

        def down(v, n):
            return v.unsqueeze(2).broadcast_to([v.shape[0], v.shape[1], n])

        def first_pool(pool):
            inc = lambda ins, step=None: S.inc(ins, "first_pool", step)
            pool.wait_ge(*S.at("rows_dve", "rows"))
            pool.wait_ge(*S.at("rown_dve", "rows", 0))
            for q, src in enumerate((rrow[:, 0, :], row[R_BETA], row[R_G], row[R_EG])):
                pool.dma_start(scratch[16 * q:16 * q + 16, :], src).then_inc(S.sem("scan_rows_out"), 16)
            pool.wait_ge(S.sem("scan_rows_out"), 64)
            pool.dma_start(bc0, on_all(scratch, 0, (T, 64), (1, META))).then_inc(S.sem("first_rows_in"), 16)
            fetch_rows(pool, 0)
            for l in range(1, L0):
                if l == 1:
                    pool.wait_ge(*S.at("first_dve", "XT0"))
                else:
                    pool.wait_ge(*S.at("first_pe", f"Y{l - 1}"))
                inc(pool.tensor_tensor(c0["Am"], c0["A0T"], over(lvl[0:META, l, 0:META], HV), ALU.mult), f"Am{l}")

        def first_dve(dve):
            inc = lambda ins, step=None: S.inc(ins, "first_dve", step)
            own = lambda: S.own(dve, "first_dve")
            dve.wait_ge(S.sem("first_rows_in"), 16)
            inc(dve.tensor_tensor(kn0, qkv[:, 8:16, 0:META], bc0[:, 8:16, :], ALU.mult))
            inc(dve.tensor_tensor(qn0, qkv[:, 0:8, 0:META], bc0[:, 0:8, :], ALU.mult), "kn")
            inc(dve.tensor_tensor(c0["dec"], bc0[0:META, 32:48, :], over(cn("causal")[0:META, 0:META], HV), ALU.add))
            own()
            inc(dve.tensor_tensor(c0["dec"], c0["dec"], down(colv[0:META, 0, 1, :], META), ALU.subtract), "diff")
            dve.wait_ge(*S.at("first_act", "dec"))
            inc(dve.tensor_tensor(c0["decb"], c0["dec"], bc0[0:META, 16:32, :], ALU.mult))
            own()
            dve.wait_ge(*S.at("first_pe", "kq"))
            kk, kq = (ps[6][0:META, 128 * i:128 * (i + 1)].rearrange("p (a b) -> p a b", b=META) for i in range(2))
            inc(dve.tensor_tensor(by2(c0["A0T"]), two(kk), by2(c0["decb"]), ALU.mult))
            inc(dve.tensor_tensor(by2(c0["attn"]), two(kq), by2(c0["dec"]), ALU.mult), "attn")
            own()
            inc(dve.tensor_tensor(c0["Y"], c0["A0T"], over(lvl[0:META, 0, 0:META], HV), ALU.mult))
            own()
            inc(dve.tensor_tensor(c0["XT"], over(ident[0:META, 0:META], HV), c0["Y"], ALU.subtract), "XT0")
            dve.wait_ge(*S.at("first_pe", "tok"))
            for b in range(2):
                kt = two(tile4(ps[b][0:META, :]))
                inc(dve.tensor_tensor(by2(ktl0[0:META, 8 * b:8 * b + 8, :]), kt, by2(down(colv[0:META, 0, 2, 8 * b:8 * b + 8], P)), ALU.mult))
            for b in range(4):
                inc(dve.tensor_tensor(vb0[0:META, 4 * b:4 * b + 4, :], tile4(ps[2 + b][0:META, :]), down(colv[0:META, 0, 0, 4 * b:4 * b + 4], P),
                                      ALU.mult), "vb" if b == 3 else None)
            for l in range(1, L0):
                if l < L0 - 1:
                    dve.wait_ge(*S.at("first_pe", f"XX{l}"))
                    inc(dve.tensor_tensor(c0["X"], c0["X"], ps[7][0:META, 256:512].rearrange("p (a b) -> p a b", b=META), ALU.subtract))
                dve.wait_ge(*S.at("first_pe", f"XXT{l}"))
                inc(dve.tensor_tensor(c0["XT"], c0["XT"], ps[6][0:META, 256:512].rearrange("p (a b) -> p a b", b=META), ALU.subtract), f"XT{l}")
            dve.wait_ge(*S.at("first_pe", "S"))
            for b in range(2):
                inc(dve.tensor_copy(St0[:, 4 * b:4 * b + 4, :], tile4(ps[b])), "S" if b else None)

        def first_act(act):
            inc = lambda ins, step=None: S.inc(ins, "first_act", step)
            act.wait_ge(*S.at("first_dve", "diff"))
            inc(act.activation(c0["dec"], c0["dec"], ACT.Exp), "dec")
            act.wait_ge(*S.at("first_pe", "X"))
            inc(act.activation(c0["X"], ps[7][0:META, 256:512].rearrange("p (a b) -> p a b", b=META), ACT.Copy), "X")
            for l in range(1, L0):
                act.wait_ge(*S.at("first_pe", f"Y{l}"))
                inc(act.activation(c0["Y"], ps[7][0:META, 0:256].rearrange("p (a b) -> p a b", b=META), ACT.Copy), f"Y{l}")
            act.wait_ge(*S.at("first_pe", "vn"))
            for b in range(4):
                inc(act.activation(vb0[0:META, 4 * b:4 * b + 4, :], tile4(ps[2 + b][0:META, :]), ACT.Copy), "vn" if b == 3 else None)
            act.wait_ge(*S.at("first_pe", "o"))
            inc(act.activation(qkv[:, 16:32, 0:META], ps[6][:, 0:256].rearrange("p (a b) -> p a b", b=META), ACT.Copy))
            act.wait_ge(*S.at("first_pe", "S"))
            for b in (2, 3):
                inc(act.activation(St0[:, 4 * b:4 * b + 4, :], tile4(ps[b]), ACT.Copy), "S" if b == 3 else None)

        def first_pe(pe):
            inc = lambda ins, step=None: S.inc(ins, "first_pe", step)
            small = lambda b, half, h: ps[b][0:META, 256 * half + h * META:256 * half + (h + 1) * META]
            pe.wait_ge(*S.at("first_dve", "kn"))
            for h in range(HQ):
                pe.matmul(small(6, 0, h), kn0[:, h, :], kn0[:, h, :], start=True, stop=True)
                mm = pe.matmul(small(6, 0, 8 + h), kn0[:, h, :], qn0[:, h, :], start=True, stop=True)
            inc(mm, "kq")
            for h in range(HQ):
                pe.transpose(ps[h // 4][0:META, h % 4 * P:(h % 4 + 1) * P], kn0[:, h, :], ident)
            for h in range(HV):
                mm = pe.transpose(ps[2 + h // 4][0:META, h % 4 * P:(h % 4 + 1) * P], qkv[:, 16 + h, 0:META], ident)
            inc(mm, "tok")
            pe.wait_ge(*S.at("first_dve", "XT0"))
            for h in range(HV):
                mm = pe.transpose(small(7, 1, h), c0["XT"][:, h, :], ident[0:META, 0:META])
            inc(mm, "X")
            for l in range(1, L0):
                pe.wait_ge(*S.at("first_pool", f"Am{l}"))
                if l == 1:
                    pe.wait_ge(*S.at("first_act", "X"))
                pe.wait_ge(*S.at("first_dve", f"XT{l - 1}"))
                for h in range(HV):
                    mm = pe.matmul(small(7, 0, h), c0["Am"][:, h, :], c0["X"][:, h, :], start=True, stop=True)
                inc(mm, f"Y{l}")
                pe.wait_ge(*S.at("first_act", f"Y{l}"))
                if l < L0 - 1:
                    for h in range(HV):
                        mm = pe.matmul(small(7, 1, h), c0["XT"][:, h, :], c0["Y"][:, h, :], start=True, stop=True)
                    inc(mm, f"XX{l}")
                for h in range(HV):
                    mm = pe.matmul(small(6, 1, h), c0["Y"][:, h, :], c0["XT"][:, h, :], start=True, stop=True)
                inc(mm, f"XXT{l}")
            pe.wait_ge(*S.at("first_dve", f"XT{L0 - 1}"))
            for h in range(HV):
                mm = pe.matmul(ps[2 + h // 4][0:META, h % 4 * P:(h % 4 + 1) * P], c0["XT"][:, h, :], vb0[0:META, h, :], start=True, stop=True)
            inc(mm, "vn")
            pe.wait_ge(*S.at("first_act", "vn"))
            for h in range(HV):
                mm = pe.matmul(ps[6][:, h * META:(h + 1) * META], vb0[0:META, h, :], c0["attn"][:, h, :], start=True, stop=True)
            inc(mm, "o")
            for h in range(HV):
                mm = pe.matmul(ps[h // 4][:, h % 4 * P:(h % 4 + 1) * P], ktl0[0:META, h, :], vb0[0:META, h, :], start=True, stop=True)
            inc(mm, "S")

        def fetch_rows(pool, t):
            pool.dma_start(bc[:, 0:2, :], on_all(scratch, t * (2 * T), (T, 2), (1, T))).then_inc(S.sem("bc_in"), 16)
            pool.dma_start(bc[:, 2:4, :], on_all(scratch, t * (2 * T) + 8 * T, (T, 2), (1, T))).then_inc(S.sem("bc_in"), 16)
            pool.dma_start(bc[:, 4:16, :].rearrange("p (a b) t -> p a b t", b=4),
                           on_all(scratch, t * (4 * T) + 16 * T, (16 * T, 3), (T, 4), (1, T))).then_inc(S.sem("bc_in"), 16)

        def ahead_kn(dve, t):
            S.begin("ahead_dve")
            dve.wait_ge(S.sem("bc_in"), t * 48 + 48)
            qk = work[:, 0:16 * T].rearrange("p (s g h t) -> p s g h t", s=2, h=2, t=T)
            S.inc(dve.tensor_tensor(qn, qk[:, 0, t, :, :], bc[:, 0:2, :], ALU.mult), "ahead_dve")
            S.inc(dve.tensor_tensor(kn, qk[:, 1, t, :, :], bc[:, 2:4, :], ALU.mult), "ahead_dve", "kn")

        def ahead_diff(dve, t):
            for c in (1, 2):
                t0, n = TILES[c]
                S.inc(dve.tensor_tensor(buf[c]["dec"], bc[:, 8:12, t0:t0 + n], over(cn("causal")[:, 0:P], 4), ALU.add), "ahead_dve")
            for c in (1, 2):
                S.own(dve, "ahead_dve", t)
                g_col = colv[:, c, 1, :].rearrange("p (g h) -> p g h", h=4)[:, t, :]
                S.inc(dve.tensor_tensor(buf[c]["dec"], buf[c]["dec"], down(g_col, P), ALU.subtract), "ahead_dve", f"diff{c}")

        def ahead_v(act, t):
            S.begin("ahead_act")
            v = work[:, 16 * T:32 * T].rearrange("p (g h t) -> p g h t", h=4, t=T)[:, t, :, META:T]
            S.inc(act.activation(vs[:, :, META:T], v, ACT.Copy), "ahead_act", "v")

        def ahead_exp(act, t):
            for c in (1, 2):
                act.wait_ge(*S.at("ahead_dve", f"diff{c}", t))
                S.inc(act.activation(buf[c]["dec"], buf[c]["dec"], ACT.Exp), "ahead_act", f"dec{c}")

        def ahead_beta(pool, t):
            S.begin("ahead_pool")
            for c in (1, 2):
                t0, n = TILES[c]
                pool.wait_ge(*S.at("ahead_act", f"dec{c}", t))
                S.inc(pool.tensor_tensor(buf[c]["decb"], buf[c]["dec"], bc[:, 4:8, t0:t0 + n], ALU.mult), "ahead_pool", f"decb{c}")

        CHUNKS, TOP = (1, 2), L1 - 1

        def group_pool(pool, g, last):
            inc = lambda ins, step=None: S.inc(ins, "scan_pool", step)
            S.begin("scan_pool")

            def on_level(c, l):
                B = buf[c]
                inc(pool.tensor_tensor(B["Am"], B["A0T"], over(lvl[:, l, :], 4), ALU.mult), f"Am{c}.{l}")
            for c in CHUNKS:
                pool.wait_ge(*S.at("scan_dve", f"A0T{c}", g))
                on_level(c, 1)
            inc(pool.tensor_tensor(by2(qd[:, :, META:T]), two(qn[:, :, META:T]), by2(bc[:, 12:16, META:T]), ALU.mult), "qd")
            for l in range(2, L1):
                for c in CHUNKS:
                    pool.wait_ge(*S.at("scan_pe", f"Y{c}.{l - 1}", g))
                    on_level(c, l)
                if l == 3 and not last:
                    pool.wait_ge(*S.at("scan_dve", "decayed", g))
                    pool.wait_ge(*S.at("scan_pool", "qd", g))
                    fetch_rows(pool, g + 1)
            if not last:
                ahead_beta(pool, g + 1)

        def group_dve(dve, g, last):
            inc = lambda ins, step=None: S.inc(ins, "scan_dve", step)
            own = lambda: S.own(dve, "scan_dve", g)
            S.begin("scan_dve")
            cv = colv[:, :, :, :].rearrange("p c q (g h) -> p c q g h", h=4)
            cb = colb[:, :, :].rearrange("p c (g h) -> p c g h", h=4)
            half = lambda v, i: tile4(v)[:, 2 * i:2 * i + 2, :]
            for c in CHUNKS:
                B = buf[c]
                dve.wait_ge(*S.at("scan_pe", f"kk{c}", g))
                dve.wait_ge(*S.at("ahead_pool", f"decb{c}", g))
                inc(dve.tensor_tensor(by2(B["A0T"]), two(half(bank(c, 0), 0)), by2(B["decb"]), ALU.mult), f"A0T{c}")
                own()
                inc(dve.tensor_tensor(B["Y"], B["A0T"], over(lvl[:, 0, :], 4), ALU.mult))
                own()
                inc(dve.tensor_tensor(B["XT"], over(ident, 4), B["Y"], ALU.subtract), f"XT{c}.0")

            def attn(c):
                B = buf[c]
                inc(dve.tensor_tensor(by2(B["attn"]), two(half(bank(c, 3), 0)), by2(B["dec"]), ALU.mult))

            def keys(c, name, scale):
                inc(dve.tensor_tensor(by2(buf[c][name]), two(half(bank(c, 3), 1)), by2(down(scale, P)), ALU.mult), f"{name}{c}")

            for l in range(1, L1):
                for c in CHUNKS:
                    B = buf[c]
                    if l < TOP:
                        dve.wait_ge(*S.at("scan_pe", f"XX{c}.{l}", g))
                        inc(dve.tensor_tensor(B["X"], B["X"], tile4(bank(c, 1)), ALU.subtract), f"X{c}.{l}")
                    dve.wait_ge(*S.at("scan_pe", f"XXT{c}.{l}", g))
                    inc(dve.tensor_tensor(B["XT"], B["XT"], tile4(bank(c, 2)), ALU.subtract), f"XT{c}.{l}")
                if l == 1:
                    attn(1)
                    attn(2)
                elif l == 2:
                    inc(dve.tensor_copy(St, St0[:, :, :].rearrange("p (g h) n -> p g h n", h=4)[:, g, :, :]))
                    own()
                    last_token = TILES[1][0] + P - 1
                    inc(dve.tensor_tensor(St2, St, bc[:, 12:16, last_token:last_token + 1].broadcast_to([P, 4, P]), ALU.mult), "decayed")
                elif l == 3:
                    for c in CHUNKS:
                        keys(c, "nkbe", cb[:, c, g, :])
                elif l == 4:
                    for c in CHUNKS:
                        keys(c, "ktl", cv[:, c, 2, g, :])
                    if not last:
                        ahead_kn(dve, g + 1)
                elif l == 5 and not last:
                    ahead_diff(dve, g + 1)
            dve.wait_ge(*S.at("scan_pe", "S", g))
            inc(dve.tensor_tensor(St2, St2, tile4(bank(1, 3)), ALU.add), "S")

        def group_act(act, g, last):
            inc = lambda ins, step=None: S.inc(ins, "scan_act", step)
            S.begin("scan_act")
            cv = colv[:, :, :, :].rearrange("p c q (g h) -> p c q g h", h=4)
            for c in CHUNKS:
                B = buf[c]
                act.wait_ge(*S.at("scan_pe", f"tok{c}", g))
                for h in range(4):
                    ins = act.activation(B["vb"][:, h, :], bank(c, 1)[:, h * P:(h + 1) * P], ACT.Copy, scale=cv[:, c, 0, g, h:h + 1])
                inc(ins, f"vb{c}")
                act.wait_ge(*S.at("scan_pe", f"X{c}", g))
                inc(act.activation(B["X"], tile4(bank(c, 2)), ACT.Copy), f"X{c}")
            for l in range(1, L1):
                for c in CHUNKS:
                    act.wait_ge(*S.at("scan_pe", f"Y{c}.{l}", g))
                    inc(act.activation(buf[c]["Y"], tile4(bank(c, 0)), ACT.Copy), f"Y{c}.{l}")
                if l == 3 and not last:
                    ahead_v(act, g + 1)
            if not last:
                ahead_exp(act, g + 1)
            for c in CHUNKS:
                act.wait_ge(*S.at("scan_pe", f"wT{c}", g))
                inc(act.activation(buf[c]["Am"], tile4(bank(c, 0)), ACT.Copy), f"wT{c}")
            for c in CHUNKS:
                t0, n = TILES[c]
                act.wait_ge(*S.at("scan_pe", f"vn{c}", g))
                inc(act.activation(buf[c]["X"], tile4(bank(c, 1)), ACT.Copy), f"vn{c}")
                act.wait_ge(*S.at("scan_pe", f"o{c}", g))
                dst = work[:, 16 * T:32 * T].rearrange("p (g h t) -> p g h t", h=4, t=T)[:, g, :, t0:t0 + n]
                ins = act.activation(dst, tile4(bank(c, 2)), ACT.Copy)
                if c == 1:
                    inc(ins, "o1")
                else:
                    ins.then_inc(S.sem("group_out"), 1)

        def group_pe(pe, g):
            inc = lambda ins, step=None: S.inc(ins, "scan_pe", step)
            S.begin("scan_pe")
            H4 = range(4)
            col = lambda h: slice(h * P, (h + 1) * P)
            pe.wait_ge(*S.at("ahead_dve", "kn", g))
            pe.wait_ge(*S.at("ahead_act", "v", g))
            for c in CHUNKS:
                t0, n = TILES[c]
                for h in range(2):
                    mm = pe.matmul(bank(c, 0)[:, col(h)], kn[:, h, t0:t0 + n], kn[:, h, t0:t0 + n], start=True, stop=True)
                inc(mm, f"kk{c}")
            for c in CHUNKS:
                t0, n = TILES[c]
                for h in H4:
                    mm = pe.transpose(bank(c, 1)[:, col(h)], vs[:, h, t0:t0 + n], ident)
                inc(mm, f"tok{c}")
                for h in range(2):
                    pe.matmul(bank(c, 3)[:, col(h)], kn[:, h, t0:t0 + n], qn[:, h, t0:t0 + n], start=True, stop=True)
                    pe.transpose(bank(c, 3)[:, col(2 + h)], kn[:, h, t0:t0 + n], ident)
            pe.wait_ge(S.sem("group_out"), g + 1)
            for c in CHUNKS:
                pe.wait_ge(*S.at("scan_dve", f"XT{c}.0", g))
                for h in H4:
                    mm = pe.transpose(bank(c, 2)[:, col(h)], buf[c]["XT"][:, h, :], ident)
                inc(mm, f"X{c}")
            for l in range(1, L1):
                for c in CHUNKS:
                    B = buf[c]
                    pe.wait_ge(*S.at("scan_pool", f"Am{c}.{l}", g))
                    if l == 1:
                        pe.wait_ge(*S.at("scan_act", f"X{c}", g))
                    else:
                        pe.wait_ge(*S.at("scan_dve", f"X{c}.{l - 1}", g))
                    for h in H4:
                        mm = pe.matmul(bank(c, 0)[:, col(h)], B["Am"][:, h, :], B["X"][:, h, :], start=True, stop=True)
                    inc(mm, f"Y{c}.{l}")
                for c in CHUNKS:
                    B = buf[c]
                    pe.wait_ge(*S.at("scan_act", f"Y{c}.{l}", g))
                    pe.wait_ge(*S.at("scan_dve", f"XT{c}.{l - 1}", g))
                    if l < TOP:
                        for h in H4:
                            mm = pe.matmul(bank(c, 1)[:, col(h)], B["XT"][:, h, :], B["Y"][:, h, :], start=True, stop=True)
                        inc(mm, f"XX{c}.{l}")
                    for h in H4:
                        mm = pe.matmul(bank(c, 2)[:, col(h)], B["Y"][:, h, :], B["XT"][:, h, :], start=True, stop=True)
                    inc(mm, f"XXT{c}.{l}")
            for c in CHUNKS:
                pe.wait_ge(*S.at("scan_dve", f"XT{c}.{TOP}", g))
                for h in H4:
                    mm = pe.matmul(bank(c, 0)[:, col(h)], buf[c]["nkbe"][:, h, :], buf[c]["XT"][:, h, :], start=True, stop=True)
                inc(mm, f"wT{c}")
            for c in CHUNKS:
                B, state = buf[c], St if c == 1 else St2
                t0, n = TILES[c]
                pe.wait_ge(*S.at("scan_act", f"wT{c}", g))
                if c == 2:
                    pe.wait_ge(*S.at("scan_dve", "S", g))
                for h in H4:
                    pe.matmul(bank(c, 1)[:, col(h)], B["XT"][:, h, :], B["vb"][:, h, :], start=True, stop=False)
                    mm = pe.matmul(bank(c, 1)[:, col(h)], B["Am"][:, h, :], state[:, h, :], start=False, stop=True)
                inc(mm, f"vn{c}")
                pe.wait_ge(*S.at("scan_act", f"vn{c}", g))
                if c == 1:
                    for h in H4:
                        mm = pe.matmul(bank(c, 3)[:, col(h)], B["ktl"][:, h, :], B["X"][:, h, :], start=True, stop=True)
                    inc(mm, "S")
                pe.wait_ge(*S.at("scan_pool", "qd", g))
                for h in H4:
                    pe.matmul(bank(c, 2)[:, col(h)], state[:, h, :], qd[:, h, t0:t0 + n], start=True, stop=False)
                    mm = pe.matmul(bank(c, 2)[:, col(h)], B["X"][:, h, :], B["attn"][:, h, :], start=False, stop=True)
                inc(mm, f"o{c}")

        GROUPS = 4

        def scan_pool(pool):
            first_pool(pool)
            ahead_beta(pool, 0)
            with pool.Fori(0, GROUPS - 1) as g:
                group_pool(pool, g, False)
            group_pool(pool, GROUPS - 1, True)

        def scan_dve(dve):
            first_dve(dve)
            ahead_kn(dve, 0)
            ahead_diff(dve, 0)
            with dve.Fori(0, GROUPS - 1) as g:
                group_dve(dve, g, False)
            group_dve(dve, GROUPS - 1, True)

        def scan_act(act):
            act.preload_act_table(ACT.Exp)
            ahead_v(act, 0)
            first_act(act)
            ahead_exp(act, 0)
            with act.Fori(0, GROUPS - 1) as g:
                group_act(act, g, False)
            group_act(act, GROUPS - 1, True)

        def scan_pe(pe):
            first_pe(pe)
            pe.wait_ge(*S.at("first_dve", "S"))
            pe.wait_ge(*S.at("first_act", "S"))
            with pe.Fori(0, GROUPS - 1) as g:
                group_pe(pe, g)
            group_pe(pe, GROUPS - 1)

        def scan_done(eng):
            eng.wait_ge(S.sem("group_out"), GROUPS + 1)
            eng.wait_ge(*S.at("scan_dve", "S", GROUPS - 1))
            eng.wait_ge(*S.at("scan_pool", turn=GROUPS - 1))

        def gate_pool(pool):
            pool.wait_ge(*S.at("rown_dve", "rows", 1))
            pool.dma_start(scr_o, rrow[:, 0, :]).then_inc(S.sem("o_rows_out"), 16)
            pool.wait_ge(S.sem("o_rows_out"), 16)
            pool.dma_start(obc, on_all(scr_o, 0, (T, HV), (1, T))).then_inc(S.sem("o_rows_in"), 16)

        def gate_act(act):
            def body(un):
                un.ready(act)
                act.wait_ge(*S.at("gate_dve", turn=un.u))
                un.free(act.activation(zs[:, un.j % 4, :], un.bank()[:, 0:T], ACT.Silu))
            each_product(act, "gdn_z", 1, body, ACT.Silu, split="hi")

        def gate_dve(dve):
            dve.wait_ge(S.sem("o_rows_in"), 16)

            def body(un):
                S.begin("gate_dve")
                o = qkv[:, 16 + un.u, :]
                S.inc(dve.scalar_tensor_tensor(out=o, in0=o, scalar=pm("gdn_norm"), in1=obc[:, un.u, :], op0=ALU.mult, op1=ALU.mult), "gate_dve")
                S.own(dve, "gate_dve", un.u + 4)
                un.was_read(dve)
                S.inc(dve.tensor_tensor(o, o, zs[:, un.j % 4, :], ALU.mult), "gate_dve")
            each_product(dve, "gdn_z", 1, body, split="lo")
            dve.wait_ge(*S.at("gate_dve", turn=15 + 4))

        def evac_mix_act(act, name):
            each_product(act, name, 1, lambda un: (un.ready(act), un.free(act.activation(mix[:, un.u, :], un.bank()[:, 0:T], ACT.Copy))), split="hi")

        def mix_was_read(eng, name):
            for j in range(4, 8):
                Unit(PLAN[name], 1, j, 0, 0).was_read(eng)

        def ffn_params(layer):
            at, n = PARAM_COLS["ffn_conv"]
            taps = Pm[:, at + n // 2 * layer:at + n // 2 * (layer + 1)].rearrange("p (b m t) -> p b m t", m=2, t=3)
            at, n = PARAM_COLS["ffn_bias"]
            return taps, Pm[:, at + n // 2 * layer:at + n // 2 * (layer + 1)].rearrange("p (b m) -> p b m", m=2)

        def conv_up_act(act, layer):
            taps, bias = ffn_params(layer)

            def project(un):
                p2 = un.j % 2
                act.wait_ge(*S.at("up_dve", turn=un.u + FB * layer))
                act.wait_ge(*S.at("up_pool", turn=un.u + FB * layer))
                for m in range(2):
                    un.ready(act, m)
                    act.activation(raw[p2][:, m, 2:T + 2], un.bank(m)[:, 0:T], ACT.Copy)
                    un.free(act.activation(y_gu[p2][:, m, :], un.bank(m)[:, 0:T], ACT.Identity, bias=bias[:, un.u, m:m + 1],
                                           scale=taps[:, un.u, m, 2:3]), m)

            def silu(un):
                S.begin("up_act")
                act.wait_ge(*S.at("up_dve", turn=un.u + FB * layer + 2))
                act.wait_ge(*S.at("up_pool", turn=un.u + FB * layer))
                S.inc(act.activation(silu_g[un.j % 2], y_gu[un.j % 2][:, 0, :], ACT.Silu), "up_act")
            each_product(act, f"up{layer}", 2, project, ACT.Silu, split="hi", late=silu, lag=1)

        def conv_up_dve(dve, layer):
            taps, bias = ffn_params(layer)

            def body(un):
                p2 = un.j % 2
                S.begin("up_dve")
                for t in range(2):
                    if t:
                        S.own(dve, "up_dve", un.u + FB * layer + 2)
                    for m in range(2):
                        if t == 0:
                            un.was_read(dve, m)
                        y = y_gu[p2][:, m, :]
                        S.inc(dve.scalar_tensor_tensor(out=y, in0=raw[p2][:, m, t:t + T], scalar=taps[:, un.u, m, t:t + 1], in1=y,
                                                       op0=ALU.mult, op1=ALU.add), "up_dve")
            each_product(dve, f"up{layer}", 2, body, split="lo")

        def conv_up_pool(pool, layer):
            def body(un):
                S.begin("up_pool")
                pool.wait_ge(*S.at("up_act", turn=un.u + 22 * layer + 2))
                turn = un.u + 22 * layer + 2
                h = h_new[un.j % 2]
                S.inc(pool.tensor_tensor(h, silu_g[un.j % 2], y_gu[un.j % 2][:, 1, :], ALU.mult), "up_pool")
                S.own(pool, "up_pool", turn)
                S.inc(pool.tensor_copy(hid_hi[:, un.u, :], h), "up_pool")
                S.own(pool, "up_pool", turn)
                S.inc(pool.tensor_tensor(hid_lo[:, un.u, :], h, hid_hi[:, un.u, :].bitcast(F32), ALU.subtract), "up_pool")
            each_product(pool, f"up{layer}", 2, body)
        MG = Unit(PLAN["ml_gates"], 1, 0, 0, 0)

        def ml_rows_act(act):
            inc = lambda ins, step=None: S.inc(ins, "mlr_act", step)
            act.wait_ge(*S.at("mlr_dve", "raw"))
            inc(act.activation(mrow[M_Y], mrow[M_Y], ACT.Tanh, scale=1.0 / 15.0))
            inc(act.activation(mrow[M_LI], mrow[M_LI], ACT.Tanh, scale=1.0 / 15.0), "tanh")
            S.own(act, "mlr_act")
            inc(act.activation(mrow[M_E], mrow[M_Y], ACT.Abs))
            S.own(act, "mlr_act")
            inc(act.activation(mrow[M_E], mrow[M_E], ACT.Exp, scale=-15.0))
            S.own(act, "mlr_act")
            inc(act.activation(mrow[M_E], mrow[M_E], ACT.Ln, bias=1.0), "ln")
            act.wait_ge(*S.at("mlr_dve", "m"))
            inc(act.activation(mrow[M_EM], mrow[M_T], ACT.Exp, scale=-1.0), "em")

        def ml_rows_dve(dve):
            inc = lambda ins, step=None: S.inc(ins, "mlr_dve", step)
            own = lambda: S.own(dve, "mlr_dve")
            MG.ready(dve)
            inc(dve.tensor_scalar(mrow[M_LI], MG.bank()[0:ML_H, 0:T], pm("ml_gate_i")[0:ML_H, :], None, ALU.add))
            own()
            MG.free(dve.tensor_scalar(mrow[M_T], MG.bank()[32:32 + ML_H, 0:T], pm("ml_gate_f")[0:ML_H, :], None, ALU.add))
            MG.was_read(dve)
            inc(dve.tensor_copy(mrow[M_Y], mrow[M_T]), "raw")
            inc(dve.memset(mrow[M_ONE], 1.0))
            dve.wait_ge(*S.at("mlr_act", "ln"))
            own()
            inc(dve.tensor_scalar(mrow[M_T], mrow[M_Y], 15.0, 0.0, ALU.mult, ALU.min))
            own()
            inc(dve.tensor_tensor(mrow[M_C], mrow[M_T], mrow[M_E], ALU.subtract))
            own()
            inc(dve.tensor_tensor_scan(mrow[M_B], mrow[M_ONE], mrow[M_C], 0.0, ALU.mult, ALU.add))
            own()
            inc(dve.scalar_tensor_tensor(out=mrow[M_C], in0=mrow[M_LI], scalar=15.0, in1=mrow[M_B], op0=ALU.mult, op1=ALU.subtract), "c")
            own()
            inc(dve.tensor_tensor_scan(mrow[M_M], mrow[M_ONE], mrow[M_C], 0.0, ALU.mult, ALU.max))
            own()
            inc(dve.tensor_tensor(mrow[M_T], mrow[M_B], mrow[M_M], ALU.add), "m")

        def ml_rows_pe(pe):
            pe.wait_ge(*S.at("mlr_dve", "c"))
            for c, (t0, n) in enumerate(TILES):
                mm = pe.transpose(PSB[0:n, c * ML_H:(c + 1) * ML_H], mrow[M_C][:, t0:t0 + n], ident[0:ML_H, 0:ML_H])
            S.inc(mm, "mlr_pe")

        def ml_cols_dve(dve):
            dve.wait_ge(*S.at("mlr_pe"))
            for c, (t0, n) in enumerate(TILES):
                S.inc(dve.tensor_copy(mcol[0:n, c, :], PSB[0:n, c * ML_H:(c + 1) * ML_H]), "mcol_dve")

        def ml_pool(pool):
            pool.wait_ge(*S.at("mlr_act", "em"))
            pool.dma_start(scr_m[0:ML_H, :], mrow[M_M]).then_inc(S.sem("ml_rows_out"), 16)
            pool.dma_start(scr_m[ML_H:2 * ML_H, :], mrow[M_EM]).then_inc(S.sem("ml_rows_out"), 16)
            pool.wait_ge(S.sem("ml_rows_out"), 32)
            pool.dma_start(bc2, on_all(scr_m, 0, (ML_H * T, 2), (T, ML_H), (1, T))).then_inc(S.sem("ml_rows_in"), 16)

        def ml_in_act(act):
            def body(un):
                un.ready(act)
                un.free(act.activation(mlT[:, un.u, :], un.bank()[:, 0:T], ACT.Copy if un.j < 16 else ACT.Sigmoid))
            each_product(act, "ml_in", 1, body, turns=2, split="hi")

        def ml_read(eng, last):
            for j in range(last - 4, last):
                Unit(PLAN["ml_in"], 1, j, 0, 0).was_read(eng)

        def ml_pe(pe):
            inc = lambda ins, step=None: S.inc(ins, "ml_pe", step)
            ml_read(pe, 24)
            for c, (t0, n) in enumerate(TILES):
                for k in range(8):
                    mm = pe.transpose(ps[4 + k // 4][0:n, (k % 4) * P:(k % 4 + 1) * P], mlT[:, 8 + k, t0:t0 + n], ident)
                    if k % 4 == 3:
                        inc(mm, f"v{c}.{k // 4}")
                if c < 2:
                    pe.wait_ge(*S.at("ml_act", f"v{c}.1"))
            pe.wait_ge(*S.at("ml_act", "v2.1"))
            for h in range(ML_H):
                bank4 = ps[4 * (h % 2):4 * (h % 2) + 4]
                if h >= 2:
                    pe.wait_ge(*S.at("ml_dve", f"h{h - 2}"))
                for c, (t0, n) in enumerate(TILES):
                    if c > 0:
                        pe.wait_ge(*S.at("ml_dve", f"P{h}.{c - 1}"))
                    inc(pe.matmul(bank4[0][0:n, 0:T - t0], mlT[:, 4 + h, t0:t0 + n], mlT[:, h, t0:T], start=True, stop=True), f"S{h}.{c}")
                for c, (t0, n) in enumerate(TILES):
                    pe.wait_ge(*S.at("ml_dve", f"P{h}.{c}"))
                    Pm_ = Pt[h % 2][c][0:n, 0:T - t0]
                    kw = dict(start=(c == 0), stop=(c == 2))
                    pe.matmul(bank4[1][:, t0:T], v_tok[0:n, c, 2 * h, :], Pm_, **kw)
                    pe.matmul(bank4[2][:, t0:T], v_tok[0:n, c, 2 * h + 1, :], Pm_, **kw)
                    mm = pe.matmul(bank4[3][:, t0:T], ones[0:n, :], Pm_, **kw)
                inc(mm, f"num{h}")

        def ml_act(act):
            inc = lambda ins, step=None: S.inc(ins, "ml_act", step)
            for c, (t0, n) in enumerate(TILES):
                for q in range(2):
                    act.wait_ge(*S.at("ml_pe", f"v{c}.{q}"))
                    inc(act.activation(v_tok[0:n, c, 4 * q:4 * q + 4, :], tile4(ps[4 + q][0:n, :]), ACT.Copy), f"v{c}.{q}")
            for h in range(ML_H):
                for c, (t0, n) in enumerate(TILES):
                    act.wait_ge(*S.at("ml_dve", f"D{h}.{c}"))
                    w = Wt[h % 2][c][0:n, 0:T - t0]
                    inc(act.activation(w, w, ACT.Exp, bias=mcol[0:n, c, h:h + 1]), f"W{h}.{c}")

        def ml_dve(dve):
            inc = lambda ins, step=None: S.inc(ins, "ml_dve", step)
            own = lambda: S.own(dve, "ml_dve")
            dve.wait_ge(S.sem("ml_rows_in"), 16)
            S.own(dve, "mcol_dve")

            def distances(h):
                for c, (t0, n) in enumerate(TILES):
                    inc(dve.scalar_tensor_tensor(out=Wt[h % 2][c][0:n, 0:T - t0], in0=bc2[0:n, 0, h, t0:T], scalar=-1.0,
                                                 in1=cn("causal")[0:n, 0:T - t0], op0=ALU.mult, op1=ALU.add), f"D{h}.{c}")

            distances(0)
            for h in range(ML_H):
                for c, (t0, n) in enumerate(TILES):
                    dve.wait_ge(*S.at("ml_pe", f"S{h}.{c}"))
                    dve.wait_ge(*S.at("ml_act", f"W{h}.{c}"))
                    inc(dve.scalar_tensor_tensor(out=Pt[h % 2][c][0:n, 0:T - t0], in0=ps[4 * (h % 2)][0:n, 0:T - t0], scalar=P ** -0.5,
                                                 in1=Wt[h % 2][c][0:n, 0:T - t0], op0=ALU.mult, op1=ALU.mult), f"P{h}.{c}")
                if h + 1 < ML_H:
                    own()
                    distances(h + 1)
                dve.wait_ge(*S.at("ml_pe", f"num{h}"))
                own()
                dn = ps[4 * (h % 2) + 3][:, 0:T]
                inc(dve.scalar_tensor_tensor(out=den[:, 0, :], in0=dn, scalar=-1.0, in1=bc2[:, 1, h, :], op0=ALU.mult, op1=ALU.max))
                own()
                inc(dve.tensor_tensor(den[:, 0, :], den[:, 0, :], dn, ALU.max))
                own()
                inc(dve.reciprocal(den[:, 1, :], den[:, 0, :]))
                own()
                inc(dve.tensor_tensor(hT[:, 2 * h, :], ps[4 * (h % 2) + 1][:, 0:T], den[:, 1, :], ALU.mult))
                inc(dve.tensor_tensor(hT[:, 2 * h + 1, :], ps[4 * (h % 2) + 2][:, 0:T], den[:, 1, :], ALU.mult), f"h{h}")
            own()

        def ml_norm_pool(pool):
            pool.wait_ge(*S.at("rown_dve", "rows", 2))
            pool.dma_start(scr_h, rrow[0:ML_H, 0, :]).then_inc(S.sem("ml_norm_out"), 16)
            pool.wait_ge(S.sem("ml_norm_out"), 16)
            pool.dma_start(mbc, on_all(scr_h, 0, (T, ML_H), (1, T))).then_inc(S.sem("ml_norm_in"), 16)

        def ml_norm_dve(dve):
            dve.wait_ge(S.sem("ml_norm_in"), 16)
            for k in range(8):
                S.inc(dve.scalar_tensor_tensor(out=hT[:, k, :], in0=hT[:, k, :], scalar=pm("ml_norm", k), in1=mbc[:, k // 2, :],
                                               op0=ALU.mult, op1=ALU.mult), "mln_dve")
            S.own(dve, "mln_dve")
            S.inc(dve.tensor_tensor(hT, hT, mlT[:, 16:24, :], ALU.mult), "mln_dve")

        h2 = hs[:, :, META:T]
        mem_sb = area(0, DB, SEQ)
        memn = area(2048, DB, SEQ)
        kmem = area(4096, MEM_H, SEQ)
        vmem = area(5120, 2, 512)
        keep_at = 6144
        hid2_hi, hid2_lo = (area(keep_at + i * FB * SEQ, FB, SEQ, of=work_r) for i in range(2))
        sg2 = [area(keep_at + 2 * FB * SEQ + i * SEQ, SEQ) for i in range(4)]
        h2_new = mix[:, 0:4, 0:SEQ]

        def mem_pool(pool):
            pool.wait_ge(*S.at("norm_dve", "done", 7))
            pool.dma_start(mem_sb, mem_t.rearrange("(k p) t -> p k t", p=P)).then_inc(S.sem("mem_in"), 16)

        def mem_act(act):
            act.wait_ge(S.sem("mem_in"), 16)
            norm_act(act, 8, mem_sb, 8, SEQ)
            ph = PLAN["mem_k"]
            for j in range(4):
                un = Unit(ph, 1, j, 0, 0)
                un.ready(act)
                un.free(act.activation(kmem[:, j, :], un.bank()[:, 0:SEQ], ACT.Copy))
            for j in range(4):
                un = Unit(PLAN["mem_v"], 1, j, 0, 0)
                un.ready(act)
                un.free(act.activation(vmem[:, j % 2, j // 2 * SEQ:(j // 2 + 1) * SEQ], un.bank()[:, 0:SEQ], ACT.Copy))

        def mem_pe(pe):
            norm_pe(pe, 8, 8, SEQ)
            pe.wait_ge(*S.at("norm_dve", "done", 8))
            stream_pe(pe, "mem_k", lambda m, k: memn[:, k, :], SEQ)
            ph = PLAN["mem_v"]
            for half in range(2):
                n = ph.slab0 + half
                pe.wait_ge(weights_in[n % SLOTS], 16 * (n // SLOTS + 1))
                for m in range(2):
                    b = ph.product0 + 2 * half + m
                    pe.wait_ge(bank_free[b % BANKS], b // BANKS + 1)
                    for k in range(8):
                        mm = pe.matmul(ps[b % BANKS][:, 0:SEQ], memn[:, k, m * P:(m + 1) * P], ring[:, n % SLOTS, k * SEQ:(k + 1) * SEQ],
                                       start=(k == 0), stop=(k == 7))
                    mm.then_inc(product_done, 1)

        def up_act(act, name):
            def body(un):
                un.ready(act)
                un.was_read(act, 1, before=8)
                un.free(act.activation(sg2[un.j % 4], un.bank()[:, 0:SEQ], ACT.Silu))
            each_product(act, name, 2, body, ACT.Silu, split="hi")

        def up_dve(dve, name):
            def body(un):
                un.ready(dve, 1)
                un.was_read(dve, 0)
                dve.wait_ge(*S.at("hid_pool", turn=un.u + (FB if name == "up3" else 0)))
                un.free(dve.tensor_tensor(h2_new[:, un.j % 4, :], un.bank(1)[:, 0:SEQ], sg2[un.j % 4], ALU.mult), 1)
            each_product(dve, name, 2, body, split="lo")

        def up_pool2(pool, name):
            def body(un):
                turn = un.u + (FB if name == "up3" else 0) + 4
                h = h2_new[:, un.j % 4, :]
                un.was_read(pool, 1)
                S.begin("hid_pool")
                S.inc(pool.tensor_copy(hid2_hi[:, un.u, :], h), "hid_pool")
                S.own(pool, "hid_pool", turn)
                S.inc(pool.tensor_tensor(hid2_lo[:, un.u, :], h, hid2_hi[:, un.u, :].bitcast(F32), ALU.subtract), "hid_pool")
            each_product(pool, name, 2, body)

        def down_dve(dve, name):
            each_product(dve, name, 1, lambda un: (
                un.ready(dve), un.free(dve.scalar_tensor_tensor(out=h2[:, un.u, :], in0=un.bank()[:, 0:SEQ], scalar=0.5,
                                                                in1=h2[:, un.u, :], op0=ALU.mult, op1=ALU.add))), split="lo")

        def phase_read(eng, name, upto=None):
            ph = PLAN[name]
            total = ph.products if upto is None else upto
            for j in range(max(0, total - 4), total):
                Unit(ph, 1, j, 0, 0).was_read(eng)

        u_at = 6144
        uT = area(u_at, 4, SEQ)
        vT = area(u_at + 1024, 4, SEQ)
        cqT = area(u_at + 2048, 4, SEQ)
        qmT = area(u_at + 3072, MEM_H, SEQ)
        ckvT = area(u_at + 4096, 2, SEQ)
        gat = area(u_at + 4608, 24, SEQ)
        br_at = u_at + 4608 + 6144
        yT = [area(br_at + i * 1024, 4, SEQ) for i in range(3)]
        t_at = br_at + 3072
        sq2 = sq[:, :, :].rearrange("p a b -> p (a b)")
        mix2 = mix[:, :, :].rearrange("p a b -> p (a b)")
        a2 = a[:, :, :].rearrange("p a b -> p (a b)")

        def in_act(act):
            for name, fn, dst in (("in_uv", ACT.Gelu, lambda j: (uT if j < 4 else vT)[:, j % 4, :]),
                                  ("in_cq_kr", ACT.Copy, lambda j: cqT[:, j, :]),
                                  ("in_qm", ACT.Copy, lambda j: qmT[:, j, :]),
                                  ("in_ckv", ACT.Copy, lambda j: ckvT[:, j, :])):
                each_product(act, name, 1, lambda un, fn=fn, dst=dst: (
                    un.ready(act), un.free(act.activation(dst(un.j), un.bank()[:, 0:SEQ], fn))), turns=0, split="hi")
            each_product(act, "in_gates", 1, lambda un: (
                un.ready(act), un.free(act.activation(gat[:, un.j, :], un.bank()[:, 0:SEQ], ACT.Sigmoid, bias=pm("b_gate", un.j)))),
                turns=0, split="hi")

        Wsg = area(0, 8, P)
        sg_tok = area(1024, 2, 512)
        sg_bt = area(2048, 4, P)
        vln = mix2[:, 0:1024].rearrange("p (a b) -> p a b", b=SEQ)
        rstat = mix2[:, 1024:2048].rearrange("p (a b) -> p a b", b=SEQ)

        def sg_pool(pool):
            pool.dma_start(Wsg, sg_w_t).then_inc(S.sem("sg_in"), 16)
            for half in range(2):
                pool.dma_start(sg_bt[64 * half:64 * half + 64, :, :],
                               bass.AP(sg_bias.tensor, half * P, [[0, 64], [2 * P, 4], [1, P]])).then_inc(S.sem("sg_in"), 16)

        def sg_pe(pe):
            inc = lambda ins, step=None: S.inc(ins, "sg_pe", step)
            for k in range(4):
                mm = pe.matmul(PSA[:, 0:SEQ], ones, vT[:, k, :], start=(k == 0), stop=(k == 3))
            inc(mm, "mean")
            pe.wait_ge(*S.at("sg_act", "squares"))
            for k in range(4):
                mm = pe.matmul(PSB[:, 0:SEQ], ones, sq[:, k, 0:SEQ], start=(k == 0), stop=(k == 3))
            inc(mm, "var")
            pe.wait_ge(*S.at("sg_dve", "vln"))
            for c in range(2):
                for k in range(4):
                    mm = pe.transpose(ps[6 + c][:, k * P:(k + 1) * P], vln[:, k, c * P:(c + 1) * P], ident)
                inc(mm, f"tok{c}")
            pe.wait_ge(*S.at("sg_dve", "w"))
            for k in range(4):
                if k == 0:
                    pe.wait_ge(*S.at("sg_act", "tok1"))
                if k >= 2:
                    pe.wait_ge(*S.at("sg_dve", f"y{k - 2}"))
                out = ps[4 + k % 2]
                for c in range(2):
                    for q in range(2):
                        mm = pe.matmul(out[64 * q:64 * q + 64, c * P:(c + 1) * P], sg_tok[:, c, (2 * k + q) * 64:(2 * k + q + 1) * 64],
                                       Wsg[:, 2 * k + q, :], start=True, stop=True)
                inc(mm, f"mix{k}")

        def sg_act(act):
            inc = lambda ins, step=None: S.inc(ins, "sg_act", step)
            act.wait_ge(*S.at("sg_dve", "centred"))
            inc(act.activation(sq[:, 0:4, 0:SEQ], vT, ACT.Square), "squares")
            act.wait_ge(*S.at("sg_dve", "var"))
            inc(act.activation(rstat[:, 2, :], rstat[:, 1, :], ACT.Sqrt), "root")
            for c in range(2):
                act.wait_ge(*S.at("sg_pe", f"tok{c}"))
                inc(act.activation(sg_tok[:, c, :], ps[6 + c], ACT.Copy), f"tok{c}")

        def sg_dve(dve):
            inc = lambda ins, step=None: S.inc(ins, "sg_dve", step)
            own = lambda: S.own(dve, "sg_dve")
            dve.wait_ge(*S.at("sg_pe", "mean"))
            inc(dve.tensor_scalar(rstat[:, 0, :], PSA[:, 0:SEQ], 1.0 / 512, None, ALU.mult))
            own()
            inc(dve.tensor_tensor(vT, vT, rstat[:, 0, :].unsqueeze(1).broadcast_to([P, 4, SEQ]), ALU.subtract), "centred")
            dve.wait_ge(*S.at("sg_pe", "var"))
            inc(dve.tensor_scalar(rstat[:, 1, :], PSB[:, 0:SEQ], 1.0 / 512, EPS, ALU.mult, ALU.add), "var")
            dve.wait_ge(*S.at("sg_act", "root"))
            inc(dve.reciprocal(rstat[:, 3, :], rstat[:, 2, :]))
            own()
            for k in range(4):
                inc(dve.scalar_tensor_tensor(out=vln[:, k, :], in0=vT[:, k, :], scalar=pm("sg_g", k), in1=rstat[:, 3, :], op0=ALU.mult, op1=ALU.mult))
            own()
            for k in range(4):
                inc(dve.tensor_scalar(vln[:, k, :], vln[:, k, :], pm("sg_b", k), None, ALU.add), "vln" if k == 3 else None)
            dve.wait_ge(S.sem("sg_in"), 48)
            inc(dve.tensor_tensor(Wsg, Wsg, cn("tri").unsqueeze(1).broadcast_to([P, 8, P]), ALU.mult), "w")
            for k in range(4):
                dve.wait_ge(*S.at("sg_pe", f"mix{k}"))
                y = yT[0][:, k, :].rearrange("p (a b) -> p a b", b=P)
                inc(dve.tensor_tensor(y, ps[4 + k % 2][:, 0:SEQ].rearrange("p (a b) -> p a b", b=P),
                                      sg_bt[:, k, :].unsqueeze(1).broadcast_to([P, 2, P]), ALU.add))
                own()
                inc(dve.tensor_tensor(yT[0][:, k, :], yT[0][:, k, :], uT[:, k, :], ALU.mult), f"y{k}")
            own()

        cqn = mix2[:, 0:768].rearrange("p (a b) -> p a b", b=SEQ)
        ckvn = mix2[:, 768:1280].rearrange("p (a b) -> p a b", b=SEQ)
        trig = a2[:, 0:6 * SEQ].rearrange("p (a b) -> p a b", b=SEQ)
        pos_i = sb("pos_i", [P, SEQ], I32)
        qk16 = area(0, 16, SEQ)
        sq_q = area(u_at, 8, SEQ)
        sq_k = sq2[:, 0:2048].rearrange("p (a b) -> p a b", b=SEQ)
        vtk = area(t_at, 2, 512)
        prob = [area(t_at + 1024 + 512 * i, 512) for i in range(2)]
        probT = [area(t_at + 2048 + 512 * i, 512) for i in range(2)]
        soft = sb("soft", [P, 2, 4, 2])

        def rope_pool(pool):
            pool.dma_start(pos_i[0:QK, :], bass.AP(positions.tensor, 0, [[0, QK], [1, SEQ]])).then_inc(S.sem("pos_in"), 16)

        def rope_dve(dve):
            inc = lambda ins, step=None: S.inc(ins, "rope_dve", step)
            own = lambda: S.own(dve, "rope_dve")
            t = lambda i: trig[0:QK, i, :]
            dve.wait_ge(S.sem("pos_in"), 16)
            inc(dve.tensor_copy(t(1), pos_i[0:QK, :]))
            own()
            inc(dve.tensor_scalar(t(0), t(1), cn("inv_freq")[0:QK, :], None, ALU.mult))
            own()
            for i, quarter in ((2, 0.0), (3, 0.25)):
                inc(dve.tensor_scalar(t(1), t(0), 1.0 / (2 * np.pi), quarter, ALU.mult, ALU.add))
                own()
                inc(dve.tensor_scalar(t(4), t(1), ROUND, None, ALU.add))
                own()
                inc(dve.tensor_scalar(t(1), t(4), -ROUND, None, ALU.add))
                own()
                inc(dve.scalar_tensor_tensor(out=t(4), in0=t(1), scalar=-TWO_PI_HI, in1=t(0), op0=ALU.mult, op1=ALU.add))
                own()
                inc(dve.scalar_tensor_tensor(out=t(i), in0=t(1), scalar=-TWO_PI_LO, in1=t(4), op0=ALU.mult, op1=ALU.add))
                own()
                if quarter:
                    inc(dve.tensor_scalar(t(i), t(i), float(np.pi / 2), None, ALU.add))
                    own()
                inc(dve.tensor_scalar(t(i), t(i), PI_IN, -PI_IN, ALU.min, ALU.max), "args" if quarter else None)
                own()

        def rope_act(act):
            act.wait_ge(*S.at("rope_dve", "args"))
            S.inc(act.activation(trig[0:QK, 2:4, :], trig[0:QK, 2:4, :], ACT.Sin), "rope_act")

        MQ, MK, MV = PLAN["mla_q"], PLAN["mla_k"], PLAN["mla_v"]

        def mla_in_pe(pe):
            stream_pe(pe, "mla_q", lambda m, k: cqn[:, k, :], SEQ)
            pe.wait_ge(*S.at("norm_dve", "done", 12))
            stream_pe(pe, "mla_k", lambda m, k: ckvn[:, k, :], SEQ)
            slot = MV.slab0 % SLOTS
            pe.wait_ge(weights_in[slot], 16 * (MV.slab0 // SLOTS + 1))
            for m in range(2):
                b = MV.product0 + m
                pe.wait_ge(bank_free[b % BANKS], b // BANKS + 1)
                for k in range(2):
                    mm = pe.matmul(ps[b % BANKS][:, :], ckvn[:, k, m * P:(m + 1) * P], ring[:, slot, k * 512:(k + 1) * 512],
                                   start=(k == 0), stop=(k == 1))
                mm.then_inc(product_done, 1)
            rown_pe(pe, 3, lambda k: (sq_q if k < 8 else sq_k)[0:QK, k % 8, :], 16, 1, SEQ, 16)
            for i in range(8):
                if i == 0:
                    pe.wait_ge(*S.at("mla_dve", "gained"))
                    pe.wait_ge(*S.at("rown_dve", "mean", 3))
                if i >= 2:
                    pe.wait_ge(*S.at("mla_dve", f"rope{i - 2}"))
                S.inc(pe.matmul(ps[4 + i % 2][0:QK, :], cn("rot")[0:QK, :], qk16[0:QK, 2 * i:2 * i + 2, :].rearrange("p a b -> p (a b)"),
                                start=True, stop=True), "mla_pe", f"rot{i}")

        def mla_in_act(act):
            inc = lambda ins, step=None: S.inc(ins, "mla_act", step)
            for h in range(8):
                un = Unit(MQ, 1, h, 0, 0)
                un.ready(act)
                inc(act.activation(sq_q[0:QK, h, :], un.bank()[0:QK, 0:SEQ], ACT.Square))
                un.free(act.activation(qk16[0:QK, h, :], un.bank()[0:QK, 0:SEQ], ACT.Identity, scale=pm("q_norm")[0:QK, :]))
            for h in range(8):
                Unit(MK, 1, h, 0, 0).was_read(act)
                inc(act.activation(sq_k[0:QK, h, :], qk16[0:QK, 8 + h, :], ACT.Square), "ksq" if h == 7 else None)
            for c in range(2):
                un = Unit(MV, 1, c, 0, 0)
                un.ready(act)
                un.free(act.activation(vtk[:, c, :], un.bank(), ACT.Copy))

        def mla_in_dve(dve):
            inc = lambda ins, step=None: S.inc(ins, "mla_dve", step)
            own = lambda: S.own(dve, "mla_dve")
            for h in range(8):
                un = Unit(MK, 1, h, 0, 0)
                un.ready(dve)
                un.free(dve.tensor_tensor(qk16[0:QK, 8 + h, :], un.bank()[0:QK, 0:SEQ], cqT[0:QK, 3, :], ALU.add))
            dve.wait_ge(*S.at("mla_act", "ksq"))
            inc(dve.tensor_scalar(qk16[0:QK, 8:16, :], qk16[0:QK, 8:16, :], pm("k_norm")[0:QK, :], None, ALU.mult), "gained")

        def mla_rope_dve(dve):
            inc = lambda ins, step=None: S.inc(ins, "mla_dve", step)
            own = lambda: S.own(dve, "mla_dve")
            dve.wait_ge(S.sem("mla_rows_in"), 32)
            dve.wait_ge(*S.at("rope_act"))
            both = lambda v: v.unsqueeze(1).broadcast_to([QK, 2, SEQ])
            for i in range(8):
                x = qk16[0:QK, 2 * i:2 * i + 2, :]
                tmp = prob[i % 2][0:QK, :].rearrange("p (a b) -> p a b", b=SEQ)
                dve.wait_ge(*S.at("mla_pe", f"rot{i}"))
                inc(dve.tensor_tensor(tmp, ps[4 + i % 2][0:QK, :].rearrange("p (a b) -> p a b", b=SEQ), both(trig[0:QK, 2, :]), ALU.mult), f"rope{i}")
                inc(dve.tensor_tensor(x, x, both(trig[0:QK, 3, :]), ALU.mult))
                own()
                inc(dve.tensor_tensor(x, x, tmp, ALU.add))
                own()
                inc(dve.tensor_tensor(x, x, (sq_q if i < 4 else sq_k)[0:QK, 2 * i % 8:2 * i % 8 + 2, :], ALU.mult), "heads" if i == 7 else None)
            own()

        def mla_pool(pool):
            pool.wait_ge(*S.at("rown_dve", "rows", 3))
            pool.dma_start(scr_q, rrow[:, 0, 0:SEQ]).then_inc(S.sem("mla_rows_out"), 16)
            pool.wait_ge(S.sem("mla_rows_out"), 16)
            pool.dma_start(sq_q, on_all(scr_q, 0, (SEQ, 8), (1, SEQ))).then_inc(S.sem("mla_rows_in"), 16)
            pool.dma_start(sq_k, on_all(scr_q, 8 * SEQ, (SEQ, 8), (1, SEQ))).then_inc(S.sem("mla_rows_in"), 16)

        def memq_act(act):
            rown_act(act, 4, [(qmT, sq_k[:, 0:4, :]), (kmem, sq_k[:, 4:8, :])], SEQ, 8)

        def memq_dve(dve):
            dve.wait_ge(S.sem("mem_rows_in"), 16)
            for h in range(4):
                for x, gain, off in ((qmT, "mq_norm", 0), (kmem, "mk_norm", 4)):
                    S.inc(dve.scalar_tensor_tensor(out=x[:, h, :], in0=x[:, h, :], scalar=pm(gain), in1=sq_q[:, off + h, :],
                                                   op0=ALU.mult, op1=ALU.mult), "memq_dve")
            S.own(dve, "memq_dve")

        def memq_pool(pool):
            pool.wait_ge(*S.at("rown_dve", "rows", 4))
            pool.dma_start(scr_c, rrow[0:8, 0, 0:SEQ]).then_inc(S.sem("mem_rows_out"), 16)
            pool.wait_ge(S.sem("mem_rows_out"), 16)
            pool.dma_start(sq_q, on_all(scr_c, 0, (SEQ, 8), (1, SEQ))).then_inc(S.sem("mem_rows_in"), 16)

        def attention(eng, engine, kind):
            causal = kind == "mla"
            H = MLA_H if causal else MEM_H
            scale = (QK if causal else P) ** -0.5
            rows = QK if causal else P
            inc = lambda ins, step=None: S.inc(ins, f"{kind}att_{engine}", step)
            wait = lambda other, step: eng.wait_ge(*S.at(f"{kind}att_{other}", step))
            own = lambda: S.own(eng, f"{kind}att_{engine}")
            q = (lambda h: qk16[0:rows, h, :]) if causal else (lambda h: qmT[:, h, :])
            k = (lambda h: qk16[0:rows, 8 + h, :]) if causal else (lambda h: kmem[:, h, :])
            v = (lambda h, c: vtk[:, c, 64 * h:64 * h + 64]) if causal else (lambda h, c: vmem[:, c, P * h:P * h + P])
            part = ((0, P), (P, 3 * P)) if causal else ((0, 2 * P), (2 * P, 4 * P))
            end = part[1][1]

            def out(h):
                return (ps[7][64 * (h % 2):64 * (h % 2) + 64, 0:SEQ], yT[1][64 * (h % 2):64 * (h % 2) + 64, h // 2, :]) if causal \
                    else (ps[7][:, 0:SEQ], yT[2][:, h, :])

            if engine == "pe":
                def scores(h):
                    if h >= 2:
                        wait(*(("dve", f"read{h - 2}") if causal else ("act", f"e{h - 2}")))
                    for i, (lo, hi) in enumerate(part):
                        mm = eng.matmul(ps[4 + h % 2][:, lo:hi], q(h)[:, i * P:(i + 1) * P], k(h)[:, 0:hi - lo], start=True, stop=True)
                    inc(mm, f"s{h}")
                scores(0)
                for h in range(H):
                    if h + 1 < H:
                        scores(h + 1)
                    wait("dve", f"p{h}")
                    if h >= 1:
                        wait("act", f"pt{h - 1}")
                    for i in range(2):
                        for kt in range(2):
                            if causal and kt > i:
                                continue
                            mm = eng.transpose(ps[6][:, kt * SEQ + i * P:kt * SEQ + (i + 1) * P],
                                               prob[h % 2][:, part[i][0] + kt * P:part[i][0] + (kt + 1) * P], ident)
                    inc(mm, f"t{h}")
                    wait("act", f"pt{h}")
                    if h >= 1:
                        wait("act", f"o{h - 1}")
                    o, _ = out(h)
                    eng.matmul(o, v(h, 0), probT[h % 2][:, 0:SEQ], start=True, stop=False)
                    if causal:
                        mm = eng.matmul(o[:, P:SEQ], v(h, 1), probT[h % 2][:, SEQ + P:2 * SEQ], start=False, stop=True)
                    else:
                        mm = eng.matmul(o, v(h, 1), probT[h % 2][:, SEQ:2 * SEQ], start=False, stop=True)
                    inc(mm, f"pv{h}")
            if engine == "dve":
                for h in range(H + 1):
                    if h < H:
                        st = soft[:, h % 2]
                        wait("pe", f"s{h}")
                        if h >= 2:
                            wait("pe", f"t{h - 2}")
                        if causal:
                            inc(eng.tensor_tensor(prob[h % 2][:, 0:end], ps[4 + h % 2][:, 0:end], cn("score_mask"), ALU.add), f"read{h}")
                            own()
                            for i, (lo, hi) in enumerate(part):
                                inc(eng.tensor_reduce(st[:, 0, i:i + 1], prob[h % 2][:, lo:hi], AX_X, ALU.max))
                        else:
                            inc(eng.tensor_reduce(st[:, 0, :], ps[4 + h % 2].rearrange("p (a b) -> p a b", b=SEQ), AX_X, ALU.max))
                        own()
                        inc(eng.tensor_scalar(st[:, 1, :], st[:, 0, :], -scale, None, ALU.mult), f"n{h}")
                    if h >= 1:
                        g = h - 1
                        st = soft[:, g % 2]
                        wait("act", f"e{g}")
                        inc(eng.reciprocal(st[:, 3, :], st[:, 2, :]))
                        own()
                        for i, (lo, hi) in enumerate(part):
                            inc(eng.tensor_scalar(prob[g % 2][:, lo:hi], prob[g % 2][:, lo:hi], st[:, 3, i:i + 1], None, ALU.mult), f"p{g}" if i else None)
            if engine == "act":
                def finish(g):
                    wait("pe", f"t{g}")
                    if causal:
                        inc(eng.activation(probT[g % 2][:, 0:SEQ], ps[6][:, 0:SEQ], ACT.Copy))
                        inc(eng.activation(probT[g % 2][:, SEQ + P:2 * SEQ], ps[6][:, SEQ + P:2 * SEQ], ACT.Copy), f"pt{g}")
                    else:
                        inc(eng.activation(probT[g % 2], ps[6], ACT.Copy), f"pt{g}")
                    wait("pe", f"pv{g}")
                    o, dst = out(g)
                    inc(eng.activation(dst, o, ACT.Copy), f"o{g}")
                for h in range(H + 1):
                    if h < H:
                        st = soft[:, h % 2]
                        wait("dve", f"n{h}")
                        for i, (lo, hi) in enumerate(part):
                            src = prob[h % 2] if causal else ps[4 + h % 2]
                            inc(eng.activation(prob[h % 2][:, lo:hi], src[:, lo:hi], ACT.Exp, bias=st[:, 1, i:i + 1], scale=scale,
                                               accum_out=st[:, 2, i:i + 1]), f"e{h}" if i else None)
                    if h >= 1:
                        finish(h - 1)

        merged = area(u_at, 8, SEQ)

        def branches_dve(dve):
            t1 = [mix2[:, i * SEQ:(i + 1) * SEQ] for i in range(2)]

            def body(un):
                c = un.j
                for m in range(3):
                    un.ready(dve, m)
                    if m and c:
                        S.own(dve, "merge_dve")
                    un.free(dve.tensor_tensor(merged[:, c, :] if m == 0 else t1[m - 1], un.bank(m)[:, 0:SEQ], gat[:, 8 * m + c, :], ALU.mult), m)
                un.was_read(dve, 0)
                un.was_read(dve, 1)
                S.inc(dve.tensor_tensor(merged[:, c, :], merged[:, c, :], t1[0], ALU.add), "merge_dve")
                un.was_read(dve, 2)
                S.own(dve, "merge_dve")
                S.inc(dve.tensor_tensor(merged[:, c, :], merged[:, c, :], t1[1], ALU.add), "merge_dve")
            for j in range(8):
                body(Unit(PLAN["branches"], 3, j, 0, 0))

        def mix_out_dve(dve):
            each_product(dve, "mix_out", 1, lambda un: (
                un.ready(dve), un.free(dve.tensor_tensor(h2[:, un.u, :], un.bank()[:, 0:SEQ], h2[:, un.u, :], ALU.add))))

        block = ctx.enter_context(nc.Block())
        H1 = lambda k: hs[:, k, :]
        A1 = lambda k: a[:, k, :]
        M1 = lambda k: mix[:, k, :]
        H2 = lambda k: h2[:, k, :]
        A2 = lambda k: a[:, k, 0:SEQ]
        gain = lambda name, base=0: (lambda k: pm(name, base + k))

        @block.sync
        def _(sp):
            sp.dma_start(Cn[:, :], consts).then_inc(S.sem("small_in"), 16)
            sp.dma_start(Pm[:, :], params).then_inc(S.sem("small_in"), 16)
            word = 0
            for n, ph in enumerate(SLAB_OF):
                size = ph.blocks * P
                if n - SLOTS in SPLIT_AT:
                    sp.wait_ge(lo_done, SPLIT_AT[n - SLOTS] + 1)
                elif n >= SLOTS:
                    sp.wait_ge(product_done, done_value(n - SLOTS))
                sp.dma_start(ring[:, n % SLOTS, 0:size],
                             stream[word:word + P * size].rearrange("(p c) -> p c", p=P)).then_inc(weights_in[n % SLOTS], 16)
                word += P * size
            phase_read(sp, "down3")
            sp.dma_start(out_t.rearrange("(k p) t -> p k t", p=P), h2).then_inc(S.sem("out_stored"), 16)
            sp.wait_ge(S.sem("out_stored"), 16)

        @block.gpsimd
        def _(pool):
            pool.dma_start(hs[:, :, META:T], x_t.rearrange("(k p) t -> p k t", p=P)).then_inc(S.sem("x_in"), 16)
            pool.dma_start(hs[:, :, 0:META], meta_t.rearrange("(k p) t -> p k t", p=P)).then_inc(S.sem("x_in"), 16)
            scan_pool(pool)
            gate_pool(pool)
            conv_up_pool(pool, 0)
            ml_pool(pool)
            ml_norm_pool(pool)
            conv_up_pool(pool, 1)
            mem_pool(pool)
            up_pool2(pool, "up2")
            phase_read(pool, "down2")
            sg_pool(pool)
            rope_pool(pool)
            mla_pool(pool)
            memq_pool(pool)
            up_pool2(pool, "up3")

        @block.scalar
        def _(act):
            act.wait_ge(S.sem("small_in"), 32)
            act.wait_ge(S.sem("x_in"), 32)
            norm_act(act, 0, hs[:, :, :], 8, T)
            split_act(act, 0, a, A_HI, 8, T, norm=0)
            prepare(act, "hi", "gdn_qkv")
            rows_act(act)
            qkv_act(act)
            act.wait_ge(*S.at("qkv_act", turn=31 + CONV_AHEAD))
            rown_act(act, 0, [(qkv[:, 0:16, :], sqh)], T, 16)
            scan_act(act)
            scan_done(act)
            prepare(act, "hi", "gdn_z")
            split_act(act, 1, a, A_HI, 8, T)
            rown_act(act, 1, [(qkv[:, 16:32, :], osq)], T, 16)
            gate_act(act)
            act.wait_ge(*S.at("gate_dve", turn=15 + 4))
            split_act(act, 2, qkv[:, 16:32, :], O_HI, 16, T)
            evac_mix_act(act, "gdn_out")
            for layer in range(2):
                if layer:
                    norm_act(act, 4, hs[:, :, :], 8, T)
                    split_act(act, 4, a, A_HI, 8, T, norm=4)
                    ml_rows_act(act)
                    ml_in_act(act)
                    ml_act(act)
                    act.wait_ge(*S.at("ml_dve"))
                    rown_act(act, 2, [(hT, hsq)], T, ML_H)
                    act.wait_ge(*S.at("mln_dve"))
                    split_act(act, 5, hT, ML_HI, 8, T)
                    evac_mix_act(act, "ml_out")
                mix_was_read(act, "gdn_out" if layer == 0 else "ml_out")
                norm_act(act, 1 + 4 * layer, mix[:, :, :], 8, T)
                act.wait_ge(*S.at("norm_dve", "done", 1 + 4 * layer))
                norm_act(act, 2 + 4 * layer, hs[:, :, :], 8, T)
                split_act(act, 3 + 3 * layer, a, A_HI, 8, T, norm=2 + 4 * layer)
                act.wait_ge(*S.at("ffn_zero", turn=layer))
                conv_up_act(act, layer)
                evac_mix_act(act, f"down{layer}")
                mix_was_read(act, f"down{layer}")
                norm_act(act, 3 + 4 * layer, mix[:, :, :], 8, T)
                act.wait_ge(*S.at("norm_dve", "done", 3 + 4 * layer))
            mem_act(act)
            prepare(act, "hi", "up2")
            norm_act(act, 9, h2, 8, SEQ)
            split_act(act, 7, a, A_HI, 8, SEQ, norm=9)
            up_act(act, "up2")
            each_product(act, "down2", 1, nothing, split="hi")
            phase_read(act, "down2")
            norm_act(act, 10, h2, 8, SEQ)
            split_act(act, 8, a, A_HI, 8, SEQ, norm=10)
            in_act(act)
            sg_act(act)
            norm_act(act, 11, cqT[:, 0:3, :], 3, SEQ)
            norm_act(act, 12, ckvT, 2, SEQ)
            rope_act(act)
            mla_in_act(act)
            rown_act(act, 3, [], SEQ, 16)
            attention(act, "act", "mla")
            memq_act(act)
            attention(act, "act", "mem")
            prepare(act, "hi", "up3")
            phase_read(act, "mix_out")
            norm_act(act, 13, h2, 8, SEQ)
            split_act(act, 9, a, A_HI, 8, SEQ, norm=13)
            up_act(act, "up3")
            each_product(act, "down3", 1, nothing, split="hi")

        @block.vector
        def _(dve):
            for i in range(BANKS):
                dve.memset(rs[:, 0, 4 * i:4 * i + 4], 0.0).then_inc(bank_free[i], 1)
            dve.memset(raw_c[:, :, 0:3], 0.0).then_inc(S.sem("qkv_dve"), CONV_AHEAD * 3)
            dve.memset(rs[:, 0, 16:20], 0.0).then_inc(S.sem("qkv_act"), CONV_AHEAD)
            dve.memset(rs[:, 0, 20:24], 0.0).then_inc(S.sem("up_dve"), 2 * 4)
            dve.memset(rs[:, 0, 32:36], 0.0).then_inc(S.sem("gate_dve"), 4 * 2)
            dve.memset(rs[:, 0, 36:40], 0.0).then_inc(S.sem("hid_pool"), 4 * 2)
            dve.memset(rs[:, 0, 24:28], 0.0).then_inc(S.sem("up_act"), 2)
            dve.memset(rs[:, 0, 28:32], 0.0).then_inc(S.sem("up_pool"), 2 * 3)
            dve.memset(rs[:, 1, :], 0.0).then_inc(S.sem("group_out"), 1)
            for i in range(BANKS):
                dve.wait_ge(bank_free[i], 1)
            dve.wait_ge(S.sem("up_pool"), 6)
            dve.wait_ge(S.sem("group_out"), 1)
            dve.wait_ge(S.sem("qkv_act"), CONV_AHEAD)
            dve.wait_ge(S.sem("gate_dve"), 8)
            dve.wait_ge(S.sem("hid_pool"), 8)
            dve.wait_ge(S.sem("up_act"), 2)
            dve.wait_ge(S.sem("up_dve"), 8)
            dve.wait_ge(S.sem("small_in"), 32)
            dve.wait_ge(S.sem("x_in"), 32)
            norm_dve(dve, 0, D, T, H1, gain("norm_w", 0), A1, 8)
            split_dve(dve, 0, a, A_HI, A_LO, 8, T)
            prepare(dve, "lo", "gdn_qkv")
            rows_dve(dve)
            qkv_dve(dve)
            cols_dve(dve)
            rown_dve(dve, 0, 1.0, EPS, T, 16, cn("l2_scale")[0:16, :])
            dve.wait_ge(*S.at("cols_dve"))
            scan_dve(dve)
            prepare(dve, "lo", "gdn_z")
            split_dve(dve, 1, a, A_HI, A_LO, 8, T)
            rown_dve(dve, 1, 1.0 / P, EPS, T, 16, 1.0)
            gate_dve(dve)
            split_dve(dve, 2, qkv[:, 16:32, :], O_HI, O_LO, 16, T)
            each_product(dve, "gdn_out", 1, nothing, split="lo")
            for layer in range(2):
                if layer:
                    norm_dve(dve, 4, D, T, H1, gain("norm_w", 4 * DB), A1, 8)
                    split_dve(dve, 4, a, A_HI, A_LO, 8, T)
                    ml_rows_dve(dve)
                    each_product(dve, "ml_in", 1, nothing, split="lo")
                    ml_cols_dve(dve)
                    ml_dve(dve)
                    rown_dve(dve, 2, 1.0 / 256, EPS, T, ML_H, 1.0)
                    ml_norm_dve(dve)
                    split_dve(dve, 5, hT, ML_HI, ML_LO, 8, T)
                    each_product(dve, "ml_out", 1, nothing, split="lo")
                mix_was_read(dve, "gdn_out" if layer == 0 else "ml_out")
                norm_dve(dve, 1 + 4 * layer, D, T, M1, gain("norm_w", (4 * layer + 1) * DB), M1, 8, add=(hs[:, :, :], mix[:, :, :]))
                dve.wait_ge(*S.at("norm_dve", "done", 1 + 4 * layer))
                S.begin("ffn_zero")
                for i in range(2):
                    S.inc(dve.memset(raw[i][:, :, 0:2], 0.0), "ffn_zero")
                norm_dve(dve, 2 + 4 * layer, D, T, H1, gain("norm_w", (4 * layer + 2) * DB), A1, 8)
                split_dve(dve, 3 + 3 * layer, a, A_HI, A_LO, 8, T)
                dve.wait_ge(*S.at("ffn_zero", turn=layer))
                conv_up_dve(dve, layer)
                each_product(dve, f"down{layer}", 1, nothing, split="lo")
                mix_was_read(dve, f"down{layer}")
                norm_dve(dve, 3 + 4 * layer, D, T, M1, gain("norm_w", (4 * layer + 3) * DB), M1, 8, add=(hs[:, :, :], mix[:, :, :]))
                dve.wait_ge(*S.at("norm_dve", "done", 3 + 4 * layer))
            dve.wait_ge(S.sem("mem_in"), 16)
            norm_dve(dve, 8, D, SEQ, lambda k: mem_sb[:, k, :], gain("mem_norm"), lambda k: memn[:, k, :], 8)
            prepare(dve, "lo", "up2")
            norm_dve(dve, 9, D, SEQ, H2, gain("ffn1_norm"), A2, 8)
            split_dve(dve, 7, a, A_HI, A_LO, 8, SEQ)
            up_dve(dve, "up2")
            down_dve(dve, "down2")
            phase_read(dve, "down2")
            norm_dve(dve, 10, D, SEQ, H2, gain("mix_norm"), A2, 8)
            split_dve(dve, 8, a, A_HI, A_LO, 8, SEQ)
            for name in ("in_uv", "in_cq_kr", "in_qm", "in_ckv", "in_gates"):
                each_product(dve, name, 1, nothing, split="lo")
            phase_read(dve, "in_uv")
            sg_dve(dve)
            phase_read(dve, "in_ckv")
            norm_dve(dve, 11, 384, SEQ, lambda k: cqT[:, k, :], gain("cq_norm"), lambda k: cqn[:, k, :], 3)
            norm_dve(dve, 12, 256, SEQ, lambda k: ckvT[:, k, :], gain("ckv_norm"), lambda k: ckvn[:, k, :], 2)
            phase_read(dve, "in_gates")
            rope_dve(dve)
            mla_in_dve(dve)
            rown_dve(dve, 3, 1.0 / QK, EPS, SEQ, 16, 1.0)
            mla_rope_dve(dve)
            attention(dve, "dve", "mla")
            rown_dve(dve, 4, 1.0 / P, EPS, SEQ, 8, 1.0)
            memq_dve(dve)
            attention(dve, "dve", "mem")
            branches_dve(dve)
            mix_out_dve(dve)
            prepare(dve, "lo", "up3")
            phase_read(dve, "mix_out")
            norm_dve(dve, 13, D, SEQ, H2, gain("ffn2_norm"), A2, 8)
            split_dve(dve, 9, a, A_HI, A_LO, 8, SEQ)
            up_dve(dve, "up3")
            down_dve(dve, "down3")

        @block.tensor
        def _(pe):
            from_a = lambda m, k: a[:, k, :]
            a_parts = lambda m, k: (A_HI[:, k, :], A_LO[:, k, :])
            a2_parts = lambda m, k: (A_HI[:, k, 0:SEQ], A_LO[:, k, 0:SEQ])
            hid2_parts = lambda m, k: (hid2_hi[:, k, :], hid2_lo[:, k, :])
            norm_pe(pe, 0, 8, T)
            pe.wait_ge(*S.at("norm_dve", "done", 0))
            stream_pe(pe, "gdn_ba", from_a, T)
            pe.wait_ge(*S.at("x_lo", turn=0))
            stream_pe(pe, "gdn_qkv", a_parts, T)
            rows_pe(pe)
            rown_pe(pe, 0, lambda k: sqh[:, k, :], 16, 1, T, 16)
            scan_pe(pe)
            pe.wait_ge(S.sem("group_out"), GROUPS + 1)
            rown_pe(pe, 1, lambda k: osq[:, k, :], 16, 1, T, 16)
            pe.wait_ge(*S.at("x_lo", turn=1))
            stream_pe(pe, "gdn_z", a_parts, T)
            pe.wait_ge(*S.at("x_lo", turn=2))
            stream_pe(pe, "gdn_out", lambda m, k: (O_HI[:, k, :], O_LO[:, k, :]), T)
            for layer in range(2):
                if layer:
                    norm_pe(pe, 4, 8, T)
                    pe.wait_ge(*S.at("norm_dve", "done", 4))
                    stream_pe(pe, "ml_gates", from_a, T)
                    pe.wait_ge(*S.at("x_lo", turn=4))
                    stream_pe(pe, "ml_in", a_parts, T)
                    ml_rows_pe(pe)
                    pe.wait_ge(*S.at("mcol_dve"))
                    ml_pe(pe)
                    rown_pe(pe, 2, lambda k: hsq[:, k, :], 8, 2, T, ML_H)
                    pe.wait_ge(*S.at("x_lo", turn=5))
                    stream_pe(pe, "ml_out", lambda m, k: (ML_HI[:, k, :], ML_LO[:, k, :]), T)
                norm_pe(pe, 1 + 4 * layer, 8, T)
                norm_pe(pe, 2 + 4 * layer, 8, T)
                pe.wait_ge(*S.at("x_lo", turn=3 + 3 * layer))
                stream_pe(pe, f"up{layer}", a_parts, T)
                pe.wait_ge(*S.at("up_pool", turn=22 * layer + 21 + 2))
                stream_pe(pe, f"down{layer}", lambda m, k: (hid_hi[:, k, :], hid_lo[:, k, :]), T)
                norm_pe(pe, 3 + 4 * layer, 8, T)
            mem_pe(pe)
            norm_pe(pe, 9, 8, SEQ)
            pe.wait_ge(*S.at("x_lo", turn=7))
            stream_pe(pe, "up2", a2_parts, SEQ)
            pe.wait_ge(*S.at("hid_pool", turn=FB - 1 + 4))
            stream_pe(pe, "down2", hid2_parts, SEQ)
            norm_pe(pe, 10, 8, SEQ)
            pe.wait_ge(*S.at("x_lo", turn=8))
            for name in ("in_uv", "in_cq_kr", "in_qm", "in_ckv", "in_gates"):
                stream_pe(pe, name, a2_parts, SEQ)
            phase_read(pe, "in_uv")
            sg_pe(pe)
            pe.wait_ge(*S.at("sg_dve", "y3"))
            norm_pe(pe, 11, 3, SEQ)
            norm_pe(pe, 12, 2, SEQ)
            pe.wait_ge(*S.at("norm_dve", "done", 11))
            mla_in_pe(pe)
            pe.wait_ge(*S.at("mla_dve", "heads"))
            phase_read(pe, "mla_k")
            phase_read(pe, "mla_v")
            attention(pe, "pe", "mla")
            rown_pe(pe, 4, lambda k: sq_k[:, k, :], 8, 1, SEQ, 8)
            pe.wait_ge(*S.at("memq_dve"))
            attention(pe, "pe", "mem")
            pe.wait_ge(*S.at("mlaatt_act", "o7"))
            pe.wait_ge(*S.at("mematt_act", "o3"))
            stream_pe(pe, "branches", lambda m, k: yT[m % 3][:, k, :], SEQ)
            pe.wait_ge(*S.at("merge_dve"))
            stream_pe(pe, "mix_out", lambda m, k: merged[:, k, :], SEQ)
            norm_pe(pe, 13, 8, SEQ)
            pe.wait_ge(*S.at("x_lo", turn=9))
            stream_pe(pe, "up3", a2_parts, SEQ)
            pe.wait_ge(*S.at("hid_pool", turn=2 * FB - 1 + 4))
            stream_pe(pe, "down3", hid2_parts, SEQ)

    return S.seen


def stream_layout(w):
    parts = []

    def cat(columns_, kb, per_slab):
        blocks = np.stack([c.reshape(kb, P, P) for c in columns_])
        m = blocks.shape[0]
        blocks = blocks.reshape(m // per_slab, per_slab * kb, P, P).transpose(0, 2, 1, 3)
        parts.append(np.ascontiguousarray(blocks).reshape(-1))

    def split(x):
        return [x[:, i:i + P] for i in range(0, x.shape[1], P)]

    def pad(x, places):
        out = np.zeros((x.shape[0], P), x.dtype)
        for at, src in places:
            out[:, at:at + src.shape[1]] = src
        return out

    def ffn(up, down):
        g, u = split(up[:, :FF]), split(up[:, FF:])
        cat([b for pair in zip(g, u) for b in pair], DB, 2)
        cat([c[r:r + FF // 2] for c in split(down) for r in (0, FF // 2)], FB // 2, 1)

    gi = w["gdn_w_in"][0]
    qkv = 2 * HQ * P + HV * P
    cat([pad(gi, [(0, gi[:, qkv + HV * P:qkv + HV * P + HV]), (32, gi[:, qkv + HV * P + HV:])])], DB, 1)
    cat(split(gi[:, :qkv]), DB, 2)
    cat(split(gi[:, qkv:qkv + HV * P]), DB, 2)
    cat(split(w["gdn_w_out"][0]), HV, 1)
    ffn(w["ffn_w_up"][0], w["ffn_w_down"][0])
    mi = w["ml_w_in"][0]
    o4 = 2 * ML_H * P + 2 * ML_H * 256
    cat([pad(mi, [(0, mi[:, o4:o4 + ML_H]), (32, mi[:, o4 + ML_H:])])], DB, 1)
    cat(split(mi[:, :o4]), DB, 2)
    cat(split(w["ml_w_out"][0]), DB, 2)
    ffn(w["ffn_w_up"][1], w["ffn_w_down"][1])
    mk = w["mem_w_kv_2"][0]
    cat(split(mk[:, :512]), DB, 2)
    parts.append(np.ascontiguousarray(mk[:, 512:].reshape(DB, P, 2, SEQ).transpose(2, 1, 0, 3)).reshape(-1))
    ffn(w["ffn1_w_gu_2"][0], w["ffn1_w_down_2"][0])
    wi = w["w_in_2"][0]
    cat(split(wi[:, 0:1024]), DB, 2)
    cat(split(wi[:, 1024:1408]) + [pad(wi, [(NOPE, wi[:, 1664:1696])])], DB, 2)
    cat(split(wi[:, 1696:2208]), DB, 2)
    cat(split(wi[:, 1408:1664]), DB, 2)
    cat(split(wi[:, 2208:]), DB, 2)
    uq, ukv = w["mla_w_uq_2"][0], w["mla_w_ukv_2"][0]
    cat([pad(uq, [(0, uq[:, QK * h:QK * (h + 1)])]) for h in range(MLA_H)], 3, 4)
    kpart = np.stack([pad(ukv, [(0, ukv[:, P * h:P * h + NOPE])]).reshape(2, P, P) for h in range(MLA_H)])
    kpart = kpart.reshape(16, P, P).transpose(1, 0, 2).reshape(P, 16 * P)
    vpart = ukv.reshape(2, P, MLA_H, 2, NOPE)[:, :, :, 1, :].reshape(2, P, 512).transpose(1, 0, 2).reshape(P, 1024)
    parts += [kpart.reshape(-1), vpart.reshape(-1)]
    br = [split(w[n][0]) for n in ("w_branch_a_2", "w_branch_b_2", "w_branch_c_2")]
    cat([b[c] for c in range(DB) for b in br], 4, 3)
    cat(split(w["w_out_2"][0]), DB, 2)
    ffn(w["ffn2_w_gu_2"][0], w["ffn2_w_down_2"][0])
    out = np.concatenate(parts)
    assert out.size == STREAM_WORDS, (out.size, STREAM_WORDS)
    return out


def const_layout():
    c = np.zeros((P, N_CONST), np.float32)
    i = np.arange(P)

    def put(name, v):
        at, n = CONST_COLS[name]
        c[:v.shape[0], at:at + n] = v

    put("ident", np.eye(P))
    put("ones", np.ones((P, P)))
    put("causal", np.where(np.arange(T)[None] >= i[:, None], 0.0, NEG))
    levels = []
    for l in range(7):
        s = 1 << l
        levels.append(((i[None] // s) % 2 == 1) & (i[None] // s == i[:, None] // s + 1))
    put("level", np.stack(levels, 1).reshape(P, 7 * P))
    rot = np.zeros((QK, QK))
    for r in range(ROPE // 2):
        rot[NOPE + ROPE // 2 + r, NOPE + r] = -1.0
        rot[NOPE + r, NOPE + ROPE // 2 + r] = 1.0
    put("rot", rot)
    half = ROPE // 2
    inv = (np.float32(10000.0) ** (-np.arange(half, dtype=np.float32) / np.float32(half))).astype(np.float32)
    f = np.zeros((QK, 1))
    f[NOPE:NOPE + half, 0] = inv
    f[NOPE + half:, 0] = inv
    put("inv_freq", f)
    row_of = np.zeros((P, 31))
    row_of[:, 15] = 1.0
    put("row_of", row_of)
    tri = np.where(i[None] <= i[:, None], 0.0, NEG)
    put("score_mask", np.concatenate([tri, np.zeros((P, P)), tri], 1))
    put("tri", (i[None] >= i[:, None]) * 1.0)
    l2 = np.ones((P, 1))
    l2[:HQ] = P ** -0.5
    put("l2_scale", l2)
    return c


def param_layout(w):
    p = np.zeros((P, N_PARAM), np.float32)

    def put(name, v):
        at, n = PARAM_COLS[name]
        assert v.shape[1] == n, (name, v.shape, n)
        p[:v.shape[0], at:at + n] = v

    def cols_of(v):
        return v.reshape(-1, P).T

    put("norm_w", cols_of(w["norm_w"].reshape(-1)))
    put("gdn_conv", w["gdn_conv_w"][0].reshape(4, 32, P).transpose(2, 1, 0).reshape(P, -1))
    put("ffn_conv", w["ffn_conv_w"].reshape(2, 3, 2, FB, P).transpose(4, 0, 3, 2, 1).reshape(P, -1))
    put("ffn_bias", w["ffn_conv_b"].reshape(2, 2, FB, P).transpose(3, 0, 2, 1).reshape(P, -1))
    put("gdn_norm", w["gdn_norm_w"][0][:, None])
    put("a_log", w["gdn_a_log"][0][:, None])
    put("dt_bias", w["gdn_dt_bias"][0][:, None])
    put("ml_gate_i", w["ml_gate_b"][0][:ML_H, None])
    put("ml_gate_f", w["ml_gate_b"][0][ML_H:, None])
    put("ml_norm", cols_of(w["ml_norm_w"][0]))
    for name, src in (("ffn1_norm", "ffn1_norm_2"), ("mix_norm", "mix_norm_2"), ("ffn2_norm", "ffn2_norm_2"), ("mem_norm", "mem_norm_2"),
                      ("b_gate", "b_gate_2"), ("sg_g", "sg_ln_g_2"), ("sg_b", "sg_ln_b_2"), ("cq_norm", "mla_cq_norm_2"),
                      ("ckv_norm", "mla_ckv_norm_2"), ("mq_norm", "mem_q_norm_2"), ("mk_norm", "mem_k_norm_2")):
        put(name, cols_of(w[src][0]))
    put("q_norm", w["mla_q_norm_2"][0][:, None])
    put("k_norm", w["mla_k_norm_2"][0][:, None])
    return p


def layout(inputs):
    w = {k: np.asarray(v) for k, v in inputs.items()}
    return {
        "x_t": np.ascontiguousarray(w["x"][0].T),
        "meta_t": np.ascontiguousarray(w["meta_tokens"].T),
        "mem_t": np.ascontiguousarray(w["mem_2"][0].T),
        "positions": np.ascontiguousarray(w["positions_2"]),
        "stream": stream_layout(w),
        "consts": const_layout(),
        "params": param_layout(w),
        "sg_w_t": np.ascontiguousarray(w["sg_w_2"][0].transpose(2, 0, 1)),
        "sg_bias": np.ascontiguousarray(w["sg_b_2"][0]),
    }


def kernel(**inputs):
    import concourse.bacc as bacc
    from concourse.bass_utils import run_bass_kernel_spmd

    arrays = layout(inputs)
    counts = {}
    for _ in range(2):
        nc = bacc.Bacc("TRN2", target_bir_lowering=False, num_devices=1)
        aps = {n: nc.dram_tensor(f"in_{n}", v.shape, mybir.dt.from_np(v.dtype), kind="ExternalInput").ap() for n, v in arrays.items()}
        out = nc.dram_tensor("out_t", (D, SEQ), F32, kind="ExternalOutput").ap()
        counts = program(nc, out_t=out, counts=counts, **aps)
    r = run_bass_kernel_spmd(nc, [{f"in_{n}": v for n, v in arrays.items()}], core_ids=[0])
    return np.ascontiguousarray(r.results[0]["out_t"].T)[None]
```

```python
from contextlib import ExitStack

import numpy as np

import concourse.bass as bass
from concourse import mybir

F32 = mybir.dt.float32
F32R = mybir.dt.float32r
I32 = mybir.dt.int32
ALU = mybir.AluOpType
ACT = mybir.ActivationFunctionType
AX_X = mybir.AxisListType.X

P = 128
D = 1024
DB = D // P
SEQ = 256
META = 16
T = META + SEQ
TILES = [(0, META), (META, P), (META + P, P)]
HQ, HV = 8, 16
FF = 2816
FB = FF // P
ML_H = 4
MLA_H, NOPE, ROPE, QK = 8, 64, 32, 96
MEM_H = 4
EPS = 1e-6
NEG = -1e30
TWO_PI_HI = 6.28125
TWO_PI_LO = float(np.float32(2 * np.pi - 6.28125))
ROUND = 12582912.0
PI_IN = 3.1415925

SLOTS = 4
SLOT = 2048
SPLIT_SLOTS = 2
WORK = 23100
BANKS = 4

PHASES = [
    ("gdn_ba", 1, 1, 1, 8, False), ("gdn_qkv", 16, 2, 1, 16, True), ("gdn_z", 8, 2, 1, 16, True), ("gdn_out", 8, 1, 1, 16, True),
    ("up0", 22, 2, 1, 16, True), ("down0", 16, 1, 2, 11, True),
    ("ml_gates", 1, 1, 1, 8, False), ("ml_in", 12, 2, 1, 16, True), ("ml_out", 4, 2, 1, 16, True),
    ("up1", 22, 2, 1, 16, True), ("down1", 16, 1, 2, 11, True),
    ("up2", 22, 2, 1, 16, True), ("down2", 16, 1, 2, 11, True),
    ("in_uv", 4, 2, 1, 16, True), ("in_cq_kr", 2, 2, 1, 16, True), ("in_qm", 2, 2, 1, 16, True), ("in_ckv", 1, 2, 1, 16, True),
    ("in_gates", 12, 2, 1, 16, True), ("mla_q", 2, 4, 1, 12, False), ("mla_k", 1, 8, 1, 16, False), ("mla_v", 1, 2, 1, 8, False),
    ("mem_k", 2, 2, 1, 16, False), ("mem_v", 2, 2, 1, 16, False),
    ("branches", 8, 3, 1, 12, True), ("mix_out", 4, 2, 1, 16, True),
    ("up3", 22, 2, 1, 16, True), ("down3", 16, 1, 2, 11, True),
]


class Phase:
    def __init__(self, name, slabs, parts, per_product, blocks, split):
        self.name, self.slabs, self.parts, self.per_product, self.blocks, self.split = name, slabs, parts, per_product, blocks, split
        self.products = slabs * parts // per_product
        self.turn = SLOTS * per_product if parts < BANKS and per_product > 1 else SLOTS


def plan():
    out, slab, product, part, word = {}, 0, 0, 0, 0
    for args in PHASES:
        ph = Phase(*args)
        ph.slab0, ph.product0, ph.part0, ph.word0 = slab, product, part, word
        slab += ph.slabs
        product += ph.products
        part += ph.slabs * ph.parts
        word += ph.slabs * ph.blocks * P * P
        ph.end = product
        out[ph.name] = ph
    return out, slab, word


PLAN, SLABS, STREAM_WORDS = plan()
SLAB_OF = [ph for ph in PLAN.values() for _ in range(ph.slabs)]
SPLITS = [n for n in range(SLABS) if SLAB_OF[n].split]
SPLIT_AT = {n: i for i, n in enumerate(SPLITS)}


def done_value(n):
    ph = SLAB_OF[n]
    return ph.part0 + (n - ph.slab0 + 1) * ph.parts


CONST_COLS, PARAM_COLS = {}, {}


def columns(table, sizes):
    at = 0
    for name, n in sizes:
        table[name] = (at, n)
        at += n
    return at


N_CONST = columns(CONST_COLS, [
    ("ident", P), ("ones", P), ("causal", T), ("level", 7 * P), ("rot", QK), ("inv_freq", 1),
    ("row_of", 31), ("score_mask", 3 * P), ("tri", P),
    ("l2_scale", 1), ("l2_eps", 1), ("eps", 1)])
N_PARAM = columns(PARAM_COLS, [
    ("norm_w", 8 * DB), ("gdn_conv", 32 * 4), ("ffn_conv", 2 * 2 * FB * 3), ("ffn_bias", 2 * 2 * FB),
    ("gdn_norm", 1), ("a_log", 1), ("dt_bias", 1), ("ml_gate_i", 1), ("ml_gate_f", 1), ("ml_norm", 8),
    ("ffn1_norm", DB), ("mix_norm", DB), ("ffn2_norm", DB), ("mem_norm", DB), ("b_gate", 24),
    ("sg_g", 4), ("sg_b", 4), ("cq_norm", 3), ("ckv_norm", 2), ("q_norm", 1), ("k_norm", 1),
    ("mq_norm", 1), ("mk_norm", 1)])


class Steps:

    def __init__(self, make_sem, counts):
        self.make_sem, self.counts, self.sems = make_sem, counts, {}
        self.pos, self.seen = {}, {}

    def sem(self, name):
        if name not in self.sems:
            self.sems[name] = self.make_sem(name)
        return self.sems[name]

    def begin(self, name):
        self.pos[name] = 0

    def inc(self, ins, name, step=None):
        self.pos[name] = self.pos.get(name, 0) + 1
        if step is not None:
            key = (name, step)
            assert self.seen.get(key, self.pos[name]) == self.pos[name], key
            self.seen[key] = self.pos[name]
        self.seen[name] = max(self.seen.get(name, 0), self.pos[name])
        return ins.then_inc(self.sem(name), 1)

    def value(self, name, step, turn=0):
        per = self.counts.get(name, 1)
        at = per if step == "last" else self.counts.get((name, step), 1)
        if self.counts and step != "last" and (name, step) not in self.counts:
            raise KeyError((name, step))
        return at if isinstance(turn, int) and turn == 0 else turn * per + at

    def at(self, name, step="last", turn=0):
        return self.sem(name), self.value(name, step, turn)

    def own(self, eng, name, turn=0):
        n = self.pos.get(name, 0)
        if n > 0:
            eng.wait_ge(self.sem(name), n if isinstance(turn, int) and turn == 0 else turn * self.counts.get(name, 1) + n)


def program(nc, x_t, meta_t, mem_t, positions, stream, consts, params, sg_w_t, sg_bias, out_t, counts):
    with ExitStack() as ctx:
        sem_list = []

        def make_sem(name):
            s = ctx.enter_context(nc.semaphore(name))
            sem_list.append(s)
            return s

        S = Steps(make_sem, counts)

        def sb(name, shape, dt=F32):
            return ctx.enter_context(nc.sbuf_tensor(name, shape, dt))

        ring = sb("ring", [P, SLOTS, SLOT])
        with nc.sbuf_tensor("w_spare", [P, 2 * SPLIT_SLOTS * SLOT], F32) as t:
            spare = t
        w_hi = sb("w_hi", [P, SPLIT_SLOTS, SLOT], F32R)
        w_lo = sb("w_lo", [P, SPLIT_SLOTS, SLOT], F32R)
        Cn = sb("consts_sb", [P, N_CONST])
        Pm = sb("params_sb", [P, N_PARAM])
        hs = sb("hs", [P, DB, T])
        a = sb("a", [P, DB, T])
        mix = sb("mix", [P, DB, T])
        sq = sb("sq", [P, DB, T])
        rs = sb("rs", [P, 2, T])
        with nc.sbuf_tensor("work_r", [P, WORK], F32R) as t:
            work_r = t
        work = sb("work", [P, WORK])
        ps = [ctx.enter_context(nc.psum_tensor(f"bank{i}", [P, 512], F32))[:, :] for i in range(8)]

        def cn(name, lo=0, n=None):
            at, size = CONST_COLS[name]
            return Cn[:, at + lo:at + lo + (size if n is None else n)]

        def pm(name, col=0):
            at, _ = PARAM_COLS[name]
            return Pm[:, at + col:at + col + 1]

        def area(at, *shape, of=None):
            n = int(np.prod(shape))
            v = (work if of is None else of)[:, at:at + n]
            if len(shape) == 2:
                v = v.rearrange("p (a b) -> p a b", b=shape[1])
            if len(shape) == 3:
                v = v.rearrange("p (a b c) -> p a b c", b=shape[1], c=shape[2])
            return v

        ident, ones = cn("ident"), cn("ones")
        weights_in = [S.sem(f"weights_in{i}") for i in range(SLOTS)]
        product_done = S.sem("product_done")
        bank_free = [S.sem(f"bank_free{i}") for i in range(BANKS)]
        small_in = S.sem("small_in")
        x_in = [S.sem(f"x_in{half}") for half in range(2)]

        class Unit:

            def __init__(self, ph, size, j, i, per_turn):
                self.j, self.ph = j, ph
                self.u = j if per_turn == 0 else i * per_turn + j
                self.at = j * size
                self.more = 0 if per_turn == 0 else i * (per_turn * size * ph.per_product)
                self.more4 = 0 if per_turn == 0 else i * (per_turn * size // BANKS)

            def ready(self, eng, m=0):
                eng.wait_ge(product_done, self.more + (self.ph.part0 + (self.at + m + 1) * self.ph.per_product))

            def bank(self, m=0):
                return ps[(self.ph.product0 + self.at + m) % BANKS]

            def free(self, ins, m=0):
                return ins.then_inc(bank_free[(self.ph.product0 + self.at + m) % BANKS], 1)

            def was_read(self, eng, m=0, before=0):
                b = self.ph.product0 + self.at + m - before
                eng.wait_ge(bank_free[b % BANKS], self.more4 + (b // BANKS + 2))

        hi_done, lo_done = S.sem("hi_done"), S.sem("lo_done")
        prepared = {"hi": 0, "lo": 0}

        def split_slab(eng, which, s, ph=None, i=None):
            n = SPLITS[s]
            size = SLAB_OF[n].blocks * P
            slot, raw_w = s % SPLIT_SLOTS, ring[:, n % SLOTS, 0:SLAB_OF[n].blocks * P]
            at = lambda per_turn, v: v if i is None else i * per_turn + v
            if which == "hi":
                eng.wait_ge(weights_in[n % SLOTS], at(16, 16 * (n // SLOTS + 1)))
                if s >= SPLIT_SLOTS:
                    eng.wait_ge(product_done, at(SLOTS * ph.parts if ph else 0, done_value(SPLITS[s - SPLIT_SLOTS])))
                eng.activation(w_hi[:, slot, 0:size], raw_w, ACT.Copy).then_inc(hi_done, 1)
            else:
                eng.wait_ge(hi_done, at(SLOTS, s + 1))
                eng.tensor_tensor(w_lo[:, slot, 0:size], raw_w, w_hi[:, slot, 0:size].bitcast(F32), ALU.subtract).then_inc(lo_done, 1)

        def prepare(eng, which, name):
            first = SPLIT_AT[PLAN[name].slab0]
            while prepared[which] < first + SPLIT_SLOTS:
                split_slab(eng, which, prepared[which])
                prepared[which] += 1

        def each_product(eng, name, size, body, table=None, turns=None, split=None, late=None, lag=0, between=None,
                         split_last=False):
            ph = PLAN[name]
            per_turn = SLOTS * ph.parts // ph.per_product // size
            total = ph.products // size
            head = lag * size // ph.parts
            most = (ph.slabs - head) // SLOTS if (per_turn * size) % BANKS == 0 else 0
            if split:
                assert prepared[split] == SPLIT_AT[ph.slab0] + SPLIT_SLOTS, name

                def may(j):
                    s = SPLIT_AT[ph.slab0 + j] + SPLIT_SLOTS
                    return s < len(SPLITS) and (name != "gdn_qkv" or j + SPLIT_SLOTS < ph.slabs) and SPLITS[s] == ph.slab0 + j + SPLIT_SLOTS and SLAB_OF[SPLITS[s]].blocks == ph.blocks
                while most and not all(may(j) for j in range(head, head + most * SLOTS)):
                    most -= 1
            turns = 0 if between is not None else most if turns is None else min(turns, most)

            def ahead(j, i):
                n = ph.slab0 + j
                s = SPLIT_AT[n] + SPLIT_SLOTS
                if s < len(SPLITS) and SPLITS[s] - SLOTS <= n and not (name == "gdn_qkv" and s > SPLIT_AT[ph.slab0] + ph.slabs - 1):
                    split_slab(eng, split, s, ph, i)
                    if i is None:
                        assert prepared[split] == s
                        prepared[split] += 1

            def unit(j, i, per_turn_):
                if between is not None and j * size * ph.per_product % ph.parts == 0:
                    between(j * size * ph.per_product // ph.parts)
                if split_last:
                    body(Unit(ph, size, j, i, per_turn_))
                if split:
                    lo, hi = j * size * ph.per_product, (j + 1) * size * ph.per_product
                    for slab in range(lo // ph.parts, hi // ph.parts):
                        ahead(slab, None if per_turn_ == 0 else i)
                if not split_last:
                    body(Unit(ph, size, j, i, per_turn_))
                if late is not None and j >= lag:
                    late(Unit(ph, size, j - lag, i, per_turn_))

            for j in range(lag):
                unit(j, 0, 0)
            done = lag
            if turns >= 2:
                if table is not None:
                    eng.preload_act_table(table)
                with eng.Fori(0, turns) as i:
                    for j in range(lag, lag + per_turn):
                        unit(j, i, per_turn)
                done += turns * per_turn
                if split:
                    prepared[split] += turns * SLOTS
            for j in range(done, total):
                unit(j, 0, 0)
            for j in range(total - lag, total):
                late(Unit(ph, size, j, 0, 0))

        def nothing(unit):
            pass

        def stream_pe(pe, name, x, n, between=None):
            ph = PLAN[name]
            kb = ph.blocks // ph.parts

            def slab(j, i, looped):
                nslab = ph.slab0 + j
                if ph.split:
                    done = SPLIT_AT[nslab] + 1
                    slot = (done - 1) % SPLIT_SLOTS
                    pe.wait_ge(lo_done, i * ph.turn + done if looped else done)
                else:
                    arrived = 16 * (nslab // SLOTS + 1)
                    pe.wait_ge(weights_in[nslab % SLOTS], i * (4 * ph.turn) + arrived if looped else arrived)
                for m in range(ph.parts):
                    part = j * ph.parts + m
                    b = ph.product0 + part // ph.per_product
                    free = b // BANKS + 1
                    begins, ends = part % ph.per_product == 0, part % ph.per_product == ph.per_product - 1
                    if begins:
                        pe.wait_ge(bank_free[b % BANKS], i * (ph.turn * ph.parts // ph.per_product // BANKS) + free if looped else free)
                    out = ps[b % BANKS][:, 0:n]
                    for k in range(kb):
                        at = (m * kb + k) * P
                        first, last = begins and k == 0, ends and k == kb - 1
                        kx = part % ph.per_product * kb + k
                        if ph.split:
                            hi, lo = x(m, kx)
                            pe.matmul(out, w_hi[:, slot, at:at + P], hi, start=first, stop=False)
                            pe.matmul(out, w_hi[:, slot, at:at + P], lo, start=False, stop=False)
                            mm = pe.matmul(out, w_lo[:, slot, at:at + P], hi, start=False, stop=last)
                        else:
                            mm = pe.matmul(out, ring[:, nslab % SLOTS, at:at + P], x(m, kx), start=first, stop=last)
                    mm.then_inc(product_done, 1)

            turns, done = 0 if between is not None else ph.slabs // ph.turn, 0
            if turns >= 2:
                with pe.Fori(0, turns) as i:
                    for j in range(ph.turn):
                        slab(j, i, True)
                done = turns * ph.turn
            for j in range(done, ph.slabs):
                if between is not None:
                    between(j)
                slab(j, 0, False)

        A_HI, A_LO = (area(at, DB, T, of=work_r) for at in (WORK - 2 * DB * T, WORK - DB * T))
        STEPS = 8

        def split_act(act, use, src, hi, blocks, n, ready=None):
            S.begin("x_hi")
            per = blocks // STEPS
            for i in range(STEPS):
                if ready is not None:
                    ready(per * i + per - 1)
                k = slice(per * i, per * i + per)
                S.inc(act.activation(hi[:, k, 0:n], src[:, k, 0:n], ACT.Copy), "x_hi", i)

        def split_dve(dve, use, src, hi, lo, blocks, n):
            S.begin("x_lo")
            per = blocks // STEPS
            for i in range(STEPS):
                k = slice(per * i, per * i + per)
                dve.wait_ge(*S.at("x_hi", i, use))
                S.inc(dve.tensor_tensor(lo[:, k, 0:n], src[:, k, 0:n], hi[:, k, 0:n].bitcast(F32), ALU.subtract), "x_lo", i)

        def split_input(pe, hi, lo, n, arrive=None):
            seen = set()

            def x(m, k):
                if arrive is not None and k not in seen:
                    seen.add(k)
                    arrive(k)
                return hi[:, k, 0:n], lo[:, k, 0:n]
            return x

        def by_step(pe, use, per=1):
            return lambda k: pe.wait_ge(*S.at("x_lo", k // per, use)) if k % per == 0 else None

        gain = lambda name, base=0: (lambda k: pm(name, base + k))

        stat = {"norm": ps[4], "cq": ps[4], "ckv": ps[5], "mem": ps[7]}
        sq_at = {"norm": 0, "cq": 0, "ckv": 3, "mem": 0}
        rms_of = {kind: rs for kind in ("norm", "cq", "mem")}
        rms_of["ckv"] = mix[:, :, :].rearrange("p a b -> p (a b)")[:, 6 * SEQ:8 * SEQ].rearrange("p (a b) -> p a b", b=SEQ)

        def square(act, k, src, n, kind="norm"):
            if k == 0:
                S.begin(f"{kind}_act")
            S.inc(act.activation(sq[:, sq_at[kind] + k, 0:n], src, ACT.Square), f"{kind}_act", f"sq{k}")

        def norm_act(act, use, src, blocks, n, width, ready=None, kind="norm"):
            if src is not None:
                for k in range(blocks):
                    if ready is not None:
                        ready(k)
                    square(act, k, src(k), n, kind)
            act.preload_act_table(ACT.Sqrt)
            act.wait_ge(*S.at(f"{kind}_pe", "sums", use))
            if use == 0 and kind == "norm":
                act.wait_ge(S.sem("small_in"), 32)
            S.inc(act.activation(rms_of[kind][:, 1, 0:n], stat[kind][:, 0:n], ACT.Sqrt, bias=cn("eps"), scale=1.0 / width), f"{kind}_act", "rms")

        def norm_pe(pe, use, blocks, n, kind="norm"):
            S.begin(f"{kind}_pe")
            for k in range(blocks):
                pe.wait_ge(*S.at(f"{kind}_act", f"sq{k}", use))
                mm = pe.matmul(stat[kind][:, 0:n], ones, sq[:, sq_at[kind] + k, 0:n], start=(k == 0), stop=(k == blocks - 1))
            S.inc(mm, f"{kind}_pe", "sums")

        def norm_dve(dve, use, n, src, gain, dst, blocks, add=None, kind="norm"):
            S.begin(f"{kind}_dve")
            dve.wait_ge(*S.at(f"{kind}_act", "rms", use))
            S.inc(dve.reciprocal(rms_of[kind][:, 0, 0:n], rms_of[kind][:, 1, 0:n]), f"{kind}_dve", "rstd")
            dve.wait_ge(*S.at(f"{kind}_dve", "rstd", use))
            if add is not None:
                S.begin("norm_add")
            for k in range(blocks + 1):
                if k < blocks:
                    S.inc(dve.scalar_tensor_tensor(out=dst(k), in0=src(k), scalar=gain(k), in1=rms_of[kind][:, 0, 0:n],
                                                   op0=ALU.mult, op1=ALU.mult), f"{kind}_dve", f"k{k}")
                if add is not None and k >= 1:
                    dve.wait_ge(*S.at(f"{kind}_dve", f"k{k - 1}", use))
                    S.inc(dve.tensor_tensor(add[1](k - 1), add[1](k - 1), dst(k - 1), ALU.add), "norm_add", k - 1)

        rrow = sb("rrow", [HV, 2, T])

        def rown_squares(act, squares):
            for src, dst in squares:
                act.activation(dst, src, ACT.Square).then_inc(S.sem("rown_squares"), 1)

        def rown_act(act, use, squares, n, rows, scale, eps):
            S.begin("rown_act")
            rown_squares(act, squares)
            act.preload_act_table(ACT.Sqrt)
            act.wait_ge(*S.at("rown_pe", "sums", use))
            if use:
                act.wait_ge(*S.at("rown_dve", "rows", use - 1))
            S.inc(act.activation(rrow[0:rows, 1, 0:n], ps[7 if use == 4 else 4][0:rows, 0:n], ACT.Sqrt, bias=eps[0:rows, :], scale=scale), "rown_act", "root")

        def rown_dve(dve, use, n, rows):
            S.begin("rown_dve")
            dve.wait_ge(*S.at("rown_act", "root", use))
            S.inc(dve.reciprocal(rrow[0:rows, 0, 0:n], rrow[0:rows, 1, 0:n]), "rown_dve", "rows")

        def rown_pe(pe, use, sqr, blocks, per_row, n, rows):
            S.begin("rown_pe")
            if use == 3:
                pe.wait_ge(*S.at("mla_act", "ksq"))
            else:
                pe.wait_ge(S.sem("rown_squares"), (1, 2, 3, 3, 5)[use])
            for k in range(blocks):
                src = sqr(k)
                h = k // per_row
                mm = pe.matmul(ps[7 if use == 4 else 4][0:rows, 0:n], cn("row_of", 15 - h, rows)[0:src.shape[0], :], src,
                               start=(k == 0), stop=(k == blocks - 1))
            S.inc(mm, "rown_pe", "sums")

        qkv = area(0, 32, T)
        raw_c = area(8704, 4, T + 3)
        conv_y = area(8704 + 4 * (T + 3), 4, T)
        rows_at = 8704 + 8 * T + 12
        R_BETA, R_G, R_EG, R_EGL, R_NBEG, R_X, R_Y, R_A, R_Z = range(9)
        row = [work[0:HV, rows_at + i * T:rows_at + (i + 1) * T] for i in range(9)]
        sqh = area(rows_at + 9 * T, 16, T)
        colv = sb("colv", [P, 3, 3, HV])
        colb = sb("colb", [P, 3, HV])

        bc = area(8704, 16, T)
        qn = area(8704 + 4352, 2, T)
        kn = area(8704 + 4896, 2, T)
        qd = area(8704 + 5440, 4, T)
        vs = area(8704 + 6528, 4, T)
        St = area(8704 + 7616, 4, P)
        St2 = area(8704 + 8128, 4, P)
        par0 = 8704 + 8704
        mixw = mix[:, :, :].rearrange("p a b -> p (a b)")
        sqw = sq[:, :, :].rearrange("p a b -> p (a b)")
        names = ["vb", "nkbe", "ktl", "A0T", "attn", "X", "XT", "Am"]

        def tile4(v):
            return v.rearrange("p (a b) -> p a b", b=P)

        buf = {2: {n: area(par0 + 512 * i, 4, P) for i, n in enumerate(names)},
               1: {n: tile4(mixw[:, 512 * i:512 * (i + 1)]) if i < 4 else tile4(sqw[:, 512 * (i - 4):512 * (i - 3)])
                   for i, n in enumerate(names)}}
        St0 = area(0, HV, P, of=spare)
        bc0 = area(2048, 64, META, of=spare)
        for i, n in enumerate(("Y", "decb", "dec")):
            for c in (1, 2):
                buf[c][n] = area(3072 + 1024 * i + 512 * (c - 1), 4, P, of=spare)
        vb0, ktl0 = (area(par0 + 2048 * i, HV, P) for i in range(2))
        c0 = {n: mixw[0:META, 256 * i:256 * (i + 1)].rearrange("p (a b) -> p a b", b=META)
              for i, n in enumerate(("dec", "decb", "A0T", "attn", "X", "XT", "Am", "Y"))}
        kn0, qn0 = (spare[:, 6144 + 128 * i:6144 + 128 * (i + 1)].rearrange("p (a b) -> p a b", b=META) for i in range(2))
        obc = area(8704, HV, T)
        osq = area(8704 + 16 * T, HV, T)
        zs = area(8704 + 32 * T, 4, T)

        hid_hi, hid_lo = (area(i * FB * T, FB, T, of=work_r) for i in range(2))
        f_at = 2 * FB * T
        raw = [area(f_at + i * 2 * (T + 2), 2, T + 2) for i in range(2)]
        y_gu = [area(f_at + 4 * (T + 2) + i * 2 * T, 2, T) for i in range(2)]
        silu_g = [area(f_at + 4 * (T + 2) + (4 + i) * T, T) for i in range(2)]
        h_new = [area(f_at + 4 * (T + 2) + (6 + i) * T, T) for i in range(2)]

        mlT = area(0, 24, T)
        v_tok = area(6528, 3, 8, P)
        bc2 = area(9600, 2, ML_H, T)
        mrow = [work[0:ML_H, 11776 + i * T:11776 + (i + 1) * T] for i in range(9)]
        M_LI, M_Y, M_E, M_ONE, M_B, M_C, M_M, M_EM, M_T = range(9)
        mcol = sb("mcol", [P, 3, ML_H])
        Wt = [[area(14300 + (3 * i + t) * T, T) for t in range(3)] for i in range(2)]
        Pt = [[area(14300 + (6 + 3 * i + t) * T, T) for t in range(3)] for i in range(2)]
        den = area(14300 + 12 * T, 2, T)
        hT = area(14300 + 14 * T, 8, T)
        mbc = area(9600, ML_H, T)
        hsq = area(0, 8, T)

        scratch = nc.dram_tensor("rows_scratch", (64, T), F32, kind="Internal").ap()
        scr_o = nc.dram_tensor("rows_scratch_o", (HV, T), F32, kind="Internal").ap()
        scr_m = nc.dram_tensor("rows_scratch_m", (2 * ML_H, T), F32, kind="Internal").ap()
        scr_h = nc.dram_tensor("rows_scratch_h", (ML_H, T), F32, kind="Internal").ap()
        scr_q = nc.dram_tensor("rows_scratch_q", (16, SEQ), F32, kind="Internal").ap()
        scr_c = nc.dram_tensor("rows_scratch_c", (8, SEQ), F32, kind="Internal").ap()

        def on_all(ap_tensor, offset, *dims):
            return bass.AP(ap_tensor.tensor, offset, [[0, P], *[list(d) for d in dims]])

        PSA, PSB, PSC, PSD = ps[4], ps[5], ps[6], ps[7]

        O_HI, O_LO = area(0, HV, T, of=work_r), area(8704 + 16 * T, HV, T, of=work_r)
        ML_HI, ML_LO = area(0, DB, T, of=work_r), area(DB * T, DB, T, of=work_r)

        BA = Unit(PLAN["gdn_ba"], 1, 0, 0, 0)

        def rows_act(act):
            BA.ready(act)
            S.inc(act.activation(row[R_BETA], BA.bank()[0:HV, 0:T], ACT.Sigmoid), "rows_act", "beta")
            act.wait_ge(*S.at("rows_dve", "x"))
            S.inc(act.activation(row[R_Y], row[R_X], ACT.Abs), "rows_act", "abs")
            S.own(act, "rows_act")
            S.inc(act.activation(row[R_Y], row[R_Y], ACT.Exp, scale=-1.0), "rows_act")
            S.inc(act.activation(row[R_A][:, 0:1], pm("a_log")[0:HV, :], ACT.Exp), "rows_act")
            S.own(act, "rows_act")
            S.inc(act.activation(row[R_Y], row[R_Y], ACT.Ln, bias=1.0), "rows_act", "ln")
            act.wait_ge(*S.at("rows_dve", "diff"))
            S.inc(act.activation(row[R_EG], row[R_G], ACT.Exp), "rows_act")
            S.inc(act.activation(row[R_EGL], row[R_EGL], ACT.Exp), "rows_act", "exps")

        def rows_dve(dve):
            BA.ready(dve)
            dve.wait_ge(*S.at("rows_act", "beta"))
            BA.free(dve.tensor_scalar(row[R_Z], BA.bank()[32:32 + HV, 0:T], pm("dt_bias")[0:HV, :], None, ALU.add))
            BA.was_read(dve)
            S.inc(dve.tensor_copy(row[R_X], row[R_Z]), "rows_dve", "x")
            dve.wait_ge(*S.at("rows_act", "ln"))
            S.inc(dve.scalar_tensor_tensor(out=row[R_Z], in0=row[R_X], scalar=0.0, in1=row[R_Y], op0=ALU.max, op1=ALU.add), "rows_dve")
            S.own(dve, "rows_dve")
            S.inc(dve.tensor_scalar(row[R_X], row[R_Z], row[R_A][:, 0:1], -1.0, ALU.mult, ALU.mult), "rows_dve")
            S.inc(dve.memset(row[R_Y], 1.0), "rows_dve")
            S.own(dve, "rows_dve")
            for t0, c in TILES:
                S.inc(dve.tensor_tensor_scan(row[R_G][:, t0:t0 + c], row[R_Y][:, t0:t0 + c], row[R_X][:, t0:t0 + c], 0.0,
                                             ALU.mult, ALU.add), "rows_dve")
            S.own(dve, "rows_dve")
            for t0, c in TILES:
                S.inc(dve.tensor_scalar(row[R_EGL][:, t0:t0 + c], row[R_G][:, t0:t0 + c], row[R_G][:, t0 + c - 1:t0 + c], -1.0,
                                        ALU.subtract, ALU.mult), "rows_dve", "diff" if t0 == TILES[-1][0] else None)
            dve.wait_ge(*S.at("rows_act", "exps"))
            S.inc(dve.scalar_tensor_tensor(out=row[R_NBEG], in0=row[R_BETA], scalar=-1.0, in1=row[R_EG], op0=ALU.mult, op1=ALU.mult),
                  "rows_dve", "rows")

        def rows_pe(pe):
            pe.wait_ge(*S.at("rows_dve", "rows"))
            for c, (t0, n) in enumerate(TILES):
                for q, r in enumerate((R_BETA, R_G, R_EGL, R_NBEG)):
                    mm = pe.transpose(PSB[0:n, (c * 4 + q) * HV:(c * 4 + q + 1) * HV], row[r][:, t0:t0 + n], ident[0:HV, 0:HV])
            S.inc(mm, "rows_pe")

        def cols_dve(dve):
            dve.wait_ge(*S.at("rows_pe"))
            for c, (t0, n) in enumerate(TILES):
                src = PSB[0:n, c * 64:c * 64 + 64].rearrange("p (a b) -> p a b", b=HV)
                S.inc(dve.tensor_copy(colv[0:n, c, :, :], src[:, 0:3, :]), "cols_dve")
                S.inc(dve.tensor_copy(colb[0:n, c, :], src[:, 3, :]), "cols_dve")

        CONV_AHEAD = 4
        at, n = PARAM_COLS["gdn_conv"]
        gdn_taps = Pm[:, at:at + n].rearrange("p (b t) -> p b t", t=4)

        def qkv_act(act):
            def project(un):
                act.wait_ge(*S.at("qkv_dve", turn=un.u))
                act.wait_ge(*S.at("qkv_act", turn=un.u))
                un.ready(act)
                act.activation(raw_c[:, un.j % 4, 3:T + 3], un.bank()[:, 0:T], ACT.Copy)
                un.free(act.activation(conv_y[:, un.j % 4, :], un.bank()[:, 0:T], ACT.Copy, scale=gdn_taps[:, un.u, 3:4]))

            def silu(un):
                S.begin("qkv_act")
                act.wait_ge(*S.at("qkv_dve", turn=un.u + CONV_AHEAD))
                S.inc(act.activation(qkv[:, un.u, :], conv_y[:, un.j % 4, :], ACT.Silu), "qkv_act", "silu")
            each_product(act, "gdn_qkv", 1, project, ACT.Silu, split="hi", late=silu, lag=2)

        def qkv_dve(dve):
            def body(un):
                S.begin("qkv_dve")
                un.was_read(dve)
                y, r = conv_y[:, un.j % 4, :], raw_c[:, un.j % 4, :]
                for t in (0, 1, 2):
                    S.own(dve, "qkv_dve", un.u + CONV_AHEAD)
                    S.inc(dve.scalar_tensor_tensor(out=y, in0=r[:, t:t + T], scalar=gdn_taps[:, un.u, t:t + 1], in1=y,
                                                   op0=ALU.mult, op1=ALU.add), "qkv_dve")
            each_product(dve, "gdn_qkv", 1, body, split="lo")

        L0, L1 = 4, 7
        lvl = cn("level").rearrange("p (l b) -> p l b", b=P)

        def bank(c, i):
            return ps[4 * (c % 2) + i]

        def two(v):
            return v.unsqueeze(2).broadcast_to([v.shape[0], v.shape[1], 2, v.shape[-1]])

        def by2(v):
            return v.rearrange("p (a b) n -> p a b n", b=2)

        def over(v, n):
            return v.unsqueeze(1).broadcast_to([v.shape[0], n, v.shape[-1]])

        def down(v, n):
            return v.unsqueeze(2).broadcast_to([v.shape[0], v.shape[1], n])

        def first_pool(pool):
            inc = lambda ins, step=None: S.inc(ins, "first_pool", step)
            pool.wait_ge(*S.at("rows_dve", "rows"))
            for q, src in ((1, row[R_BETA]), (2, row[R_G]), (3, row[R_EG])):
                pool.dma_start(scratch[16 * q:16 * q + 16, :], src).then_inc(S.sem("scan_rows_out"), 16)
            pool.wait_ge(S.sem("scan_rows_out"), 48)
            pool.wait_ge(*S.at("cols_dve"))
            pool.wait_ge(*S.at("qkv_act", turn=31 + CONV_AHEAD))
            pool.dma_start(bc0[:, 16:64, :], on_all(scratch, 16 * T, (T, 48), (1, META))).then_inc(S.sem("first_rows_in"), 16)
            fetch_gate_rows(pool, 0)
            pool.wait_ge(*S.at("rown_dve", "rows", 0))
            pool.dma_start(scratch[0:16, :], rrow[:, 0, :]).then_inc(S.sem("scan_rows_out"), 16)
            pool.wait_ge(S.sem("scan_rows_out"), 64)
            pool.dma_start(bc0[:, 0:16, :], on_all(scratch, 0, (T, 16), (1, META))).then_inc(S.sem("first_rows_in"), 16)
            fetch_norm_rows(pool, 0)
            for l in range(1, L0):
                if l == 1:
                    pool.wait_ge(*S.at("first_dve", "XT0"))
                else:
                    pool.wait_ge(*S.at("first_pe", f"Y{l - 1}"))
                inc(pool.tensor_tensor(c0["Am"], c0["A0T"], over(lvl[0:META, l, 0:META], HV), ALU.mult), f"Am{l}")

        def first_dve(dve):
            inc = lambda ins, step=None: S.inc(ins, "first_dve", step)
            own = lambda: S.own(dve, "first_dve")
            dve.wait_ge(S.sem("first_rows_in"), 32)
            inc(dve.tensor_tensor(kn0, qkv[:, 8:16, 0:META], bc0[:, 8:16, :], ALU.mult))
            inc(dve.tensor_tensor(qn0, qkv[:, 0:8, 0:META], bc0[:, 0:8, :], ALU.mult), "kn")
            inc(dve.tensor_tensor(c0["dec"], bc0[0:META, 32:48, :], over(cn("causal")[0:META, 0:META], HV), ALU.add))
            own()
            inc(dve.tensor_tensor(c0["dec"], c0["dec"], down(colv[0:META, 0, 1, :], META), ALU.subtract), "diff")
            dve.wait_ge(*S.at("first_act", "dec"))
            inc(dve.tensor_tensor(c0["decb"], c0["dec"], bc0[0:META, 16:32, :], ALU.mult))
            own()
            dve.wait_ge(*S.at("first_pe", "kq"))
            kk, kq = (ps[6][0:META, 128 * i:128 * (i + 1)].rearrange("p (a b) -> p a b", b=META) for i in range(2))
            inc(dve.tensor_tensor(by2(c0["A0T"]), two(kk), by2(c0["decb"]), ALU.mult))
            inc(dve.tensor_tensor(by2(c0["attn"]), two(kq), by2(c0["dec"]), ALU.mult), "attn")
            own()
            inc(dve.tensor_tensor(c0["Y"], c0["A0T"], over(lvl[0:META, 0, 0:META], HV), ALU.mult))
            own()
            inc(dve.tensor_tensor(c0["XT"], over(ident[0:META, 0:META], HV), c0["Y"], ALU.subtract), "XT0")
            dve.wait_ge(*S.at("first_pe", "tok"))
            for b in range(2):
                kt = two(tile4(ps[b][0:META, :]))
                inc(dve.tensor_tensor(by2(ktl0[0:META, 8 * b:8 * b + 8, :]), kt, by2(down(colv[0:META, 0, 2, 8 * b:8 * b + 8], P)), ALU.mult))
            for b in range(4):
                inc(dve.tensor_tensor(vb0[0:META, 4 * b:4 * b + 4, :], tile4(ps[2 + b][0:META, :]), down(colv[0:META, 0, 0, 4 * b:4 * b + 4], P),
                                      ALU.mult), "vb" if b == 3 else None)
            for l in range(1, L0):
                if l < L0 - 1:
                    dve.wait_ge(*S.at("first_pe", f"XX{l}"))
                    inc(dve.tensor_tensor(c0["X"], c0["X"], ps[7][0:META, 256:512].rearrange("p (a b) -> p a b", b=META), ALU.subtract))
                dve.wait_ge(*S.at("first_pe", f"XXT{l}"))
                inc(dve.tensor_tensor(c0["XT"], c0["XT"], ps[6][0:META, 256:512].rearrange("p (a b) -> p a b", b=META), ALU.subtract), f"XT{l}")
            dve.wait_ge(*S.at("first_pe", "S"))
            for b in range(2):
                inc(dve.tensor_copy(St0[:, 4 * b:4 * b + 4, :], tile4(ps[b])), "S" if b else None)

        def first_act(act):
            inc = lambda ins, step=None: S.inc(ins, "first_act", step)
            act.wait_ge(*S.at("first_dve", "diff"))
            inc(act.activation(c0["dec"], c0["dec"], ACT.Exp), "dec")
            act.wait_ge(*S.at("first_pe", "X"))
            inc(act.activation(c0["X"], ps[7][0:META, 256:512].rearrange("p (a b) -> p a b", b=META), ACT.Copy), "X")
            for l in range(1, L0):
                act.wait_ge(*S.at("first_pe", f"Y{l}"))
                inc(act.activation(c0["Y"], ps[7][0:META, 0:256].rearrange("p (a b) -> p a b", b=META), ACT.Copy), f"Y{l}")
            act.wait_ge(*S.at("first_pe", "vn"))
            for b in range(4):
                inc(act.activation(vb0[0:META, 4 * b:4 * b + 4, :], tile4(ps[2 + b][0:META, :]), ACT.Copy), "vn" if b == 3 else None)
            act.wait_ge(*S.at("first_pe", "o"))
            inc(act.activation(qkv[:, 16:32, 0:META], ps[6][:, 0:256].rearrange("p (a b) -> p a b", b=META), ACT.Copy))
            act.wait_ge(*S.at("first_pe", "S"))
            for b in (2, 3):
                inc(act.activation(St0[:, 4 * b:4 * b + 4, :], tile4(ps[b]), ACT.Copy), "S" if b == 3 else None)

        def first_pe(pe):
            inc = lambda ins, step=None: S.inc(ins, "first_pe", step)
            small = lambda b, half, h: ps[b][0:META, 256 * half + h * META:256 * half + (h + 1) * META]
            pe.wait_ge(*S.at("first_dve", "kn"))
            for h in range(HQ):
                pe.matmul(small(6, 0, h), kn0[:, h, :], kn0[:, h, :], start=True, stop=True)
                mm = pe.matmul(small(6, 0, 8 + h), kn0[:, h, :], qn0[:, h, :], start=True, stop=True)
            inc(mm, "kq")
            for h in range(HQ):
                pe.transpose(ps[h // 4][0:META, h % 4 * P:(h % 4 + 1) * P], kn0[:, h, :], ident)
            for h in range(HV):
                mm = pe.transpose(ps[2 + h // 4][0:META, h % 4 * P:(h % 4 + 1) * P], qkv[:, 16 + h, 0:META], ident)
            inc(mm, "tok")
            pe.wait_ge(*S.at("first_dve", "XT0"))
            for h in range(HV):
                mm = pe.transpose(small(7, 1, h), c0["XT"][:, h, :], ident[0:META, 0:META])
            inc(mm, "X")
            for l in range(1, L0):
                pe.wait_ge(*S.at("first_pool", f"Am{l}"))
                if l == 1:
                    pe.wait_ge(*S.at("first_act", "X"))
                pe.wait_ge(*S.at("first_dve", f"XT{l - 1}"))
                for h in range(HV):
                    mm = pe.matmul(small(7, 0, h), c0["Am"][:, h, :], c0["X"][:, h, :], start=True, stop=True)
                inc(mm, f"Y{l}")
                pe.wait_ge(*S.at("first_act", f"Y{l}"))
                if l < L0 - 1:
                    for h in range(HV):
                        mm = pe.matmul(small(7, 1, h), c0["XT"][:, h, :], c0["Y"][:, h, :], start=True, stop=True)
                    inc(mm, f"XX{l}")
                for h in range(HV):
                    mm = pe.matmul(small(6, 1, h), c0["Y"][:, h, :], c0["XT"][:, h, :], start=True, stop=True)
                inc(mm, f"XXT{l}")
            pe.wait_ge(*S.at("first_dve", f"XT{L0 - 1}"))
            for h in range(HV):
                mm = pe.matmul(ps[2 + h // 4][0:META, h % 4 * P:(h % 4 + 1) * P], c0["XT"][:, h, :], vb0[0:META, h, :], start=True, stop=True)
            inc(mm, "vn")
            pe.wait_ge(*S.at("first_act", "vn"))
            for h in range(HV):
                mm = pe.matmul(ps[6][:, h * META:(h + 1) * META], vb0[0:META, h, :], c0["attn"][:, h, :], start=True, stop=True)
            inc(mm, "o")
            for h in range(HV):
                mm = pe.matmul(ps[h // 4][:, h % 4 * P:(h % 4 + 1) * P], ktl0[0:META, h, :], vb0[0:META, h, :], start=True, stop=True)
            inc(mm, "S")

        def fetch_gate_rows(pool, t):
            pool.dma_start(bc[:, 4:16, :].rearrange("p (a b) t -> p a b t", b=4),
                           on_all(scratch, t * (4 * T) + 16 * T, (16 * T, 3), (T, 4), (1, T))).then_inc(S.sem("bc_in"), 16)

        def fetch_norm_rows(pool, t):
            pool.dma_start(bc[:, 0:4, :].rearrange("p (a b) t -> p a b t", b=2),
                           on_all(scratch, t * (2 * T), (8 * T, 2), (T, 2), (1, T))).then_inc(S.sem("bc_in"), 16)

        def ahead_kn(dve, t):
            S.begin("ahead_dve")
            dve.wait_ge(S.sem("bc_in"), t * 32 + 32)
            qk = work[:, 0:16 * T].rearrange("p (s g h t) -> p s g h t", s=2, h=2, t=T)
            S.inc(dve.tensor_tensor(qn, qk[:, 0, t, :, :], bc[:, 0:2, :], ALU.mult), "ahead_dve")
            S.inc(dve.tensor_tensor(kn, qk[:, 1, t, :, :], bc[:, 2:4, :], ALU.mult), "ahead_dve", "kn")

        def ahead_diff(dve, t):
            for c in (1, 2):
                t0, n = TILES[c]
                S.inc(dve.tensor_tensor(buf[c]["dec"], bc[:, 8:12, t0:t0 + n], over(cn("causal")[:, 0:P], 4), ALU.add), "ahead_dve")
            for c in (1, 2):
                S.own(dve, "ahead_dve", t)
                g_col = colv[:, c, 1, :].rearrange("p (g h) -> p g h", h=4)[:, t, :]
                S.inc(dve.tensor_tensor(buf[c]["dec"], buf[c]["dec"], down(g_col, P), ALU.subtract), "ahead_dve", f"diff{c}")

        def ahead_v(act, t):
            S.begin("ahead_act")
            v = work[:, 16 * T:32 * T].rearrange("p (g h t) -> p g h t", h=4, t=T)[:, t, :, META:T]
            S.inc(act.activation(vs[:, :, META:T], v, ACT.Copy), "ahead_act", "v")

        def ahead_exp(act, t):
            for c in (1, 2):
                act.wait_ge(*S.at("ahead_dve", f"diff{c}", t))
                S.inc(act.activation(buf[c]["dec"], buf[c]["dec"], ACT.Exp), "ahead_act", f"dec{c}")

        def ahead_beta(pool, t):
            S.begin("ahead_pool")
            for c in (1, 2):
                t0, n = TILES[c]
                pool.wait_ge(*S.at("ahead_act", f"dec{c}", t))
                S.inc(pool.tensor_tensor(buf[c]["decb"], buf[c]["dec"], bc[:, 4:8, t0:t0 + n], ALU.mult), "ahead_pool", f"decb{c}")

        CHUNKS, TOP = (1, 2), L1 - 1

        def group_pool(pool, g, last):
            inc = lambda ins, step=None: S.inc(ins, "scan_pool", step)
            S.begin("scan_pool")

            def on_level(c, l):
                B = buf[c]
                inc(pool.tensor_tensor(B["Am"], B["A0T"], over(lvl[:, l, :], 4), ALU.mult), f"Am{c}.{l}")
            for c in CHUNKS:
                pool.wait_ge(*S.at("scan_dve", f"A0T{c}", g))
                on_level(c, 1)
            inc(pool.tensor_tensor(by2(qd[:, :, META:T]), two(qn[:, :, META:T]), by2(bc[:, 12:16, META:T]), ALU.mult), "qd")
            for l in range(2, L1):
                for c in CHUNKS:
                    pool.wait_ge(*S.at("scan_pe", f"Y{c}.{l - 1}", g))
                    on_level(c, l)
                if l == 3 and not last:
                    pool.wait_ge(*S.at("scan_dve", "decayed", g))
                    pool.wait_ge(*S.at("scan_pool", "qd", g))
                    fetch_gate_rows(pool, g + 1)
                    fetch_norm_rows(pool, g + 1)
            if not last:
                ahead_beta(pool, g + 1)

        def group_dve(dve, g, last):
            inc = lambda ins, step=None: S.inc(ins, "scan_dve", step)
            own = lambda: S.own(dve, "scan_dve", g)
            S.begin("scan_dve")
            cv = colv[:, :, :, :].rearrange("p c q (g h) -> p c q g h", h=4)
            cb = colb[:, :, :].rearrange("p c (g h) -> p c g h", h=4)
            half = lambda v, i: tile4(v)[:, 2 * i:2 * i + 2, :]
            for c in CHUNKS:
                B = buf[c]
                dve.wait_ge(*S.at("scan_pe", f"kk{c}", g))
                dve.wait_ge(*S.at("ahead_pool", f"decb{c}", g))
                inc(dve.tensor_tensor(by2(B["A0T"]), two(half(bank(c, 0), 0)), by2(B["decb"]), ALU.mult), f"A0T{c}")
                own()
                inc(dve.tensor_tensor(B["Y"], B["A0T"], over(lvl[:, 0, :], 4), ALU.mult))
                own()
                inc(dve.tensor_tensor(B["XT"], over(ident, 4), B["Y"], ALU.subtract), f"XT{c}.0")

            def attn(c):
                B = buf[c]
                inc(dve.tensor_tensor(by2(B["attn"]), two(half(bank(c, 3), 0)), by2(B["dec"]), ALU.mult))

            def keys(c, name, scale):
                inc(dve.tensor_tensor(by2(buf[c][name]), two(half(bank(c, 3), 1)), by2(down(scale, P)), ALU.mult), f"{name}{c}")

            for l in range(1, L1):
                for c in CHUNKS:
                    B = buf[c]
                    if l < TOP:
                        dve.wait_ge(*S.at("scan_pe", f"XX{c}.{l}", g))
                        inc(dve.tensor_tensor(B["X"], B["X"], tile4(bank(c, 1)), ALU.subtract), f"X{c}.{l}")
                    dve.wait_ge(*S.at("scan_pe", f"XXT{c}.{l}", g))
                    inc(dve.tensor_tensor(B["XT"], B["XT"], tile4(bank(c, 2)), ALU.subtract), f"XT{c}.{l}")
                if l == 1:
                    attn(1)
                    attn(2)
                elif l == 2:
                    inc(dve.tensor_copy(St, St0[:, :, :].rearrange("p (g h) n -> p g h n", h=4)[:, g, :, :]))
                    own()
                    last_token = TILES[1][0] + P - 1
                    inc(dve.tensor_tensor(St2, St, bc[:, 12:16, last_token:last_token + 1].broadcast_to([P, 4, P]), ALU.mult), "decayed")
                elif l == 3:
                    for c in CHUNKS:
                        keys(c, "nkbe", cb[:, c, g, :])
                elif l == 4:
                    for c in CHUNKS:
                        keys(c, "ktl", cv[:, c, 2, g, :])
                    if not last:
                        ahead_kn(dve, g + 1)
                elif l == 5 and not last:
                    ahead_diff(dve, g + 1)
            dve.wait_ge(*S.at("scan_pe", "S", g))
            inc(dve.tensor_tensor(St2, St2, tile4(bank(1, 3)), ALU.add), "S")

        def group_act(act, g, last):
            inc = lambda ins, step=None: S.inc(ins, "scan_act", step)
            S.begin("scan_act")
            cv = colv[:, :, :, :].rearrange("p c q (g h) -> p c q g h", h=4)
            for c in CHUNKS:
                B = buf[c]
                act.wait_ge(*S.at("scan_pe", f"tok{c}", g))
                for h in range(4):
                    ins = act.activation(B["vb"][:, h, :], bank(c, 1)[:, h * P:(h + 1) * P], ACT.Copy, scale=cv[:, c, 0, g, h:h + 1])
                inc(ins, f"vb{c}")
                act.wait_ge(*S.at("scan_pe", f"X{c}", g))
                inc(act.activation(B["X"], tile4(bank(c, 2)), ACT.Copy), f"X{c}")
            for l in range(1, L1):
                for c in CHUNKS:
                    act.wait_ge(*S.at("scan_pe", f"Y{c}.{l}", g))
                    inc(act.activation(buf[c]["Y"], tile4(bank(c, 0)), ACT.Copy), f"Y{c}.{l}")
                if l == 3 and not last:
                    ahead_v(act, g + 1)
            if not last:
                ahead_exp(act, g + 1)
            for c in CHUNKS:
                act.wait_ge(*S.at("scan_pe", f"wT{c}", g))
                inc(act.activation(buf[c]["Am"], tile4(bank(c, 0)), ACT.Copy), f"wT{c}")
            for c in CHUNKS:
                t0, n = TILES[c]
                act.wait_ge(*S.at("scan_pe", f"vn{c}", g))
                inc(act.activation(buf[c]["X"], tile4(bank(c, 1)), ACT.Copy), f"vn{c}")
                act.wait_ge(*S.at("scan_pe", f"o{c}", g))
                dst = work[:, 16 * T:32 * T].rearrange("p (g h t) -> p g h t", h=4, t=T)[:, g, :, t0:t0 + n]
                ins = act.activation(dst, tile4(bank(c, 2)), ACT.Copy)
                if c == 1:
                    inc(ins, "o1")
                else:
                    ins.then_inc(S.sem("group_out"), 1)

        def group_pe(pe, g):
            inc = lambda ins, step=None: S.inc(ins, "scan_pe", step)
            S.begin("scan_pe")
            H4 = range(4)
            col = lambda h: slice(h * P, (h + 1) * P)
            pe.wait_ge(*S.at("ahead_dve", "kn", g))
            pe.wait_ge(*S.at("ahead_act", "v", g))
            for c in CHUNKS:
                t0, n = TILES[c]
                for h in range(2):
                    mm = pe.matmul(bank(c, 0)[:, col(h)], kn[:, h, t0:t0 + n], kn[:, h, t0:t0 + n], start=True, stop=True)
                inc(mm, f"kk{c}")
            for c in CHUNKS:
                t0, n = TILES[c]
                for h in H4:
                    mm = pe.transpose(bank(c, 1)[:, col(h)], vs[:, h, t0:t0 + n], ident)
                inc(mm, f"tok{c}")
                for h in range(2):
                    pe.matmul(bank(c, 3)[:, col(h)], kn[:, h, t0:t0 + n], qn[:, h, t0:t0 + n], start=True, stop=True)
                    pe.transpose(bank(c, 3)[:, col(2 + h)], kn[:, h, t0:t0 + n], ident)
            pe.wait_ge(S.sem("group_out"), g + 1)
            for c in CHUNKS:
                pe.wait_ge(*S.at("scan_dve", f"XT{c}.0", g))
                for h in H4:
                    mm = pe.transpose(bank(c, 2)[:, col(h)], buf[c]["XT"][:, h, :], ident)
                inc(mm, f"X{c}")
            for l in range(1, L1):
                for c in CHUNKS:
                    B = buf[c]
                    pe.wait_ge(*S.at("scan_pool", f"Am{c}.{l}", g))
                    if l == 1:
                        pe.wait_ge(*S.at("scan_act", f"X{c}", g))
                    else:
                        pe.wait_ge(*S.at("scan_dve", f"X{c}.{l - 1}", g))
                    for h in H4:
                        mm = pe.matmul(bank(c, 0)[:, col(h)], B["Am"][:, h, :], B["X"][:, h, :], start=True, stop=True)
                    inc(mm, f"Y{c}.{l}")
                for c in CHUNKS:
                    B = buf[c]
                    pe.wait_ge(*S.at("scan_act", f"Y{c}.{l}", g))
                    pe.wait_ge(*S.at("scan_dve", f"XT{c}.{l - 1}", g))
                    if l < TOP:
                        for h in H4:
                            mm = pe.matmul(bank(c, 1)[:, col(h)], B["XT"][:, h, :], B["Y"][:, h, :], start=True, stop=True)
                        inc(mm, f"XX{c}.{l}")
                    for h in H4:
                        mm = pe.matmul(bank(c, 2)[:, col(h)], B["Y"][:, h, :], B["XT"][:, h, :], start=True, stop=True)
                    inc(mm, f"XXT{c}.{l}")
            for c in CHUNKS:
                pe.wait_ge(*S.at("scan_dve", f"XT{c}.{TOP}", g))
                for h in H4:
                    mm = pe.matmul(bank(c, 0)[:, col(h)], buf[c]["nkbe"][:, h, :], buf[c]["XT"][:, h, :], start=True, stop=True)
                inc(mm, f"wT{c}")
            for c in CHUNKS:
                B, state = buf[c], St if c == 1 else St2
                t0, n = TILES[c]
                pe.wait_ge(*S.at("scan_act", f"wT{c}", g))
                if c == 2:
                    pe.wait_ge(*S.at("scan_dve", "S", g))
                for h in H4:
                    pe.matmul(bank(c, 1)[:, col(h)], B["XT"][:, h, :], B["vb"][:, h, :], start=True, stop=False)
                    mm = pe.matmul(bank(c, 1)[:, col(h)], B["Am"][:, h, :], state[:, h, :], start=False, stop=True)
                inc(mm, f"vn{c}")
                pe.wait_ge(*S.at("scan_act", f"vn{c}", g))
                if c == 1:
                    for h in H4:
                        mm = pe.matmul(bank(c, 3)[:, col(h)], B["ktl"][:, h, :], B["X"][:, h, :], start=True, stop=True)
                    inc(mm, "S")
                pe.wait_ge(*S.at("scan_pool", "qd", g))
                for h in H4:
                    pe.matmul(bank(c, 2)[:, col(h)], state[:, h, :], qd[:, h, t0:t0 + n], start=True, stop=False)
                    mm = pe.matmul(bank(c, 2)[:, col(h)], B["X"][:, h, :], B["attn"][:, h, :], start=False, stop=True)
                inc(mm, f"o{c}")

        GROUPS = 4

        def scan_pool(pool):
            first_pool(pool)
            ahead_beta(pool, 0)
            with pool.Fori(0, GROUPS - 1) as g:
                group_pool(pool, g, False)
            group_pool(pool, GROUPS - 1, True)

        def scan_dve(dve):
            first_dve(dve)
            ahead_kn(dve, 0)
            ahead_diff(dve, 0)
            with dve.Fori(0, GROUPS - 1) as g:
                group_dve(dve, g, False)
            group_dve(dve, GROUPS - 1, True)

        def scan_act(act):
            act.preload_act_table(ACT.Exp)
            ahead_v(act, 0)
            first_act(act)
            ahead_exp(act, 0)
            with act.Fori(0, GROUPS - 1) as g:
                group_act(act, g, False)
            group_act(act, GROUPS - 1, True)

        def scan_pe(pe):
            first_pe(pe)
            pe.wait_ge(*S.at("first_dve", "S"))
            pe.wait_ge(*S.at("first_act", "S"))
            with pe.Fori(0, GROUPS - 1) as g:
                group_pe(pe, g)
            group_pe(pe, GROUPS - 1)

        def scan_done(eng):
            eng.wait_ge(S.sem("group_out"), GROUPS + 1)
            eng.wait_ge(*S.at("scan_dve", "S", GROUPS - 1))
            eng.wait_ge(*S.at("scan_pool", turn=GROUPS - 1))

        def gate_pool(pool):
            pool.wait_ge(*S.at("rown_dve", "rows", 1))
            pool.dma_start(scr_o, rrow[:, 0, :]).then_inc(S.sem("o_rows_out"), 16)
            pool.wait_ge(S.sem("o_rows_out"), 16)
            pool.dma_start(obc, on_all(scr_o, 0, (T, HV), (1, T))).then_inc(S.sem("o_rows_in"), 16)

        def gate_act(act):
            def body(un):
                un.ready(act)
                act.wait_ge(*S.at("gate_dve", turn=un.u))
                un.free(act.activation(zs[:, un.j % 4, :], un.bank()[:, 0:T], ACT.Silu))
            each_product(act, "gdn_z", 1, body, ACT.Silu, split="hi")

        def gate_dve(dve):
            def body(un):
                S.begin("gate_dve")
                dve.wait_ge(S.sem("o_rows_in"), 16)
                o = qkv[:, 16 + un.u, :]
                S.inc(dve.scalar_tensor_tensor(out=o, in0=o, scalar=pm("gdn_norm"), in1=obc[:, un.u, :], op0=ALU.mult, op1=ALU.mult), "gate_dve")
                S.own(dve, "gate_dve", un.u + 4)
                un.was_read(dve)
                S.inc(dve.tensor_tensor(o, o, zs[:, un.j % 4, :], ALU.mult), "gate_dve")
            each_product(dve, "gdn_z", 1, nothing, split="lo", late=body, lag=2)
            dve.wait_ge(*S.at("gate_dve", turn=15 + 4))

        def evac_mix_act(act, name, use):
            def body(un):
                un.ready(act)
                square(act, un.j, un.bank()[:, 0:T], T)
                un.free(act.activation(mix[:, un.j, :], un.bank()[:, 0:T], ACT.Copy))
            each_product(act, name, 1, body, turns=0, split="hi")

        def mix_was_read(eng, name):
            for j in range(4, 8):
                Unit(PLAN[name], 1, j, 0, 0).was_read(eng)

        def ffn_params(layer):
            at, n = PARAM_COLS["ffn_conv"]
            taps = Pm[:, at + n // 2 * layer:at + n // 2 * (layer + 1)].rearrange("p (b m t) -> p b m t", m=2, t=3)
            at, n = PARAM_COLS["ffn_bias"]
            return taps, Pm[:, at + n // 2 * layer:at + n // 2 * (layer + 1)].rearrange("p (b m) -> p b m", m=2)

        def conv_up_act(act, layer):
            taps, bias = ffn_params(layer)

            def project(un):
                p2 = un.j % 2
                act.wait_ge(*S.at("up_dve", turn=un.u + FB * layer))
                act.wait_ge(*S.at("up_pool", turn=un.u + FB * layer))
                for m in range(2):
                    un.ready(act, m)
                    act.activation(raw[p2][:, m, 2:T + 2], un.bank(m)[:, 0:T], ACT.Copy)
                    un.free(act.activation(y_gu[p2][:, m, :], un.bank(m)[:, 0:T], ACT.Identity, bias=bias[:, un.u, m:m + 1],
                                           scale=taps[:, un.u, m, 2:3]), m)

            def silu(un):
                S.begin("up_act")
                act.wait_ge(*S.at("up_dve", turn=un.u + FB * layer + 2))
                act.wait_ge(*S.at("up_pool", turn=un.u + FB * layer))
                S.inc(act.activation(silu_g[un.j % 2], y_gu[un.j % 2][:, 0, :], ACT.Silu), "up_act")
            each_product(act, f"up{layer}", 2, project, ACT.Silu, split="hi", late=silu, lag=1)

        def conv_up_dve(dve, layer):
            taps, bias = ffn_params(layer)

            def body(un):
                p2 = un.j % 2
                S.begin("up_dve")
                for t in range(2):
                    if t:
                        S.own(dve, "up_dve", un.u + FB * layer + 2)
                    for m in range(2):
                        if t == 0:
                            un.was_read(dve, m)
                        y = y_gu[p2][:, m, :]
                        S.inc(dve.scalar_tensor_tensor(out=y, in0=raw[p2][:, m, t:t + T], scalar=taps[:, un.u, m, t:t + 1], in1=y,
                                                       op0=ALU.mult, op1=ALU.add), "up_dve")
            each_product(dve, f"up{layer}", 2, body, split="lo")

        def conv_up_pool(pool, layer):
            def body(un):
                S.begin("up_pool")
                pool.wait_ge(*S.at("up_act", turn=un.u + 22 * layer + 2))
                turn = un.u + 22 * layer + 2
                h = h_new[un.j % 2]
                S.inc(pool.tensor_tensor(h, silu_g[un.j % 2], y_gu[un.j % 2][:, 1, :], ALU.mult), "up_pool")
                S.own(pool, "up_pool", turn)
                S.inc(pool.tensor_copy(hid_hi[:, un.u, :], h), "up_pool")
                S.own(pool, "up_pool", turn)
                S.inc(pool.tensor_tensor(hid_lo[:, un.u, :], h, hid_hi[:, un.u, :].bitcast(F32), ALU.subtract), "up_pool")
            each_product(pool, f"up{layer}", 2, body)
        MG = Unit(PLAN["ml_gates"], 1, 0, 0, 0)

        def ml_rows_act(act):
            inc = lambda ins, step=None: S.inc(ins, "mlr_act", step)
            act.wait_ge(*S.at("mlr_dve", "raw"))
            inc(act.activation(mrow[M_Y], mrow[M_Y], ACT.Tanh, scale=1.0 / 15.0))
            inc(act.activation(mrow[M_LI], mrow[M_LI], ACT.Tanh, scale=1.0 / 15.0), "tanh")
            S.own(act, "mlr_act")
            inc(act.activation(mrow[M_E], mrow[M_Y], ACT.Abs))
            S.own(act, "mlr_act")
            inc(act.activation(mrow[M_E], mrow[M_E], ACT.Exp, scale=-15.0))
            S.own(act, "mlr_act")
            inc(act.activation(mrow[M_E], mrow[M_E], ACT.Ln, bias=1.0), "ln")
            act.wait_ge(*S.at("mlr_dve", "m"))
            inc(act.activation(mrow[M_EM], mrow[M_T], ACT.Exp, scale=-1.0), "em")

        def ml_rows_dve(dve):
            inc = lambda ins, step=None: S.inc(ins, "mlr_dve", step)
            own = lambda: S.own(dve, "mlr_dve")
            MG.ready(dve)
            inc(dve.tensor_scalar(mrow[M_LI], MG.bank()[0:ML_H, 0:T], pm("ml_gate_i")[0:ML_H, :], None, ALU.add))
            own()
            MG.free(dve.tensor_scalar(mrow[M_T], MG.bank()[32:32 + ML_H, 0:T], pm("ml_gate_f")[0:ML_H, :], None, ALU.add))
            MG.was_read(dve)
            inc(dve.tensor_copy(mrow[M_Y], mrow[M_T]), "raw")
            inc(dve.memset(mrow[M_ONE], 1.0))
            dve.wait_ge(*S.at("mlr_act", "ln"))
            own()
            inc(dve.tensor_scalar(mrow[M_T], mrow[M_Y], 15.0, 0.0, ALU.mult, ALU.min))
            own()
            inc(dve.tensor_tensor(mrow[M_C], mrow[M_T], mrow[M_E], ALU.subtract))
            own()
            inc(dve.tensor_tensor_scan(mrow[M_B], mrow[M_ONE], mrow[M_C], 0.0, ALU.mult, ALU.add))
            own()
            inc(dve.scalar_tensor_tensor(out=mrow[M_C], in0=mrow[M_LI], scalar=15.0, in1=mrow[M_B], op0=ALU.mult, op1=ALU.subtract), "c")
            own()
            inc(dve.tensor_tensor_scan(mrow[M_M], mrow[M_ONE], mrow[M_C], 0.0, ALU.mult, ALU.max))
            own()
            inc(dve.tensor_tensor(mrow[M_T], mrow[M_B], mrow[M_M], ALU.add), "m")

        def ml_rows_pe(pe):
            pe.wait_ge(*S.at("mlr_dve", "c"))
            for c, (t0, n) in enumerate(TILES):
                mm = pe.transpose(PSB[0:n, c * ML_H:(c + 1) * ML_H], mrow[M_C][:, t0:t0 + n], ident[0:ML_H, 0:ML_H])
            S.inc(mm, "mlr_pe")

        def ml_cols_dve(dve):
            dve.wait_ge(*S.at("mlr_pe"))
            for c, (t0, n) in enumerate(TILES):
                S.inc(dve.tensor_copy(mcol[0:n, c, :], PSB[0:n, c * ML_H:(c + 1) * ML_H]), "mcol_dve")

        def ml_pool(pool):
            pool.wait_ge(*S.at("mlr_act", "em"))
            pool.dma_start(scr_m[0:ML_H, :], mrow[M_M]).then_inc(S.sem("ml_rows_out"), 16)
            pool.dma_start(scr_m[ML_H:2 * ML_H, :], mrow[M_EM]).then_inc(S.sem("ml_rows_out"), 16)
            pool.wait_ge(S.sem("ml_rows_out"), 32)
            pool.dma_start(bc2, on_all(scr_m, 0, (ML_H * T, 2), (T, ML_H), (1, T))).then_inc(S.sem("ml_rows_in"), 16)

        def ml_in_act(act):
            def body(un):
                un.ready(act)
                un.free(act.activation(mlT[:, un.u, :], un.bank()[:, 0:T], ACT.Copy if un.j < 16 else ACT.Sigmoid))
            each_product(act, "ml_in", 1, body, turns=2, split="hi")

        def ml_read(eng, last):
            for j in range(last - 4, last):
                Unit(PLAN["ml_in"], 1, j, 0, 0).was_read(eng)

        def ml_scores(h, c):
            bank4 = ps[4 * (h % 2):4 * (h % 2) + 4]
            return (bank4[3][:, 0:T], bank4[0][:, 0:2 * P], bank4[0][:, 2 * P:3 * P])[c]

        def ml_pe(pe):
            inc = lambda ins, step=None: S.inc(ins, "ml_pe", step)
            ml_read(pe, 24)
            for c, (t0, n) in enumerate(TILES):
                for k in range(8):
                    mm = pe.transpose(ps[4 + k // 4][0:n, (k % 4) * P:(k % 4 + 1) * P], mlT[:, 8 + k, t0:t0 + n], ident)
                    if k % 4 == 3:
                        inc(mm, f"v{c}.{k // 4}")
                if c < 2:
                    pe.wait_ge(*S.at("ml_act", f"v{c}.1"))
            pe.wait_ge(*S.at("ml_act", "v2.1"))
            def scores(h):
                if h >= 2:
                    pe.wait_ge(*S.at("ml_dve", f"h{h - 2}"))
                for c, (t0, n) in enumerate(TILES):
                    out = ml_scores(h, c)
                    inc(pe.matmul(out[0:n, :], mlT[:, 4 + h, t0:t0 + n], mlT[:, h, t0:T], start=True, stop=True), f"S{h}.{c}")
            scores(0)
            for h in range(ML_H):
                if h + 1 < ML_H:
                    scores(h + 1)
                bank4 = ps[4 * (h % 2):4 * (h % 2) + 4]
                for c, (t0, n) in enumerate(TILES):
                    if c == 0:
                        pe.wait_ge(*S.at("ml_dve", f"P{h}.2"))
                    Pm_ = Pt[h % 2][c][0:n, 0:T - t0]
                    kw = dict(start=(c == 0), stop=(c == 2))
                    pe.matmul(bank4[1][:, t0:T], v_tok[0:n, c, 2 * h, :], Pm_, **kw)
                    pe.matmul(bank4[2][:, t0:T], v_tok[0:n, c, 2 * h + 1, :], Pm_, **kw)
                    mm = pe.matmul(bank4[3][:, t0:T], ones[0:n, :], Pm_, **kw)
                inc(mm, f"num{h}")

        def ml_act(act):
            inc = lambda ins, step=None: S.inc(ins, "ml_act", step)
            for c, (t0, n) in enumerate(TILES):
                for q in range(2):
                    act.wait_ge(*S.at("ml_pe", f"v{c}.{q}"))
                    inc(act.activation(v_tok[0:n, c, 4 * q:4 * q + 4, :], tile4(ps[4 + q][0:n, :]), ACT.Copy), f"v{c}.{q}")
            for h in range(ML_H):
                for c, (t0, n) in enumerate(TILES):
                    act.wait_ge(*S.at("ml_dve", f"D{h}.{c}"))
                    w = Wt[h % 2][c][0:n, 0:T - t0]
                    inc(act.activation(w, w, ACT.Exp, bias=mcol[0:n, c, h:h + 1]), f"W{h}.{c}")

        def ml_dve(dve):
            inc = lambda ins, step=None: S.inc(ins, "ml_dve", step)
            own = lambda: S.own(dve, "ml_dve")
            dve.wait_ge(S.sem("ml_rows_in"), 16)
            S.own(dve, "mcol_dve")

            def distances(h):
                for c, (t0, n) in enumerate(TILES):
                    inc(dve.scalar_tensor_tensor(out=Wt[h % 2][c][0:n, 0:T - t0], in0=bc2[0:n, 0, h, t0:T], scalar=-1.0,
                                                 in1=cn("causal")[0:n, 0:T - t0], op0=ALU.mult, op1=ALU.add), f"D{h}.{c}")

            distances(0)
            for h in range(ML_H):
                for c, (t0, n) in enumerate(TILES):
                    dve.wait_ge(*S.at("ml_pe", f"S{h}.{2 if c else 0}"))
                    dve.wait_ge(*S.at("ml_act", f"W{h}.{c}"))
                    inc(dve.scalar_tensor_tensor(out=Pt[h % 2][c][0:n, 0:T - t0], in0=ml_scores(h, c)[0:n, :], scalar=P ** -0.5,
                                                 in1=Wt[h % 2][c][0:n, 0:T - t0], op0=ALU.mult, op1=ALU.mult), f"P{h}.{c}")
                if h + 1 < ML_H:
                    own()
                    distances(h + 1)
                dve.wait_ge(*S.at("ml_pe", f"num{h}"))
                own()
                dn = ps[4 * (h % 2) + 3][:, 0:T]
                inc(dve.scalar_tensor_tensor(out=den[:, 0, :], in0=dn, scalar=-1.0, in1=bc2[:, 1, h, :], op0=ALU.mult, op1=ALU.max))
                own()
                inc(dve.tensor_tensor(den[:, 0, :], den[:, 0, :], dn, ALU.max))
                own()
                inc(dve.reciprocal(den[:, 1, :], den[:, 0, :]))
                own()
                inc(dve.tensor_tensor(hT[:, 2 * h, :], ps[4 * (h % 2) + 1][:, 0:T], den[:, 1, :], ALU.mult))
                inc(dve.tensor_tensor(hT[:, 2 * h + 1, :], ps[4 * (h % 2) + 2][:, 0:T], den[:, 1, :], ALU.mult), f"h{h}")
            own()

        def ml_norm_pool(pool):
            pool.wait_ge(*S.at("rown_dve", "rows", 2))
            pool.dma_start(scr_h, rrow[0:ML_H, 0, :]).then_inc(S.sem("ml_norm_out"), 16)
            pool.wait_ge(S.sem("ml_norm_out"), 16)
            pool.dma_start(mbc, on_all(scr_h, 0, (T, ML_H), (1, T))).then_inc(S.sem("ml_norm_in"), 16)

        def ml_gate_dve(dve):
            S.inc(dve.tensor_tensor(mlT[:, 16:24, :], hT, mlT[:, 16:24, :], ALU.mult), "mlg_dve")

        def ml_norm_dve(dve):
            dve.wait_ge(S.sem("ml_norm_in"), 16)
            S.own(dve, "mlg_dve")
            for k in range(8):
                S.inc(dve.scalar_tensor_tensor(out=hT[:, k, :], in0=mlT[:, 16 + k, :], scalar=pm("ml_norm", k), in1=mbc[:, k // 2, :],
                                               op0=ALU.mult, op1=ALU.mult), "mln_dve", k)

        h2 = hs[:, :, META:T]
        memn = area(4096, DB, SEQ)
        kmem = mix[:, :, :].rearrange("p a b -> p (a b)")[:, 0:1024].rearrange("p (a b) -> p a b", b=SEQ)
        vmem = mix[:, :, :].rearrange("p a b -> p (a b)")[:, 1024:2048].rearrange("p (a b) -> p a b", b=512)
        keep_at = 6144
        hid2_hi, hid2_lo = (area(keep_at + i * FB * SEQ, FB, SEQ, of=work_r) for i in range(2))
        sg2 = [area(keep_at + 2 * FB * SEQ + i * SEQ, SEQ) for i in range(4)]
        h2_new = mix[:, 0:4, 0:SEQ]

        def mem_pool(pool):
            pool.wait_ge(*S.at("norm_add", 7, 3))
            pool.dma_start(memn, mem_t.rearrange("(k p) t -> p k t", p=P)).then_inc(S.sem("mem_in"), 16)

        def mem_squares(act):
            act.wait_ge(S.sem("mem_in"), 16)
            for k in range(DB):
                square(act, k, memn[:, k, :], SEQ, "mem")

        def mem_k_act(act):
            for j in range(4):
                un = Unit(PLAN["mem_k"], 1, j, 0, 0)
                un.ready(act)
                un.free(act.activation(kmem[:, j, :], un.bank()[:, 0:SEQ], ACT.Copy))

        def mem_v_act(act, j):
            un = Unit(PLAN["mem_v"], 1, j, 0, 0)
            un.ready(act)
            un.free(act.activation(vmem[:, j % 2, j // 2 * SEQ:(j // 2 + 1) * SEQ], un.bank()[:, 0:SEQ], ACT.Copy))

        def mem_v_pe(pe, j):
            ph = PLAN["mem_v"]
            n, b = ph.slab0 + j // 2, ph.product0 + j
            pe.wait_ge(weights_in[n % SLOTS], 16 * (n // SLOTS + 1))
            pe.wait_ge(bank_free[b % BANKS], b // BANKS + 1)
            for k in range(8):
                mm = pe.matmul(ps[b % BANKS][:, 0:SEQ], memn[:, k, j % 2 * P:(j % 2 + 1) * P], ring[:, n % SLOTS, k * SEQ:(k + 1) * SEQ],
                               start=(k == 0), stop=(k == 7))
            mm.then_inc(product_done, 1)

        def up_act(act, name):
            def body(un):
                un.ready(act)
                un.was_read(act, 1, before=8)
                un.free(act.activation(sg2[un.j % 4], un.bank()[:, 0:SEQ], ACT.Silu))
            each_product(act, name, 2, body, ACT.Silu, split="hi")

        def up_dve(dve, name):
            def body(un):
                un.ready(dve, 1)
                un.was_read(dve, 0)
                dve.wait_ge(*S.at("hid_pool", turn=un.u + (FB if name == "up3" else 0)))
                un.free(dve.tensor_tensor(h2_new[:, un.j % 4, :], un.bank(1)[:, 0:SEQ], sg2[un.j % 4], ALU.mult), 1)
            each_product(dve, name, 2, body, split="lo")

        def up_pool2(pool, name):
            def body(un):
                turn = un.u + (FB if name == "up3" else 0) + 4
                h = h2_new[:, un.j % 4, :]
                un.was_read(pool, 1)
                S.begin("hid_pool")
                S.inc(pool.tensor_copy(hid2_hi[:, un.u, :], h), "hid_pool")
                S.own(pool, "hid_pool", turn)
                S.inc(pool.tensor_tensor(hid2_lo[:, un.u, :], h, hid2_hi[:, un.u, :].bitcast(F32), ALU.subtract), "hid_pool")
            each_product(pool, name, 2, body)

        def hidden_input(pe, hi, lo, n, sem, turn0):
            def arrive(k):
                if k == 0:
                    pe.wait_ge(*S.at(sem, turn=turn0 + FB - 4))
                elif k > FB - 4:
                    pe.wait_ge(*S.at(sem, turn=turn0 + k))
            return split_input(pe, hi, lo, n, arrive)

        def down_dve(dve, name):
            each_product(dve, name, 1, lambda un: (
                un.ready(dve), un.free(dve.scalar_tensor_tensor(out=h2[:, un.u, :], in0=un.bank()[:, 0:SEQ], scalar=0.5,
                                                                in1=h2[:, un.u, :], op0=ALU.mult, op1=ALU.add))), split="lo")

        def residual_squares(act, name, split):
            each_product(act, name, 1, lambda un: (un.was_read(act), square(act, un.j, h2[:, un.j, :], SEQ)), turns=0, split=split)

        def phase_read(eng, name, upto=None):
            ph = PLAN[name]
            total = ph.products if upto is None else upto
            for j in range(max(0, total - 4), total):
                Unit(ph, 1, j, 0, 0).was_read(eng)

        u_at = 6144
        uT = area(u_at, 4, SEQ)
        vT = area(u_at + 1024, 4, SEQ)
        cqT = area(u_at + 2048, 4, SEQ)
        qmT = area(u_at + 3072, MEM_H, SEQ)
        ckvT = area(u_at + 4096, 2, SEQ)
        gat = area(u_at + 4608, 24, SEQ)
        br_at = u_at + 4608 + 6144
        yT = [area(br_at + i * 1024, 4, SEQ) for i in range(3)]
        t_at = br_at + 3072
        sq2 = sq[:, :, :].rearrange("p a b -> p (a b)")
        mix2 = mix[:, :, :].rearrange("p a b -> p (a b)")
        a2 = a[:, :, :].rearrange("p a b -> p (a b)")

        def in_act(act):
            for name, fn, dst in (("in_uv", ACT.Gelu, lambda j: (uT if j < 4 else vT)[:, j % 4, :]),
                                  ("in_cq_kr", ACT.Copy, lambda j: cqT[:, j, :]),
                                  ("in_qm", ACT.Copy, lambda j: qmT[:, j, :]),
                                  ("in_ckv", ACT.Copy, lambda j: ckvT[:, j, :])):
                each_product(act, name, 1, lambda un, fn=fn, dst=dst: (
                    un.ready(act), un.free(act.activation(dst(un.j), un.bank()[:, 0:SEQ], fn))), turns=0, split="hi")
            mem_squares(act)
            each_product(act, "in_gates", 1, lambda un: (
                un.ready(act), un.free(act.activation(gat[:, un.j, :], un.bank()[:, 0:SEQ], ACT.Sigmoid, bias=pm("b_gate", un.j)))),
                split="hi", between=lambda j: sg_act(act, j))

        Wsg = area(0, 8, P)
        sg_tok = area(1024, 2, 512)
        sg_bt = area(2048, 4, P)
        vln = mix2[:, 0:1024].rearrange("p (a b) -> p a b", b=SEQ)
        rstat = mix2[:, 1024:2048].rearrange("p (a b) -> p a b", b=SEQ)

        def sg_pool(pool):
            pool.dma_start(Wsg, sg_w_t).then_inc(S.sem("sg_in"), 16)
            for half in range(2):
                pool.dma_start(sg_bt[64 * half:64 * half + 64, :, :],
                               bass.AP(sg_bias.tensor, half * P, [[0, 64], [2 * P, 4], [1, P]])).then_inc(S.sem("sg_in"), 16)


        def sg_pe(pe, slab):
            inc = lambda ins, step=None: S.inc(ins, "sg_pe", step)
            if slab == 1:
                norm_pe(pe, 0, 8, SEQ, kind="mem")
                phase_read(pe, "in_uv")
                for k in range(4):
                    mm = pe.matmul(PSA[:, 0:SEQ], ones, vT[:, k, :], start=(k == 0), stop=(k == 3))
                inc(mm, "mean")
            if slab == 3:
                pe.wait_ge(*S.at("sg_act", "squares"))
                for k in range(4):
                    mm = pe.matmul(PSB[:, 0:SEQ], ones, sq[:, k, 0:SEQ], start=(k == 0), stop=(k == 3))
                inc(mm, "var")
            if slab == 6:
                pe.wait_ge(*S.at("sg_dve", "vln"))
                pe.wait_ge(*S.at("mem_act", "rms"))
                for c in range(2):
                    for k in range(4):
                        mm = pe.transpose(ps[6 + c][:, k * P:(k + 1) * P], vln[:, k, c * P:(c + 1) * P], ident)
                    inc(mm, f"tok{c}")
            if slab == 8:
                pe.wait_ge(*S.at("sg_dve", "w"))
                for k in range(4):
                    if k == 0:
                        pe.wait_ge(*S.at("sg_act", "tok1"))
                    if k >= 2:
                        pe.wait_ge(*S.at("sg_dve", f"y{k - 2}"))
                    out = ps[4 + k % 2]
                    for c in range(2):
                        for q in range(2):
                            mm = pe.matmul(out[64 * q:64 * q + 64, c * P:(c + 1) * P], sg_tok[:, c, (2 * k + q) * 64:(2 * k + q + 1) * 64],
                                           Wsg[:, 2 * k + q, :], start=True, stop=True)
                    inc(mm, f"mix{k}")
            if slab == 10:
                pe.wait_ge(*S.at("sg_dve", "y3"))
                norm_pe(pe, 0, 3, SEQ, kind="cq")
                norm_pe(pe, 0, 2, SEQ, kind="ckv")

        def sg_act(act, slab):
            inc = lambda ins, step=None: S.inc(ins, "sg_act", step)
            latent = (("cq", 3, 384, lambda k: cqT[:, k, :]), ("ckv", 2, 256, lambda k: ckvT[:, k, :]))
            if slab == 2:
                act.wait_ge(*S.at("sg_dve", "centred"))
                inc(act.activation(sq[:, 0:4, 0:SEQ], vT, ACT.Square), "squares")
            if slab == 4:
                act.wait_ge(*S.at("sg_dve", "var"))
                inc(act.activation(rstat[:, 2, :], rstat[:, 1, :], ACT.Sqrt), "root")
            if slab == 5:
                norm_act(act, 0, None, 8, SEQ, D, kind="mem")
            if slab == 7:
                for c in range(2):
                    act.wait_ge(*S.at("sg_pe", f"tok{c}"))
                    inc(act.activation(sg_tok[:, c, :], ps[6 + c], ACT.Copy), f"tok{c}")
            if slab == 9:
                for kind, blocks, width, src in latent:
                    for k in range(blocks):
                        square(act, k, src(k), SEQ, kind)
            if slab == 11:
                for kind, blocks, width, src in latent:
                    norm_act(act, 0, None, blocks, SEQ, width, kind=kind)

        def sg_dve(dve, slab):
            inc = lambda ins, step=None: S.inc(ins, "sg_dve", step)
            own = lambda: S.own(dve, "sg_dve")
            if slab == 5:
                norm_dve(dve, 0, SEQ, lambda k: memn[:, k, :], gain("mem_norm"), lambda k: memn[:, k, :], 8, kind="mem")
            if slab == 2:
                dve.wait_ge(*S.at("sg_pe", "mean"))
                inc(dve.tensor_scalar(rstat[:, 0, :], PSA[:, 0:SEQ], 1.0 / 512, None, ALU.mult))
                own()
                inc(dve.tensor_tensor(vT, vT, rstat[:, 0, :].unsqueeze(1).broadcast_to([P, 4, SEQ]), ALU.subtract), "centred")
            if slab == 4:
                dve.wait_ge(*S.at("sg_pe", "var"))
                inc(dve.tensor_scalar(rstat[:, 1, :], PSB[:, 0:SEQ], 1.0 / 512, EPS, ALU.mult, ALU.add), "var")
                dve.wait_ge(*S.at("sg_act", "root"))
                inc(dve.reciprocal(rstat[:, 3, :], rstat[:, 2, :]))
                own()
                for k in range(4):
                    inc(dve.scalar_tensor_tensor(out=vln[:, k, :], in0=vT[:, k, :], scalar=pm("sg_g", k), in1=rstat[:, 3, :],
                                                 op0=ALU.mult, op1=ALU.mult))
                own()
                for k in range(4):
                    inc(dve.tensor_scalar(vln[:, k, :], vln[:, k, :], pm("sg_b", k), None, ALU.add), "vln" if k == 3 else None)
            if slab == 3:
                dve.wait_ge(S.sem("sg_in"), 48)
                inc(dve.tensor_tensor(Wsg, Wsg, cn("tri").unsqueeze(1).broadcast_to([P, 8, P]), ALU.mult), "w")
            if slab == 8:
                for k in range(4):
                    dve.wait_ge(*S.at("sg_pe", f"mix{k}"))
                    y = yT[0][:, k, :].rearrange("p (a b) -> p a b", b=P)
                    inc(dve.tensor_tensor(y, ps[4 + k % 2][:, 0:SEQ].rearrange("p (a b) -> p a b", b=P),
                                          sg_bt[:, k, :].unsqueeze(1).broadcast_to([P, 2, P]), ALU.add))
                    own()
                    inc(dve.tensor_tensor(yT[0][:, k, :], yT[0][:, k, :], uT[:, k, :], ALU.mult), f"y{k}")
                own()
            if slab == 9:
                rope_dve(dve)
            if slab == 11:
                norm_dve(dve, 0, SEQ, lambda k: cqT[:, k, :], gain("cq_norm"), lambda k: cqn[:, k, :], 3, kind="cq")
                norm_dve(dve, 0, SEQ, lambda k: ckvT[:, k, :], gain("ckv_norm"), lambda k: ckvn[:, k, :], 2, kind="ckv")

        cqn = mix2[:, 0:768].rearrange("p (a b) -> p a b", b=SEQ)
        ckvn = mix2[:, 768:1280].rearrange("p (a b) -> p a b", b=SEQ)
        trig = a2[:, 0:6 * SEQ].rearrange("p (a b) -> p a b", b=SEQ)
        pos_i = sb("pos_i", [P, SEQ], I32)
        qk16 = area(0, 16, SEQ)
        sq_q = area(u_at, 8, SEQ)
        sq_k = sq2[:, 0:2048].rearrange("p (a b) -> p a b", b=SEQ)
        vtk = area(t_at, 2, 512)
        prob = [area(t_at + 1024 + 512 * i, 512) for i in range(2)]
        probT = [area(t_at + 2048 + 512 * i, 512) for i in range(2)]
        soft = sb("soft", [P, 2, 4, 2])

        def rope_pool(pool):
            pool.dma_start(pos_i[0:QK, :], bass.AP(positions.tensor, 0, [[0, QK], [1, SEQ]])).then_inc(S.sem("pos_in"), 16)

        def rope_dve(dve):
            inc = lambda ins, step=None: S.inc(ins, "rope_dve", step)
            own = lambda: S.own(dve, "rope_dve")
            t = lambda i: trig[0:QK, i, :]
            dve.wait_ge(S.sem("pos_in"), 16)
            inc(dve.tensor_copy(t(1), pos_i[0:QK, :]))
            own()
            inc(dve.tensor_scalar(t(0), t(1), cn("inv_freq")[0:QK, :], None, ALU.mult))
            own()
            for i, quarter in ((2, 0.0), (3, 0.25)):
                inc(dve.tensor_scalar(t(1), t(0), 1.0 / (2 * np.pi), quarter, ALU.mult, ALU.add))
                own()
                inc(dve.tensor_scalar(t(4), t(1), ROUND, None, ALU.add))
                own()
                inc(dve.tensor_scalar(t(1), t(4), -ROUND, None, ALU.add))
                own()
                inc(dve.scalar_tensor_tensor(out=t(4), in0=t(1), scalar=-TWO_PI_HI, in1=t(0), op0=ALU.mult, op1=ALU.add))
                own()
                inc(dve.scalar_tensor_tensor(out=t(i), in0=t(1), scalar=-TWO_PI_LO, in1=t(4), op0=ALU.mult, op1=ALU.add))
                own()
                if quarter:
                    inc(dve.tensor_scalar(t(i), t(i), float(np.pi / 2), None, ALU.add))
                    own()
                inc(dve.tensor_scalar(t(i), t(i), PI_IN, -PI_IN, ALU.min, ALU.max), "args" if quarter else None)
                own()

        def rope_act(act):
            act.wait_ge(*S.at("rope_dve", "args"))
            S.inc(act.activation(trig[0:QK, 2:4, :], trig[0:QK, 2:4, :], ACT.Sin), "rope_act")

        MQ, MK, MV = PLAN["mla_q"], PLAN["mla_k"], PLAN["mla_v"]

        def mla_in_pe(pe):
            stream_pe(pe, "mla_q", lambda m, k: cqn[:, k, :], SEQ)
            pe.wait_ge(*S.at("ckv_dve", "k1", 0))
            stream_pe(pe, "mla_k", lambda m, k: ckvn[:, k, :], SEQ)
            slot = MV.slab0 % SLOTS
            pe.wait_ge(weights_in[slot], 16 * (MV.slab0 // SLOTS + 1))
            for m in range(2):
                b = MV.product0 + m
                pe.wait_ge(bank_free[b % BANKS], b // BANKS + 1)
                for k in range(2):
                    mm = pe.matmul(ps[b % BANKS][:, :], ckvn[:, k, m * P:(m + 1) * P], ring[:, slot, k * 512:(k + 1) * 512],
                                   start=(k == 0), stop=(k == 1))
                mm.then_inc(product_done, 1)
            rown_pe(pe, 3, lambda k: (sq_q if k < 8 else sq_k)[0:QK, k % 8, :], 16, 1, SEQ, 16)
            stream_pe(pe, "mem_k", lambda m, k: memn[:, k, :], SEQ)
            rown_pe(pe, 4, lambda k: mem_sq[:, k, :], 8, 1, SEQ, 8)
            for i in range(8):
                if i == 0:
                    pe.wait_ge(*S.at("mla_dve", "gained"))
                    pe.wait_ge(*S.at("rown_act", "root", 3))
                if i >= 2:
                    pe.wait_ge(*S.at("mla_dve", f"rope{i - 2}"))
                S.inc(pe.matmul(ps[4 + i % 2][0:QK, :], cn("rot")[0:QK, :], qk16[0:QK, 2 * i:2 * i + 2, :].rearrange("p a b -> p (a b)"),
                                start=True, stop=True), "mla_pe", f"rot{i}")

        def mla_in_act(act):
            inc = lambda ins, step=None: S.inc(ins, "mla_act", step)
            for h in range(8):
                un = Unit(MQ, 1, h, 0, 0)
                un.ready(act)
                inc(act.activation(sq_q[0:QK, h, :], un.bank()[0:QK, 0:SEQ], ACT.Square))
                un.free(act.activation(qk16[0:QK, h, :], un.bank()[0:QK, 0:SEQ], ACT.Identity, scale=pm("q_norm")[0:QK, :]))
            for h in range(8):
                Unit(MK, 1, h, 0, 0).was_read(act)
                inc(act.activation(sq_k[0:QK, h, :], qk16[0:QK, 8 + h, :], ACT.Square), "ksq" if h == 7 else None)
            for c in range(2):
                un = Unit(MV, 1, c, 0, 0)
                un.ready(act)
                un.free(act.activation(vtk[:, c, :], un.bank(), ACT.Copy))

        def mla_in_dve(dve):
            inc = lambda ins, step=None: S.inc(ins, "mla_dve", step)
            own = lambda: S.own(dve, "mla_dve")
            for h in range(8):
                un = Unit(MK, 1, h, 0, 0)
                un.ready(dve)
                un.free(dve.tensor_tensor(qk16[0:QK, 8 + h, :], un.bank()[0:QK, 0:SEQ], cqT[0:QK, 3, :], ALU.add))
            dve.wait_ge(*S.at("mla_act", "ksq"))
            inc(dve.tensor_scalar(qk16[0:QK, 8:16, :], qk16[0:QK, 8:16, :], pm("k_norm")[0:QK, :], None, ALU.mult), "gained")

        def mla_rope_dve(dve):
            inc = lambda ins, step=None: S.inc(ins, "mla_dve", step)
            own = lambda: S.own(dve, "mla_dve")
            dve.wait_ge(S.sem("mla_rows_in"), 32)
            dve.wait_ge(*S.at("rope_act"))
            both = lambda v: v.unsqueeze(1).broadcast_to([QK, 2, SEQ])
            for i in range(8):
                x = qk16[0:QK, 2 * i:2 * i + 2, :]
                tmp = prob[i % 2][0:QK, :].rearrange("p (a b) -> p a b", b=SEQ)
                dve.wait_ge(*S.at("mla_pe", f"rot{i}"))
                inc(dve.tensor_tensor(tmp, ps[4 + i % 2][0:QK, :].rearrange("p (a b) -> p a b", b=SEQ), both(trig[0:QK, 2, :]), ALU.mult), f"rope{i}")
                inc(dve.tensor_tensor(x, x, both(trig[0:QK, 3, :]), ALU.mult))
                own()
                inc(dve.tensor_tensor(x, x, tmp, ALU.add))
                own()
                if i == 3:
                    rown_dve(dve, 4, SEQ, 8)
                inc(dve.tensor_tensor(x, x, (sq_q if i < 4 else sq_k)[0:QK, 2 * i % 8:2 * i % 8 + 2, :], ALU.mult), "heads" if i == 7 else None)
            own()

        def mla_pool(pool):
            pool.wait_ge(*S.at("rown_dve", "rows", 3))
            pool.dma_start(scr_q, rrow[:, 0, 0:SEQ]).then_inc(S.sem("mla_rows_out"), 16)
            pool.wait_ge(S.sem("mla_rows_out"), 16)
            pool.dma_start(sq_q, on_all(scr_q, 0, (SEQ, 8), (1, SEQ))).then_inc(S.sem("mla_rows_in"), 16)
            pool.dma_start(sq_k, on_all(scr_q, 8 * SEQ, (SEQ, 8), (1, SEQ))).then_inc(S.sem("mla_rows_in"), 16)

        mem_sq = area(br_at + 1024, 8, SEQ)

        def memq_act(act):
            rown_act(act, 4, [(qmT, mem_sq[:, 0:4, :]), (kmem, mem_sq[:, 4:8, :])], SEQ, 8, 1.0 / P, cn("eps"))

        def memq_dve(dve):
            dve.wait_ge(S.sem("mem_rows_in"), 16)
            for h in range(4):
                for x, gain, off in ((qmT, "mq_norm", 0), (kmem, "mk_norm", 4)):
                    S.inc(dve.scalar_tensor_tensor(out=x[:, h, :], in0=x[:, h, :], scalar=pm(gain), in1=sq_q[:, off + h, :],
                                                   op0=ALU.mult, op1=ALU.mult), "memq_dve")
            S.own(dve, "memq_dve")

        def memq_pool(pool):
            pool.wait_ge(*S.at("rown_dve", "rows", 4))
            pool.wait_ge(*S.at("mla_dve", "heads"))
            pool.dma_start(scr_c, rrow[0:8, 0, 0:SEQ]).then_inc(S.sem("mem_rows_out"), 16)
            pool.wait_ge(S.sem("mem_rows_out"), 16)
            pool.dma_start(sq_q, on_all(scr_c, 0, (SEQ, 8), (1, SEQ))).then_inc(S.sem("mem_rows_in"), 16)

        def attention(eng, engine, kind):
            causal = kind == "mla"
            H = MLA_H if causal else MEM_H
            scale = (QK if causal else P) ** -0.5
            rows = QK if causal else P
            inc = lambda ins, step=None: S.inc(ins, f"{kind}att_{engine}", step)
            wait = lambda other, step: eng.wait_ge(*S.at(f"{kind}att_{other}", step))
            own = lambda: S.own(eng, f"{kind}att_{engine}")
            q = (lambda h: qk16[0:rows, h, :]) if causal else (lambda h: qmT[:, h, :])
            k = (lambda h: qk16[0:rows, 8 + h, :]) if causal else (lambda h: kmem[:, h, :])
            v = (lambda h, c: vtk[:, c, 64 * h:64 * h + 64]) if causal else (lambda h, c: vmem[:, c, P * h:P * h + P])
            part = ((0, P), (P, 3 * P)) if causal else ((0, 2 * P), (2 * P, 4 * P))
            end = part[1][1]

            def out(h):
                return (ps[7][64 * (h % 2):64 * (h % 2) + 64, 0:SEQ], yT[1][64 * (h % 2):64 * (h % 2) + 64, h // 2, :]) if causal \
                    else (ps[7][:, 0:SEQ], yT[2][:, h, :])

            if engine == "pe":
                def scores(h):
                    if h >= 2:
                        wait(*(("dve", f"read{h - 2}") if causal else ("act", f"e{h - 2}")))
                    for i, (lo, hi) in enumerate(part):
                        mm = eng.matmul(ps[4 + h % 2][:, lo:hi], q(h)[:, i * P:(i + 1) * P], k(h)[:, 0:hi - lo], start=True, stop=True)
                    inc(mm, f"s{h}")
                scores(0)
                for h in range(H):
                    if h + 1 < H:
                        scores(h + 1)
                    if causal and h < 4:
                        mem_v_pe(eng, h)
                    wait("dve", f"p{h}")
                    if h >= 1:
                        wait("act", f"pt{h - 1}")
                    for i in range(2):
                        for kt in range(2):
                            if causal and kt > i:
                                continue
                            mm = eng.transpose(ps[6][:, kt * SEQ + i * P:kt * SEQ + (i + 1) * P],
                                               prob[h % 2][:, part[i][0] + kt * P:part[i][0] + (kt + 1) * P], ident)
                    inc(mm, f"t{h}")
                    wait("act", f"pt{h}")
                    if h >= 1:
                        wait("act", f"o{h - 1}")
                    o, _ = out(h)
                    eng.matmul(o, v(h, 0), probT[h % 2][:, 0:SEQ], start=True, stop=False)
                    if causal:
                        mm = eng.matmul(o[:, P:SEQ], v(h, 1), probT[h % 2][:, SEQ + P:2 * SEQ], start=False, stop=True)
                    else:
                        mm = eng.matmul(o, v(h, 1), probT[h % 2][:, SEQ:2 * SEQ], start=False, stop=True)
                    inc(mm, f"pv{h}")
            if engine == "dve":
                for h in range(H + 1):
                    if h < H:
                        st = soft[:, h % 2]
                        wait("pe", f"s{h}")
                        if h >= 2:
                            wait("pe", f"t{h - 2}")
                        if causal:
                            inc(eng.tensor_tensor(prob[h % 2][:, 0:end], ps[4 + h % 2][:, 0:end], cn("score_mask"), ALU.add), f"read{h}")
                            own()
                            for i, (lo, hi) in enumerate(part):
                                inc(eng.tensor_reduce(st[:, 0, i:i + 1], prob[h % 2][:, lo:hi], AX_X, ALU.max))
                        else:
                            inc(eng.tensor_reduce(st[:, 0, :], ps[4 + h % 2].rearrange("p (a b) -> p a b", b=SEQ), AX_X, ALU.max))
                        own()
                        inc(eng.tensor_scalar(st[:, 1, :], st[:, 0, :], -scale, None, ALU.mult), f"n{h}")
                    if not causal and h == 1:
                        prepare(eng, "lo", "branches")
                    if not causal and h in (2, 3):
                        split_branch_dve(eng, h - 2)
                    if h >= 1:
                        g = h - 1
                        st = soft[:, g % 2]
                        wait("act", f"e{g}")
                        inc(eng.reciprocal(st[:, 3, :], st[:, 2, :]))
                        own()
                        for i, (lo, hi) in enumerate(part):
                            inc(eng.tensor_scalar(prob[g % 2][:, lo:hi], prob[g % 2][:, lo:hi], st[:, 3, i:i + 1], None, ALU.mult), f"p{g}" if i else None)
            if engine == "act":
                def finish(g):
                    wait("pe", f"t{g}")
                    if causal:
                        inc(eng.activation(probT[g % 2][:, 0:SEQ], ps[6][:, 0:SEQ], ACT.Copy))
                        inc(eng.activation(probT[g % 2][:, SEQ + P:2 * SEQ], ps[6][:, SEQ + P:2 * SEQ], ACT.Copy), f"pt{g}")
                    else:
                        inc(eng.activation(probT[g % 2], ps[6], ACT.Copy), f"pt{g}")
                    wait("pe", f"pv{g}")
                    o, dst = out(g)
                    inc(eng.activation(dst, o, ACT.Copy), f"o{g}")
                for h in range(H + 1):
                    if h < H:
                        st = soft[:, h % 2]
                        wait("dve", f"n{h}")
                        for i, (lo, hi) in enumerate(part):
                            src = prob[h % 2] if causal else ps[4 + h % 2]
                            inc(eng.activation(prob[h % 2][:, lo:hi], src[:, lo:hi], ACT.Exp, bias=st[:, 1, i:i + 1], scale=scale,
                                               accum_out=st[:, 2, i:i + 1]), f"e{h}" if i else None)
                    if h >= 1:
                        finish(h - 1)
                    if causal and 1 <= h <= 4:
                        mem_v_act(eng, h - 1)

        merged = area(u_at, 8, SEQ)
        M_HI, M_LO = area(u_at + 2048, 8, SEQ, of=work_r), area(t_at, 8, SEQ, of=work_r)
        Y_HI, Y_LO = area(0, 12, SEQ, of=work_r), area(3072, 12, SEQ, of=work_r)

        def split_branch_act(act, m):
            S.inc(act.activation(Y_HI[:, 4 * m:4 * m + 4, :], yT[m], ACT.Copy), "y_hi", m)

        def split_branch_dve(dve, m):
            dve.wait_ge(*S.at("y_hi", m))
            S.inc(dve.tensor_tensor(Y_LO[:, 4 * m:4 * m + 4, :], yT[m], Y_HI[:, 4 * m:4 * m + 4, :].bitcast(F32), ALU.subtract), "y_lo", m)

        gated = [[mix2[:, (2 * i + m) * SEQ:(2 * i + m + 1) * SEQ] for m in range(2)] for i in range(2)]

        def branches_dve(dve):
            def body(un):
                c = un.j
                if c >= 2:
                    dve.wait_ge(*S.at("merge_pool", c - 2))
                for m in range(3):
                    un.ready(dve, m)
                    un.free(dve.tensor_tensor(merged[:, c, :] if m == 0 else gated[c % 2][m - 1], un.bank(m)[:, 0:SEQ], gat[:, 8 * m + c, :],
                                              ALU.mult), m)
            each_product(dve, "branches", 3, body, turns=0, split="lo", split_last=True)

        def branches_pool(pool):
            for c in range(8):
                un = Unit(PLAN["branches"], 3, c, 0, 0)
                un.was_read(pool, 0)
                un.was_read(pool, 1)
                S.inc(pool.tensor_tensor(merged[:, c, :], merged[:, c, :], gated[c % 2][0], ALU.add), "merge_pool")
                un.was_read(pool, 2)
                S.own(pool, "merge_pool")
                S.inc(pool.tensor_tensor(merged[:, c, :], merged[:, c, :], gated[c % 2][1], ALU.add), "merge_pool", c)

        def mix_out_dve(dve):
            each_product(dve, "mix_out", 1, lambda un: (
                un.ready(dve), un.free(dve.tensor_tensor(h2[:, un.u, :], un.bank()[:, 0:SEQ], h2[:, un.u, :], ALU.add))), split="lo")

        block = ctx.enter_context(nc.Block())
        H1 = lambda k: hs[:, k, :]
        A1 = lambda k: a[:, k, :]
        M1 = lambda k: mix[:, k, :]
        H2 = lambda k: h2[:, k, :]
        A2 = lambda k: a[:, k, 0:SEQ]
        normed = lambda eng, use: (lambda k: eng.wait_ge(*S.at("norm_dve", f"k{k}", use)))

        @block.sync
        def _(sp):
            for half in range(2):
                rows = slice(half * D // 2, (half + 1) * D // 2)
                sp.dma_start(hs[:, half * DB // 2:(half + 1) * DB // 2, META:T],
                             x_t[rows, :].rearrange("(k p) t -> p k t", p=P)).then_inc(x_in[half], 16)
            sp.dma_start(Cn[:, :], consts).then_inc(S.sem("small_in"), 16)
            sp.dma_start(Pm[:, :], params).then_inc(S.sem("small_in"), 16)
            word = 0
            for n, ph in enumerate(SLAB_OF):
                size = ph.blocks * P
                if n - SLOTS in SPLIT_AT:
                    sp.wait_ge(lo_done, SPLIT_AT[n - SLOTS] + 1)
                elif n >= SLOTS:
                    sp.wait_ge(product_done, done_value(n - SLOTS))
                sp.dma_start(ring[:, n % SLOTS, 0:size],
                             stream[word:word + P * size].rearrange("(p c) -> p c", p=P)).then_inc(weights_in[n % SLOTS], 16)
                word += P * size
            phase_read(sp, "down3")
            sp.dma_start(out_t.rearrange("(k p) t -> p k t", p=P), h2).then_inc(S.sem("out_stored"), 16)
            sp.wait_ge(S.sem("out_stored"), 16)

        @block.gpsimd
        def _(pool):
            pool.dma_start(hs[:, :, 0:META], meta_t.rearrange("(k p) t -> p k t", p=P)).then_inc(S.sem("meta_in"), 16)
            scan_pool(pool)
            gate_pool(pool)
            conv_up_pool(pool, 0)
            ml_pool(pool)
            ml_norm_pool(pool)
            conv_up_pool(pool, 1)
            mem_pool(pool)
            up_pool2(pool, "up2")
            phase_read(pool, "down2")
            sg_pool(pool)
            rope_pool(pool)
            mla_pool(pool)
            memq_pool(pool)
            branches_pool(pool)
            up_pool2(pool, "up3")

        @block.scalar
        def _(act):
            act.wait_ge(S.sem("meta_in"), 16)
            act.wait_ge(S.sem("group_out"), 1)
            norm_act(act, 0, H1, 8, T, D, ready=lambda k: act.wait_ge(x_in[k // (DB // 2)], 16))
            split_act(act, 0, a, A_HI, 8, T, ready=normed(act, 0))
            prepare(act, "hi", "gdn_qkv")
            rows_act(act)
            qkv_act(act)
            act.wait_ge(*S.at("qkv_act", turn=31 + CONV_AHEAD))
            rown_act(act, 0, [(qkv[:, 0:16, :], sqh)], T, 16, cn("l2_scale")[0:16, :], cn("l2_eps"))
            scan_act(act)
            scan_done(act)
            rown_squares(act, [(qkv[:, 16:32, :], osq)])
            prepare(act, "hi", "gdn_z")
            split_act(act, 1, a, A_HI, 8, T)
            rown_act(act, 1, [], T, 16, 1.0 / P, cn("eps"))
            gate_act(act)
            split_act(act, 2, qkv[:, 16:32, :], O_HI, 16, T, ready=lambda k: act.wait_ge(*S.at("gate_dve", turn=k + 4)))
            evac_mix_act(act, "gdn_out", 1)
            for layer in range(2):
                if layer:
                    norm_act(act, 4, H1, 8, T, D, ready=lambda k: act.wait_ge(*S.at("norm_add", k, 1)))
                    split_act(act, 4, a, A_HI, 8, T, ready=normed(act, 4))
                    ml_rows_act(act)
                    ml_in_act(act)
                    ml_act(act)
                    act.wait_ge(*S.at("ml_dve"))
                    rown_act(act, 2, [(hT, hsq)], T, ML_H, 1.0 / 256, cn("eps"))
                    split_act(act, 5, hT, ML_HI, 8, T, ready=lambda k: act.wait_ge(*S.at("mln_dve", k)))
                    evac_mix_act(act, "ml_out", 5)
                norm_act(act, 1 + 4 * layer, None, 8, T, D)
                norm_act(act, 2 + 4 * layer, H1, 8, T, D, ready=lambda k: act.wait_ge(*S.at("norm_add", k, 2 * layer)))
                act.wait_ge(*S.at("ffn_zero", turn=layer))
                split_act(act, 3 + 3 * layer, a, A_HI, 8, T, ready=normed(act, 2 + 4 * layer))
                conv_up_act(act, layer)
                evac_mix_act(act, f"down{layer}", 3 + 4 * layer)
                norm_act(act, 3 + 4 * layer, None, 8, T, D)
            prepare(act, "hi", "up2")
            norm_act(act, 8, H2, 8, SEQ, D, ready=lambda k: act.wait_ge(*S.at("norm_add", k, 3)))
            split_act(act, 7, a, A_HI, 8, SEQ, ready=normed(act, 8))
            up_act(act, "up2")
            residual_squares(act, "down2", "hi")
            norm_act(act, 9, None, 8, SEQ, D)
            split_act(act, 8, a, A_HI, 8, SEQ, ready=normed(act, 9))
            in_act(act)
            rope_act(act)
            mla_in_act(act)
            rown_act(act, 3, [], SEQ, 16, 1.0 / QK, cn("eps"))
            mem_k_act(act)
            phase_read(act, "mem_k")
            memq_act(act)
            attention(act, "act", "mla")
            prepare(act, "hi", "branches")
            act.wait_ge(*S.at("mlaatt_act", "o7"))
            split_branch_act(act, 0)
            split_branch_act(act, 1)
            attention(act, "act", "mem")
            act.wait_ge(*S.at("mematt_act", "o3"))
            split_branch_act(act, 2)
            each_product(act, "branches", 3, nothing, split="hi")
            split_act(act, 9, merged, M_HI, 8, SEQ, ready=lambda k: act.wait_ge(*S.at("merge_pool", k)))
            residual_squares(act, "mix_out", "hi")
            norm_act(act, 10, None, 8, SEQ, D)
            split_act(act, 10, a, A_HI, 8, SEQ, ready=normed(act, 10))
            up_act(act, "up3")
            each_product(act, "down3", 1, nothing, split="hi")

        @block.vector
        def _(dve):
            for i in range(BANKS):
                dve.memset(rs[:, 0, 4 * i:4 * i + 4], 0.0).then_inc(bank_free[i], 1)
            dve.memset(raw_c[:, :, 0:3], 0.0).then_inc(S.sem("qkv_dve"), CONV_AHEAD * 3)
            dve.memset(rs[:, 0, 16:20], 0.0).then_inc(S.sem("qkv_act"), CONV_AHEAD)
            dve.memset(rs[:, 0, 20:24], 0.0).then_inc(S.sem("up_dve"), 2 * 4)
            dve.memset(rs[:, 0, 32:36], 0.0).then_inc(S.sem("gate_dve"), 4 * 2)
            dve.memset(rs[:, 0, 36:40], 0.0).then_inc(S.sem("hid_pool"), 4 * 2)
            dve.memset(rs[:, 0, 24:28], 0.0).then_inc(S.sem("up_act"), 2)
            dve.memset(rs[:, 0, 28:32], 0.0).then_inc(S.sem("up_pool"), 2 * 3)
            for i in range(BANKS):
                dve.wait_ge(bank_free[i], 1)
            dve.wait_ge(S.sem("up_pool"), 6)
            dve.wait_ge(S.sem("qkv_act"), CONV_AHEAD)
            dve.wait_ge(S.sem("gate_dve"), 8)
            dve.wait_ge(S.sem("hid_pool"), 8)
            dve.wait_ge(S.sem("up_act"), 2)
            dve.wait_ge(S.sem("up_dve"), 8)
            dve.memset(rs[:, 1, :], 0.0).then_inc(S.sem("group_out"), 1)
            dve.wait_ge(S.sem("group_out"), 1)
            dve.wait_ge(S.sem("small_in"), 32)
            for half in range(2):
                dve.wait_ge(x_in[half], 16)
            dve.wait_ge(S.sem("meta_in"), 16)
            norm_dve(dve, 0, T, H1, gain("norm_w", 0), A1, 8)
            split_dve(dve, 0, a, A_HI, A_LO, 8, T)
            prepare(dve, "lo", "gdn_qkv")
            rows_dve(dve)
            qkv_dve(dve)
            cols_dve(dve)
            rown_dve(dve, 0, T, 16)
            S.own(dve, "cols_dve")
            scan_dve(dve)
            prepare(dve, "lo", "gdn_z")
            split_dve(dve, 1, a, A_HI, A_LO, 8, T)
            rown_dve(dve, 1, T, 16)
            gate_dve(dve)
            split_dve(dve, 2, qkv[:, 16:32, :], O_HI, O_LO, 16, T)
            each_product(dve, "gdn_out", 1, nothing, split="lo")
            for layer in range(2):
                if layer:
                    norm_dve(dve, 4, T, H1, gain("norm_w", 4 * DB), A1, 8)
                    split_dve(dve, 4, a, A_HI, A_LO, 8, T)
                    ml_rows_dve(dve)
                    each_product(dve, "ml_in", 1, nothing, split="lo")
                    ml_cols_dve(dve)
                    ml_dve(dve)
                    ml_gate_dve(dve)
                    rown_dve(dve, 2, T, ML_H)
                    ml_norm_dve(dve)
                    split_dve(dve, 5, hT, ML_HI, ML_LO, 8, T)
                    each_product(dve, "ml_out", 1, nothing, split="lo")
                mix_was_read(dve, "gdn_out" if layer == 0 else "ml_out")
                norm_dve(dve, 1 + 4 * layer, T, M1, gain("norm_w", (4 * layer + 1) * DB), M1, 8, add=(2 * layer, H1))
                S.begin("ffn_zero")
                for i in range(2):
                    S.inc(dve.memset(raw[i][:, :, 0:2], 0.0), "ffn_zero")
                norm_dve(dve, 2 + 4 * layer, T, H1, gain("norm_w", (4 * layer + 2) * DB), A1, 8)
                split_dve(dve, 3 + 3 * layer, a, A_HI, A_LO, 8, T)
                conv_up_dve(dve, layer)
                each_product(dve, f"down{layer}", 1, nothing, split="lo")
                mix_was_read(dve, f"down{layer}")
                norm_dve(dve, 3 + 4 * layer, T, M1, gain("norm_w", (4 * layer + 3) * DB), M1, 8, add=(2 * layer + 1, H1))
            prepare(dve, "lo", "up2")
            norm_dve(dve, 8, SEQ, H2, gain("ffn1_norm"), A2, 8)
            split_dve(dve, 7, a, A_HI, A_LO, 8, SEQ)
            up_dve(dve, "up2")
            down_dve(dve, "down2")
            norm_dve(dve, 9, SEQ, H2, gain("mix_norm"), A2, 8)
            split_dve(dve, 8, a, A_HI, A_LO, 8, SEQ)
            for name in ("in_uv", "in_cq_kr", "in_qm", "in_ckv"):
                each_product(dve, name, 1, nothing, split="lo")
            phase_read(dve, "in_uv")
            each_product(dve, "in_gates", 1, nothing, split="lo", between=lambda j: sg_dve(dve, j))
            phase_read(dve, "in_gates")
            mla_in_dve(dve)
            rown_dve(dve, 3, SEQ, 16)
            mla_rope_dve(dve)
            attention(dve, "dve", "mla")
            memq_dve(dve)
            attention(dve, "dve", "mem")
            split_branch_dve(dve, 2)
            branches_dve(dve)
            split_dve(dve, 9, merged, M_HI, M_LO, 8, SEQ)
            mix_out_dve(dve)
            norm_dve(dve, 10, SEQ, H2, gain("ffn2_norm"), A2, 8)
            split_dve(dve, 10, a, A_HI, A_LO, 8, SEQ)
            up_dve(dve, "up3")
            down_dve(dve, "down3")

        @block.tensor
        def _(pe):
            from_a = lambda m, k: a[:, k, :]
            a_parts = lambda use, n: split_input(pe, A_HI, A_LO, n, by_step(pe, use))
            pe.wait_ge(S.sem("small_in"), 32)
            norm_pe(pe, 0, 8, T)
            pe.wait_ge(*S.at("norm_dve", "k7", 0))
            stream_pe(pe, "gdn_ba", from_a, T)
            stream_pe(pe, "gdn_qkv", a_parts(0, T), T)
            rows_pe(pe)
            rown_pe(pe, 0, lambda k: sqh[:, k, :], 16, 1, T, 16)
            scan_pe(pe)
            pe.wait_ge(S.sem("group_out"), GROUPS + 1)
            rown_pe(pe, 1, lambda k: osq[:, k, :], 16, 1, T, 16)
            stream_pe(pe, "gdn_z", a_parts(1, T), T)
            stream_pe(pe, "gdn_out", split_input(pe, O_HI, O_LO, T, by_step(pe, 2, per=2)), T)
            for layer in range(2):
                if layer:
                    norm_pe(pe, 4, 8, T)
                    pe.wait_ge(*S.at("norm_dve", "k7", 4))
                    stream_pe(pe, "ml_gates", from_a, T)
                    stream_pe(pe, "ml_in", a_parts(4, T), T)
                    ml_rows_pe(pe)
                    pe.wait_ge(*S.at("mcol_dve"))
                    ml_pe(pe)
                    rown_pe(pe, 2, lambda k: hsq[:, k, :], 8, 2, T, ML_H)
                    stream_pe(pe, "ml_out", split_input(pe, ML_HI, ML_LO, T, by_step(pe, 5)), T)
                norm_pe(pe, 1 + 4 * layer, 8, T)
                norm_pe(pe, 2 + 4 * layer, 8, T)
                stream_pe(pe, f"up{layer}", a_parts(3 + 3 * layer, T), T)
                stream_pe(pe, f"down{layer}", hidden_input(pe, hid_hi, hid_lo, T, "up_pool", FB * layer + 2), T)
                norm_pe(pe, 3 + 4 * layer, 8, T)
            norm_pe(pe, 8, 8, SEQ)
            stream_pe(pe, "up2", a_parts(7, SEQ), SEQ)
            stream_pe(pe, "down2", hidden_input(pe, hid2_hi, hid2_lo, SEQ, "hid_pool", 4), SEQ)
            norm_pe(pe, 9, 8, SEQ)
            in_x = a_parts(8, SEQ)
            for name in ("in_uv", "in_cq_kr", "in_qm", "in_ckv"):
                stream_pe(pe, name, in_x, SEQ)
            stream_pe(pe, "in_gates", in_x, SEQ, between=lambda j: sg_pe(pe, j))
            pe.wait_ge(*S.at("cq_dve", "k2", 0))
            mla_in_pe(pe)
            pe.wait_ge(*S.at("mla_dve", "heads"))
            phase_read(pe, "mla_k")
            phase_read(pe, "mla_v")
            attention(pe, "pe", "mla")
            pe.wait_ge(*S.at("memq_dve"))
            attention(pe, "pe", "mem")
            def branch_input(m, k):
                if k == 0:
                    pe.wait_ge(*S.at("y_lo", m))
                return Y_HI[:, 4 * m + k, :], Y_LO[:, 4 * m + k, :]
            stream_pe(pe, "branches", branch_input, SEQ)
            stream_pe(pe, "mix_out", split_input(pe, M_HI, M_LO, SEQ, by_step(pe, 9)), SEQ)
            norm_pe(pe, 10, 8, SEQ)
            stream_pe(pe, "up3", a_parts(10, SEQ), SEQ)
            stream_pe(pe, "down3", hidden_input(pe, hid2_hi, hid2_lo, SEQ, "hid_pool", FB + 4), SEQ)

    return S.seen


def stream_layout(w):
    parts = []

    def cat(columns_, kb, per_slab):
        blocks = np.stack([c.reshape(kb, P, P) for c in columns_])
        m = blocks.shape[0]
        blocks = blocks.reshape(m // per_slab, per_slab * kb, P, P).transpose(0, 2, 1, 3)
        parts.append(np.ascontiguousarray(blocks).reshape(-1))

    def split(x):
        return [x[:, i:i + P] for i in range(0, x.shape[1], P)]

    def pad(x, places):
        out = np.zeros((x.shape[0], P), x.dtype)
        for at, src in places:
            out[:, at:at + src.shape[1]] = src
        return out

    def ffn(up, down):
        g, u = split(up[:, :FF]), split(up[:, FF:])
        cat([b for pair in zip(g, u) for b in pair], DB, 2)
        cat([c[r:r + FF // 2] for c in split(down) for r in (0, FF // 2)], FB // 2, 1)

    gi = w["gdn_w_in"][0]
    qkv = 2 * HQ * P + HV * P
    cat([pad(gi, [(0, gi[:, qkv + HV * P:qkv + HV * P + HV]), (32, gi[:, qkv + HV * P + HV:])])], DB, 1)
    cat(split(gi[:, :qkv]), DB, 2)
    cat(split(gi[:, qkv:qkv + HV * P]), DB, 2)
    cat(split(w["gdn_w_out"][0]), HV, 1)
    ffn(w["ffn_w_up"][0], w["ffn_w_down"][0])
    mi = w["ml_w_in"][0]
    o4 = 2 * ML_H * P + 2 * ML_H * 256
    cat([pad(mi, [(0, mi[:, o4:o4 + ML_H]), (32, mi[:, o4 + ML_H:])])], DB, 1)
    cat(split(mi[:, :o4]), DB, 2)
    cat(split(w["ml_w_out"][0]), DB, 2)
    ffn(w["ffn_w_up"][1], w["ffn_w_down"][1])
    ffn(w["ffn1_w_gu_2"][0], w["ffn1_w_down_2"][0])
    wi = w["w_in_2"][0]
    cat(split(wi[:, 0:1024]), DB, 2)
    cat(split(wi[:, 1024:1408]) + [pad(wi, [(NOPE, wi[:, 1664:1696])])], DB, 2)
    cat(split(wi[:, 1696:2208]), DB, 2)
    cat(split(wi[:, 1408:1664]), DB, 2)
    cat(split(wi[:, 2208:]), DB, 2)
    uq, ukv = w["mla_w_uq_2"][0], w["mla_w_ukv_2"][0]
    cat([pad(uq, [(0, uq[:, QK * h:QK * (h + 1)])]) for h in range(MLA_H)], 3, 4)
    kpart = np.stack([pad(ukv, [(0, ukv[:, P * h:P * h + NOPE])]).reshape(2, P, P) for h in range(MLA_H)])
    kpart = kpart.reshape(16, P, P).transpose(1, 0, 2).reshape(P, 16 * P)
    vpart = ukv.reshape(2, P, MLA_H, 2, NOPE)[:, :, :, 1, :].reshape(2, P, 512).transpose(1, 0, 2).reshape(P, 1024)
    parts += [kpart.reshape(-1), vpart.reshape(-1)]
    mk = w["mem_w_kv_2"][0]
    cat(split(mk[:, :512]), DB, 2)
    parts.append(np.ascontiguousarray(mk[:, 512:].reshape(DB, P, 2, SEQ).transpose(2, 1, 0, 3)).reshape(-1))
    br = [split(w[n][0]) for n in ("w_branch_a_2", "w_branch_b_2", "w_branch_c_2")]
    cat([b[c] for c in range(DB) for b in br], 4, 3)
    cat(split(w["w_out_2"][0]), DB, 2)
    ffn(w["ffn2_w_gu_2"][0], w["ffn2_w_down_2"][0])
    out = np.concatenate(parts)
    assert out.size == STREAM_WORDS, (out.size, STREAM_WORDS)
    return out


def const_layout():
    c = np.zeros((P, N_CONST), np.float32)
    i = np.arange(P)

    def put(name, v):
        at, n = CONST_COLS[name]
        c[:v.shape[0], at:at + n] = v

    put("ident", np.eye(P))
    put("ones", np.ones((P, P)))
    put("causal", np.where(np.arange(T)[None] >= i[:, None], 0.0, NEG))
    levels = []
    for l in range(7):
        s = 1 << l
        levels.append(((i[None] // s) % 2 == 1) & (i[None] // s == i[:, None] // s + 1))
    put("level", np.stack(levels, 1).reshape(P, 7 * P))
    rot = np.zeros((QK, QK))
    for r in range(ROPE // 2):
        rot[NOPE + ROPE // 2 + r, NOPE + r] = -1.0
        rot[NOPE + r, NOPE + ROPE // 2 + r] = 1.0
    put("rot", rot)
    half = ROPE // 2
    inv = (np.float32(10000.0) ** (-np.arange(half, dtype=np.float32) / np.float32(half))).astype(np.float32)
    f = np.zeros((QK, 1))
    f[NOPE:NOPE + half, 0] = inv
    f[NOPE + half:, 0] = inv
    put("inv_freq", f)
    row_of = np.zeros((P, 31))
    row_of[:, 15] = 1.0
    put("row_of", row_of)
    tri = np.where(i[None] <= i[:, None], 0.0, NEG)
    put("score_mask", np.concatenate([tri, np.zeros((P, P)), tri], 1))
    put("tri", (i[None] >= i[:, None]) * 1.0)
    l2 = np.ones((P, 1))
    l2[:HQ] = P
    put("l2_scale", l2)
    put("l2_eps", l2 * EPS)
    put("eps", np.full((P, 1), EPS))
    return c


def param_layout(w):
    p = np.zeros((P, N_PARAM), np.float32)

    def put(name, v):
        at, n = PARAM_COLS[name]
        assert v.shape[1] == n, (name, v.shape, n)
        p[:v.shape[0], at:at + n] = v

    def cols_of(v):
        return v.reshape(-1, P).T

    put("norm_w", cols_of(w["norm_w"].reshape(-1)))
    put("gdn_conv", w["gdn_conv_w"][0].reshape(4, 32, P).transpose(2, 1, 0).reshape(P, -1))
    put("ffn_conv", w["ffn_conv_w"].reshape(2, 3, 2, FB, P).transpose(4, 0, 3, 2, 1).reshape(P, -1))
    put("ffn_bias", w["ffn_conv_b"].reshape(2, 2, FB, P).transpose(3, 0, 2, 1).reshape(P, -1))
    put("gdn_norm", w["gdn_norm_w"][0][:, None])
    put("a_log", w["gdn_a_log"][0][:, None])
    put("dt_bias", w["gdn_dt_bias"][0][:, None])
    put("ml_gate_i", w["ml_gate_b"][0][:ML_H, None])
    put("ml_gate_f", w["ml_gate_b"][0][ML_H:, None])
    put("ml_norm", cols_of(w["ml_norm_w"][0]))
    for name, src in (("ffn1_norm", "ffn1_norm_2"), ("mix_norm", "mix_norm_2"), ("ffn2_norm", "ffn2_norm_2"), ("mem_norm", "mem_norm_2"),
                      ("b_gate", "b_gate_2"), ("sg_g", "sg_ln_g_2"), ("sg_b", "sg_ln_b_2"), ("cq_norm", "mla_cq_norm_2"),
                      ("ckv_norm", "mla_ckv_norm_2"), ("mq_norm", "mem_q_norm_2"), ("mk_norm", "mem_k_norm_2")):
        put(name, cols_of(w[src][0]))
    put("q_norm", w["mla_q_norm_2"][0][:, None])
    put("k_norm", w["mla_k_norm_2"][0][:, None])
    return p


def layout(inputs):
    w = {k: np.asarray(v) for k, v in inputs.items()}
    return {
        "x_t": np.ascontiguousarray(w["x"][0].T),
        "meta_t": np.ascontiguousarray(w["meta_tokens"].T),
        "mem_t": np.ascontiguousarray(w["mem_2"][0].T),
        "positions": np.ascontiguousarray(w["positions_2"]),
        "stream": stream_layout(w),
        "consts": const_layout(),
        "params": param_layout(w),
        "sg_w_t": np.ascontiguousarray(w["sg_w_2"][0].transpose(2, 0, 1)),
        "sg_bias": np.ascontiguousarray(w["sg_b_2"][0]),
    }


def kernel(**inputs):
    import concourse.bacc as bacc
    from concourse.bass_utils import run_bass_kernel_spmd

    arrays = layout(inputs)
    counts = {}
    for _ in range(2):
        nc = bacc.Bacc("TRN2", target_bir_lowering=False, num_devices=1)
        aps = {n: nc.dram_tensor(f"in_{n}", v.shape, mybir.dt.from_np(v.dtype), kind="ExternalInput").ap() for n, v in arrays.items()}
        out = nc.dram_tensor("out_t", (D, SEQ), F32, kind="ExternalOutput").ap()
        counts = program(nc, out_t=out, counts=counts, **aps)
    r = run_bass_kernel_spmd(nc, [{f"in_{n}": v for n, v in arrays.items()}], core_ids=[0])
    return np.ascontiguousarray(r.results[0]["out_t"].T)[None]
```
